# Optimizing a Trainium2 kernel written in Bass

```python
import jax, jax.numpy as jnp
from jax import lax
import numpy as np

D_MODEL = 1024
BATCH = 1
SEQ = 4096
DEPTH = 1

CHUNK = 64
HEAD_DIM = 64
A_HEADS = 8
A_LEFT_CHUNKS = 8
A_BAND = (A_LEFT_CHUNKS + 1) * CHUNK
REL_CLIP = 128
B_HEADS = 8
B_KV_HEADS = 2
WINDOW = 128
B_LEFT_CHUNKS = WINDOW // CHUNK - 1
ROPE_THETA = 500000.0
ROT_DIM = HEAD_DIM // 4
D_A = A_HEADS * HEAD_DIM
D_B = B_HEADS * HEAD_DIM
D_BKV = B_KV_HEADS * HEAD_DIM
D_MIX = D_A + D_B
IN_SPLITS = (D_A, D_A, D_A, D_A, D_B, D_BKV, D_BKV, D_B)
D_IN = sum(IN_SPLITS)
PLE_DIM = 256
DN_ALPHA = (2 * DEPTH) ** 0.25
DN_BETA = (8 * DEPTH) ** -0.25
LN_EPS = 1e-5

kernel_name = "hybrid_chunked_relbias_swa_sink_deepnorm"

def layer_norm(x, g, b):
    xf = x.astype(jnp.float32)
    mu = jnp.mean(xf, axis=-1, keepdims=True)
    var = jnp.mean(jnp.square(xf - mu), axis=-1, keepdims=True)
    y = (xf - mu) * lax.rsqrt(var + LN_EPS) * g.astype(jnp.float32) + b.astype(jnp.float32)
    return y.astype(x.dtype)

def gather_band(t, n_left):
    nb, nc = t.shape[0], t.shape[1]
    tp = jnp.pad(t, ((0, 0), (n_left, 0), (0, 0), (0, 0), (0, 0)))
    band = jnp.stack([tp[:, j:j + nc] for j in range(n_left + 1)], axis=2)
    return band.reshape(nb, nc, (n_left + 1) * t.shape[2], t.shape[3], t.shape[4])

def band_valid(nc, n_left):
    src = jnp.arange(nc)[:, None] - n_left + jnp.arange(n_left + 1)[None, :]
    return jnp.repeat(src >= 0, CHUNK, axis=1)

def partial_rope(t, pos):
    half = ROT_DIM // 2
    inv = ROPE_THETA ** (-jnp.arange(half, dtype=jnp.float32) / half)
    ang = pos.astype(jnp.float32)[..., None] * inv
    cos = jnp.cos(ang)[:, :, None, :]
    sin = jnp.sin(ang)[:, :, None, :]
    tr = t[..., :ROT_DIM].astype(jnp.float32)
    x1, x2 = tr[..., :half], tr[..., half:]
    rot = jnp.concatenate([x1 * cos - x2 * sin, x2 * cos + x1 * sin], axis=-1).astype(t.dtype)
    return jnp.concatenate([rot, t[..., ROT_DIM:]], axis=-1)

def chunk_relbias_attention(q, k, v, rel_bias):
    nb, s, h, d = q.shape
    nc = s // CHUNK
    qc = q.reshape(nb, nc, CHUNK, h, d)
    kb = gather_band(k.reshape(nb, nc, CHUNK, h, d), A_LEFT_CHUNKS)
    vb = gather_band(v.reshape(nb, nc, CHUNK, h, d), A_LEFT_CHUNKS)
    scores = jnp.einsum('bnqhd,bnkhd->bnhqk', qc, kb,
                        preferred_element_type=jnp.float32) * (d ** -0.5)
    q_slot = jnp.arange(CHUNK) + A_LEFT_CHUNKS * CHUNK
    rel = q_slot[:, None] - jnp.arange(A_BAND)[None, :]
    idx = jnp.clip(rel, -REL_CLIP, REL_CLIP) + REL_CLIP
    bias = rel_bias[:, idx].astype(jnp.float32)
    scores = scores + bias[None, None]
    valid = band_valid(nc, A_LEFT_CHUNKS)
    scores = jnp.where(valid[None, :, None, None, :], scores, -jnp.inf)
    probs = jax.nn.softmax(scores, axis=-1).astype(v.dtype)
    out = jnp.einsum('bnhqk,bnkhd->bnqhd', probs, vb)
    return out.reshape(nb, s, h * d)

def sliding_window_sink_gqa(q, k, v, sinks):
    nb, s, hq, d = q.shape
    hkv = k.shape[2]
    g = hq // hkv
    nc = s // CHUNK
    qc = q.reshape(nb, nc, CHUNK, hkv, g, d)
    kb = gather_band(k.reshape(nb, nc, CHUNK, hkv, d), B_LEFT_CHUNKS)
    vb = gather_band(v.reshape(nb, nc, CHUNK, hkv, d), B_LEFT_CHUNKS)
    scores = jnp.einsum('bnqhgd,bnkhd->bnhgqk', qc, kb,
                        preferred_element_type=jnp.float32) * (d ** -0.5)
    valid = band_valid(nc, B_LEFT_CHUNKS)
    scores = jnp.where(valid[None, :, None, None, None, :], scores, -jnp.inf)
    sink = jnp.broadcast_to(sinks.astype(jnp.float32).reshape(1, 1, hkv, g, 1, 1),
                            scores.shape[:-1] + (1,))
    probs = jax.nn.softmax(jnp.concatenate([scores, sink], axis=-1), axis=-1)[..., :-1]
    out = jnp.einsum('bnhgqk,bnkhd->bnqhgd', probs.astype(v.dtype), vb)
    return out.reshape(nb, s, hq * d)

def setup_inputs(seed: int = 0) -> dict:
    key = jax.random.key(seed)
    ks = jax.random.split(key, 12)
    f32 = jnp.float32
    x = jax.random.normal(ks[0], (BATCH, SEQ, D_MODEL), f32)
    p = jax.random.normal(ks[1], (DEPTH, BATCH, SEQ, PLE_DIM), f32)
    positions = jnp.broadcast_to(jnp.arange(SEQ, dtype=jnp.int32)[None, :], (BATCH, SEQ))
    col_scales = (1.0, 1.0, DN_BETA, 1.0, 1.0, 1.0, DN_BETA, 1.0)
    col_scale = jnp.concatenate([jnp.full((n,), sc, f32) for n, sc in zip(IN_SPLITS, col_scales)])
    w_in = jax.random.normal(ks[2], (DEPTH, D_MODEL, D_IN), f32) * (D_MODEL ** -0.5) * col_scale
    rel_bias = jax.random.normal(ks[3], (DEPTH, A_HEADS, 2 * REL_CLIP + 1), f32) * 0.1
    sinks = jax.random.normal(ks[4], (DEPTH, B_HEADS), f32) * 0.5
    w_out = jax.random.normal(ks[5], (DEPTH, D_MIX, D_MODEL), f32) * (D_MIX ** -0.5) * DN_BETA
    ln_g = 1.0 + 0.02 * jax.random.normal(ks[6], (DEPTH, D_MODEL), f32)
    ln_b = 0.02 * jax.random.normal(ks[7], (DEPTH, D_MODEL), f32)
    w_ple_proj = jax.random.normal(ks[8], (DEPTH, PLE_DIM, D_MODEL), f32) * (PLE_DIM ** -0.5)
    w_ple_gate = jax.random.normal(ks[9], (DEPTH, D_MODEL, D_MODEL), f32) * (D_MODEL ** -0.5)
    return {"x": x, "p": p, "positions": positions, "w_in": w_in, "rel_bias": rel_bias,
            "sinks": sinks, "w_out": w_out, "ln_g": ln_g, "ln_b": ln_b,
            "w_ple_proj": w_ple_proj, "w_ple_gate": w_ple_gate}

def reference(x, p, positions, w_in, rel_bias, sinks, w_out, ln_g, ln_b, w_ple_proj, w_ple_gate):
    nb, s, _ = x.shape
    split_at = [int(c) for c in np.cumsum(IN_SPLITS)[:-1]]
    for i in range(DEPTH):
        proj = x @ w_in[i]
        aq, ak, av, ag, bq, bk, bv, bg = jnp.split(proj, split_at, axis=-1)
        ya = chunk_relbias_attention(aq.reshape(nb, s, A_HEADS, HEAD_DIM),
                                     ak.reshape(nb, s, A_HEADS, HEAD_DIM),
                                     av.reshape(nb, s, A_HEADS, HEAD_DIM), rel_bias[i])
        ya = ya * jax.nn.silu(ag)
        qb = partial_rope(bq.reshape(nb, s, B_HEADS, HEAD_DIM), positions)
        kbh = partial_rope(bk.reshape(nb, s, B_KV_HEADS, HEAD_DIM), positions)
        yb = sliding_window_sink_gqa(qb, kbh, bv.reshape(nb, s, B_KV_HEADS, HEAD_DIM), sinks[i])
        yb = yb * jax.nn.silu(bg)
        mix = jnp.concatenate([ya, yb], axis=-1) @ w_out[i]
        h = DN_ALPHA * x + mix
        h = h + jax.nn.sigmoid(h @ w_ple_gate[i]) * (p[i] @ w_ple_proj[i])
        x = layer_norm(h, ln_g[i], ln_b[i])
    return x


_drawn_inputs = setup_inputs


def setup_inputs(seed=0):
    import zlib

    import numpy as np

    out = dict(_drawn_inputs(seed))
    spreads = {}
    factors = {'rel_bias': 22.336, 'sinks': 31.967, 'w_out': 2.887, 'ln_g': 7.508, 'ln_b': 7.858}
    for name, (base, spread) in spreads.items():
        noise = np.random.default_rng([zlib.crc32(name.encode()), seed]).standard_normal(out[name].shape)
        drawn = base * np.exp(spread * noise) if base else spread * noise
        out[name] = __import__('jax').numpy.asarray(drawn.astype(out[name].dtype))
    for name, factor in factors.items():
        out[name] = (out[name] * factor).astype(out[name].dtype)
    return out
```

```python
import numpy as np
import concourse.bass as bass
from concourse import mybir
from contextlib import ExitStack

D_MODEL, SEQ, CHUNK, HEAD = 1024, 4096, 64, 64
A_HEADS, A_LEFT, REL_CLIP = 8, 8, 128
B_HEADS, B_KV = 8, 2
THETA, ROT = 500000.0, 16
PLE = 256
LN_EPS = 1e-5
ALPHA = 2.0 ** 0.25
SCALE = HEAD ** -0.5
MASKED = -1e30

P = 128
KT = D_MODEL // P
TB = 512
HALF = SEQ // 2
JB = HALF // TB
D_A, D_B, D_KV = A_HEADS * HEAD, B_HEADS * HEAD, B_KV * HEAD
COL_QK, COL_G, COL_BQ, COL_BK, COL_BV, COL_AV = 0, 1024, 2048, 2560, 2688, 2816
D_IN = COL_AV + D_A
PW = 256
PANELS = 14
UNITS = 104
ROW_BK, ROW_BV = 1024, 1152
ROWS = 1280

NT = SEQ // P
BAND = A_LEFT // 2 + 1
NBW = BAND * P
QUADS = SEQ // TB

B_HALF = SEQ // 2
B_UNITS = B_HALF // (4 * CHUNK)

ALPHA32 = float(np.float32(ALPHA))


def build(nc, xT, x, pT, pos, w_in, rel_rev, sinks, w_out, w_gate, w_ple, ln_g, ln_b, rope_const, out):
    f32, f32r, i32 = mybir.dt.float32, mybir.dt.float32r, mybir.dt.int32
    ALU, ACT, AX = mybir.AluOpType, mybir.ActivationFunctionType, mybir.AxisListType

    ctx = ExitStack()
    with ctx:
        def sem(name):
            return ctx.enter_context(nc.semaphore(name))

        def scratch(name, shape):
            return nc.dram_tensor(name, shape, f32, kind="Internal").ap()

        qk_d = scratch("qk_d", [2, ROWS, SEQ])
        bq_d = scratch("bq_d", [B_HEADS // 2, HEAD, SEQ // TB, 2, TB // CHUNK, 2, CHUNK])
        g_d = scratch("g_d", [D_A + D_B, SEQ])
        v_d = scratch("v_d", [SEQ, A_HEADS, 2, HEAD])
        y_d = scratch("y_d", [D_A + D_B, SEQ])
        trig_d = scratch("trig_d", [2, ROT, SEQ])
        bias_d = scratch("bias_d", [A_HEADS, 384])
        bias_q_d = scratch("bias_q_d", [A_HEADS * P, 256])

        psum = ctx.enter_context(nc.psum_tensor("psum", [P, 8, 512], f32))

        ident = ctx.enter_context(nc.sbuf_tensor("ident", [P, P], f32))
        sink_sb = ctx.enter_context(nc.sbuf_tensor("sink_sb", [P, 2, 4], f32))
        small = ctx.enter_context(nc.sbuf_tensor("small", [P, 64], f32))
        credit = ctx.enter_context(nc.sbuf_tensor("credit", [P, 8], f32))

        stage = ExitStack()

        def sb(name, shape, dt=f32):
            return stage.enter_context(nc.sbuf_tensor(name, shape, dt))

        x_hi, x_lo = (sb(n, [P, KT, HALF], f32r) for n in ("x_hi", "x_lo"))
        x_raw = sb("x_raw", [P, 2, 2, TB])
        w_raw = sb("w_raw", [P, KT, PW])
        w_hi, w_lo = (sb(n, [P, 2, KT, PW], f32r) for n in ("w_hi", "w_lo"))
        stage_out = sb("stage_out", [P, 2, 2, TB])
        work = sb("work", [P, 2, TB])
        trig = sb("trig", [P, 2, 2, TB])
        swap = sb("swap", [P, 2, TB])
        bias_row = sb("bias_row", [A_HEADS, 384])
        rope_c = sb("rope_c", [P, 2])
        stage.close()

        aq_hi, aq_lo = (sb(n, [P, 2, SEQ], f32r) for n in ("aq_hi", "aq_lo"))
        ak = sb("ak", [P, 2, SEQ], f32r)
        av = sb("av", [P, 2, NT, P], f32r)
        prob = sb("prob", [P, 4, NBW])
        pt_hi, pt_lo = (sb(n, [P, 2, BAND + 1, 2 * P], f32r) for n in ("pt_hi", "pt_lo"))
        bias = sb("bias", [P, 2, NBW])
        y_low = sb("y_low", [HEAD, 2, 2 * P])
        y_a = sb("y_a", [HEAD, 2, TB])
        g_a = sb("g_a", [HEAD, 2, TB])
        stage.close()

        bq_hi, bq_lo = (sb(n, [P, 2, 2 * B_HALF], f32r) for n in ("bq_hi", "bq_lo"))
        bk = sb("bk", [P, 2, CHUNK + B_HALF], f32r)
        bvt = sb("bvt", [P, 2, CHUNK + B_HALF])
        prob_b = sb("prob_b", [P, 4, 4, P])
        ptb_hi, ptb_lo = (sb(n, [P, 2, 4, P], f32r) for n in ("ptb_hi", "ptb_lo"))
        v_b = sb("v_b", [P, 2, 4, P], f32r)
        yb_low = sb("yb_low", [HEAD, 2, 4 * P])
        y_b = sb("y_b", [HEAD, 2, 2, 4, CHUNK])
        g_b = sb("g_b", [HEAD, 2, 2, 4 * CHUNK])
        stage.close()

        wo_hi, wo_lo = (sb(n, [P, KT, D_MODEL], f32r) for n in ("wo_hi", "wo_lo"))
        wg_hi, wg_lo = (sb(n, [P, KT, D_MODEL], f32r) for n in ("wg_hi", "wg_lo"))
        wp_hi, wp_lo = (sb(n, [P, 2, D_MODEL], f32r) for n in ("wp_hi", "wp_lo"))
        y_raw = sb("y_raw", [P, 2, KT, P])
        p_raw = sb("p_raw", [P, 2, 2, P])
        y_hi, y_lo = (sb(n, [P, KT, P], f32r) for n in ("y_hi", "y_lo"))
        p_hi, p_lo = (sb(n, [P, 2, 2, P], f32r) for n in ("p_hi", "p_lo"))
        hT_hi, hT_lo = (sb(n, [P, KT, P], f32r) for n in ("hT_hi", "hT_lo"))
        x_nat = sb("x_nat", [P, D_MODEL])
        h = sb("h", [P, 3, D_MODEL])
        sg = sb("sg", [P, D_MODEL])
        lng, lnb = (sb(n, [P, D_MODEL]) for n in ("lng", "lnb"))
        stage.close()

        setup = sem("setup")
        ident_ready = sem("ident_ready")
        consts_loaded = sem("consts_loaded")
        setup_stored = sem("setup_stored")
        setup_step = sem("setup_step")
        bias_stored = sem("bias_stored")

        p_over, a_over, b_over = sem("p_over"), sem("a_over"), sem("b_over")

        x_loaded = [sem(f"x_loaded{i}") for i in range(2)]
        x_hi_done, x_split = sem("x_hi_done"), sem("x_split")
        w_loaded = sem("w_loaded")
        w_hi_done, w_split = sem("w_hi_done"), sem("w_split")
        acc_done, acc_free = sem("acc_done"), sem("acc_free")
        unit_act = sem("unit_act")
        unit_stored = [sem(f"unit_stored{i}") for i in range(2)]
        bq_stored = [sem(f"bq_stored{i}") for i in range(2)]
        rope_row, rope_step, rope_done = sem("rope_row"), sem("rope_step"), sem("rope_done")
        trig_loaded = [sem(f"trig_loaded{i}") for i in range(2)]

        job_loaded = [sem(f"job_loaded{i}") for i in range(2)]
        scores_done, scores_used = sem("scores_done"), sem("scores_used")
        shift_ready, exp_done, recip_ready = sem("shift_ready"), sem("exp_done"), sem("recip_ready")
        normed = [sem(f"normed{i}") for i in range(2)]
        probsT_done, probsT_hi, probsT_split = sem("probsT_done"), sem("probsT_hi"), sem("probsT_split")
        values_done, y_low_ready, y_summed = sem("values_done"), sem("y_low_ready"), sem("y_summed")
        y_gated = sem("y_gated")
        gate_loaded = [sem(f"gate_loaded{i}") for i in range(2)]
        y_stored = [sem(f"y_stored{i}") for i in range(2)]

        bjob_loaded = [sem(f"bjob_loaded{i}") for i in range(2)]
        bscores_done, bmax_done, bshift_ready = sem("bscores_done"), sem("bmax_done"), sem("bshift_ready")
        bexp_done, bden_step, bnormed = sem("bexp_done"), sem("bden_step"), sem("bnormed")
        bprobsT_done, bprobsT_hi, bprobsT_split = sem("bprobsT_done"), sem("bprobsT_hi"), sem("bprobsT_split")
        bv_done, bv_ready = sem("bv_done"), sem("bv_ready")
        bvalues_done, by_low_ready, by_summed = sem("bvalues_done"), sem("by_low_ready"), sem("by_summed")
        by_gated = sem("by_gated")
        bgate_loaded = [sem(f"bgate_loaded{i}") for i in range(2)]
        by_stored = [sem(f"by_stored{i}") for i in range(2)]

        cw_loaded = [sem(f"cw_loaded{i}") for i in range(2)]
        cw_hi_done, cw_split = sem("cw_hi_done"), sem("cw_split")
        ln_loaded = sem("ln_loaded")
        y_loaded = [sem(f"y_loaded{i}") for i in range(2)]
        xn_loaded = sem("xn_loaded")
        y_hi_done, y_split = sem("y_hi_done"), sem("y_split")
        mix_done, h_done = sem("mix_done"), sem("h_done")
        hT_done, hT_hi_done, hT_split = sem("hT_done"), sem("hT_hi_done"), sem("hT_split")
        ple_done, gate_done, sig_done = sem("ple_done"), sem("gate_done"), sem("sig_done")
        ple_gated, h2_done = sem("ple_gated"), sem("h2_done")
        ln_step, normalized, scaled = sem("ln_step"), sem("normalized"), sem("scaled")
        shifted = sem("shifted")
        inverse_done, root_done = sem("inverse_done"), sem("root_done")
        out_stored = [sem(f"out_stored{i}") for i in range(3)]

        block = ctx.enter_context(nc.Block())

        @block.sync
        def _(sp):
            for sm in (*unit_stored, *bq_stored, *y_stored, *out_stored):
                sp.sem_inc(sm, 16)
            sp.dma_start(rope_c[:, :], rope_const).then_inc(consts_loaded, 16)
            for g in range(8):
                sp.dma_start(work[16 * g:16 * g + 16, 0, :].bitcast(i32),
                             bass.AP(tensor=pos.tensor, offset=TB * g, ap=[[0, 16], [1, TB]])
                             ).then_inc(consts_loaded, 16)
            sp.dma_start(bias_row[:, 127:384], rel_rev).then_inc(consts_loaded, 16)
            for hd in range(2):
                sp.dma_start(sink_sb[64 * hd:64 * hd + 64, 0, :],
                             bass.AP(tensor=sinks.tensor, offset=4 * hd, ap=[[0, 64], [1, 4]]),
                             ).then_inc(consts_loaded, 16)

            def load_panel(col, width):
                sp.dma_start(w_raw[:, :, 0:width],
                             w_in[:, bass.ds(col, width)].rearrange("(k p) n -> p k n", p=P)).then_inc(w_loaded, 16)

            load_panel(COL_QK, PW)
            sp.wait_ge(setup, 3)
            sp.wait_ge(rope_step, 2)
            for g in range(8):
                for s, t in ((0, swap[16 * g:16 * g + 16, 0, :]), (1, swap[16 * g:16 * g + 16, 1, :])):
                    sp.dma_start(trig_d[s, :, TB * g:TB * g + TB], t).then_inc(setup_stored, 16)
            sp.dma_start(bias_d[:, 0:384], bias_row[:, :]).then_inc(setup_stored, 16)

            sp.wait_ge(setup_stored, 16 * 17)
            sp.dma_start(bias_q_d.rearrange("(h q) c -> h q c", q=P),
                         bass.AP(tensor=bias_d.tensor, offset=127, ap=[[384, A_HEADS], [-1, P], [1, 256]])
                         ).then_inc(bias_stored, 16)

            def store_unit(unit, slot, dst, n=2):
                sp.wait_ge(acc_free, unit + 9)
                src = stage_out[:, slot, 0:n, :]
                if n == 1:
                    src = stage_out[:, slot, 0, :]
                sp.dma_start(dst, src).then_inc(unit_stored[slot], 16)

            with sp.Fori(0, 2) as half:
                base = half * UNITS
                tok = half * HALF
                for j in range(JB):
                    for kp in range(4):
                        c = 4 * j + kp
                        sp.wait_ge(x_split, half * 16 + c + 1)
                        sp.dma_start(x_raw[:, c % 2, :, :],
                                     xT[2 * kp * P:2 * kp * P + 2 * P, bass.ds(tok + j * TB, TB)]
                                     .rearrange("(k p) t -> p k t", p=P)).then_inc(x_loaded[c % 2], 16)

                def next_panel(panel, col, width):
                    sp.wait_ge(w_split, 4 * (half * PANELS + panel))
                    load_panel(col, width)

                def rows(row, j):
                    return qk_d[:, bass.ds(row, P), bass.ds(tok + j * TB, TB)].rearrange("c p t -> p c t")

                with sp.Fori(0, 2) as it:
                    for s in range(2):
                        next_panel(2 * it + s + 1, COL_QK + (2 * it + s + 1) * PW, PW)
                        for r in range(8):
                            store_unit(base + 16 * it + 8 * s + r, r % 2,
                                       rows((2 * it + s) * PW + (r % 2) * P, r // 2))
                with sp.Fori(0, 2) as it:
                    for s in range(2):
                        next_panel(5 + 2 * it + s, COL_G + (2 * it + s + 1) * PW, PW)
                        for r in range(8):
                            store_unit(base + 32 + 16 * it + 8 * s + r, r % 2,
                                       g_d[bass.ds((2 * it + s) * PW + (r % 2) * P, P),
                                           bass.ds(tok + (r // 2) * TB, TB)], 1)

                def load_trig(n, j):
                    earlier = 0 if n < 2 else 2 * (n - 1) if n <= 9 else n + 7
                    sp.wait_ge(rope_done, half * 20 + earlier + 1)
                    for r0 in (0, HEAD):
                        sp.dma_start(trig[r0:r0 + ROT, j % 2, :, :],
                                     trig_d[:, :, bass.ds(tok + j * TB, TB)].rearrange("c r t -> r c t")
                                     ).then_inc(trig_loaded[j % 2], 16)
                for w in range(2):
                    if w == 0:
                        next_panel(9, COL_BQ + PW, PW)
                    else:
                        next_panel(10, COL_BK, P)
                    for j in range(JB):
                        load_trig(4 * w + j, j)
                        for c in range(2):
                            sp.wait_ge(acc_free, base + 64 + 8 * w + 2 * j + c + 9)
                            for hd, stored in ((0, unit_stored), (1, bq_stored)):
                                sp.dma_start(
                                    bq_d[2 * w + c, :, bass.ds(half * JB + j, 1), :, :, hd, :]
                                    .rearrange("d b c n q -> d (b c n) q"),
                                    stage_out[hd * HEAD:hd * HEAD + HEAD, c, :, :]
                                    .rearrange("d c (n q) -> d (c n) q", q=CHUNK)).then_inc(stored[c], 16)
                next_panel(11, COL_BV, P)
                for j in range(JB):
                    load_trig(8 + j, j)
                    store_unit(base + 80 + j, j % 2, rows(ROW_BK, j))
                next_panel(12, COL_AV, PW)
                for j in range(JB):
                    store_unit(base + 84 + j, j % 2, rows(ROW_BV, j))
                for w in range(2):
                    if w == 0:
                        next_panel(13, COL_AV + PW, PW)
                    else:
                        next_panel(14, COL_QK, PW)
                    for r in range(8):
                        store_unit(base + 88 + 8 * w + r, r % 2,
                                   v_d[bass.ds(tok + r * 2 * P, 2 * P), 4 * w:4 * w + 4, :, :]
                                   .rearrange("(t p) h c d -> p t (h c d)", p=P))

            sp.wait_ge(unit_stored[0], 16 * UNITS + 16)
            sp.wait_ge(unit_stored[1], 16 * UNITS + 16)
            sp.wait_ge(bq_stored[0], 16 * 17)
            sp.wait_ge(bq_stored[1], 16 * 17)
            sp.wait_ge(bias_stored, 16)
            sp.wait_ge(w_split, 4 * (2 * PANELS + 1))
            sp.sem_inc(p_over, 1)

            def load_job(head, s):
                def q(c):
                    return qk_d[c, bass.ds(head * HEAD, HEAD), :]
                for dst, c in ((aq_hi, 0), (aq_lo, 1)):
                    for r0 in (0, HEAD):
                        sp.dma_start(dst[r0:r0 + HEAD, s, :].bitcast(f32), q(c)).then_inc(job_loaded[s], 16)
                for c in range(2):
                    sp.dma_start(ak[c * HEAD:c * HEAD + HEAD, s, :].bitcast(f32),
                                 qk_d[c, bass.ds(D_A + head * HEAD, HEAD), :]).then_inc(job_loaded[s], 16)
                sp.dma_start(av[:, s, :, :].bitcast(f32),
                             v_d[:, bass.ds(head, 1), :, :].rearrange("(t p) h c d -> p t (h c d)", p=P)
                             ).then_inc(job_loaded[s], 16)
                for r0, n in ((0, 192), (64, 256)):
                    sp.dma_start(bias[r0:r0 + 64, s, NBW - 256:NBW - 256 + n],
                                 bias_q_d[bass.ds(head * P + r0, 64), 0:n]).then_inc(job_loaded[s], 16)

            def stage_a(it, load_next):
                for s in range(2):
                    quad0 = 16 * it + 8 * s
                    head = 2 * it + s
                    for i in range(QUADS + 1):
                        if i < QUADS:
                            sp.wait_ge(y_gated, quad0 + i + 1)
                            sp.dma_start(g_a[:, i % 2, :], g_d[bass.ds(head * HEAD, HEAD), i * TB:i * TB + TB]
                                         ).then_inc(gate_loaded[i % 2], 16)
                        if i > 0:
                            sp.wait_ge(y_gated, quad0 + i + 2)
                            sp.dma_start(y_d[bass.ds(head * HEAD, HEAD), (i - 1) * TB:i * TB], y_a[:, (i - 1) % 2, :]
                                         ).then_inc(y_stored[(i - 1) % 2], 16)
                    if load_next:
                        load_job(head + 2, s)

            load_job(0, 0)
            load_job(1, 1)
            with sp.Fori(0, 3) as it:
                stage_a(it, True)
            stage_a(3, False)
            sp.wait_ge(y_stored[0], 16 * 33)
            sp.wait_ge(y_stored[1], 16 * 33)
            sp.sem_inc(a_over, 1)

            def load_bjob(pair, kv, s):
                lo_tok = 0 if s == 0 else B_HALF - CHUNK
                c0 = CHUNK if s == 0 else 0
                n = B_HALF if s == 0 else B_HALF + CHUNK
                for dst, c in ((bq_hi, 0), (bq_lo, 1)):
                    for r0 in (0, HEAD):
                        sp.dma_start(dst[r0:r0 + HEAD, s, :].bitcast(f32).rearrange("d (b n) -> d b n", n=2 * TB),
                                     bq_d[pair, :, s * JB:(s + 1) * JB, c, :, :, :]
                                     .rearrange("d b n h q -> d b (n h q)")).then_inc(bjob_loaded[s], 16)
                for c in range(2):
                    for dst, row in ((bk, ROW_BK), (bvt, ROW_BV)):
                        sp.dma_start(dst[c * HEAD:c * HEAD + HEAD, s, c0:c0 + n].bitcast(f32),
                                     qk_d[c, bass.ds(row + kv * HEAD, HEAD), lo_tok:lo_tok + n]
                                     ).then_inc(bjob_loaded[s], 16)

            def stage_b(pair, kv_next, load_next):
                for s in range(2):
                    unit0 = 16 * pair + 8 * s
                    rows_g = D_A + pair * P

                    def tokens(t, i):
                        return (t[bass.ds(rows_g, P), s * B_HALF + i * 4 * CHUNK:s * B_HALF + (i + 1) * 4 * CHUNK]
                                .rearrange("(h d) t -> d h t", h=2))
                    for i in range(B_UNITS + 1):
                        if i < B_UNITS:
                            sp.wait_ge(by_gated, unit0 + i + 1)
                            sp.dma_start(g_b[:, i % 2, :, :], tokens(g_d, i)).then_inc(bgate_loaded[i % 2], 16)
                        if i > 0:
                            sp.wait_ge(by_gated, unit0 + i + 2)
                            sp.dma_start(tokens(y_d, i - 1),
                                         y_b[:, (i - 1) % 2, :, :, :].rearrange("p h c q -> p h (c q)")
                                         ).then_inc(by_stored[(i - 1) % 2], 16)
                    if load_next:
                        load_bjob(pair + 1, kv_next, s)

            load_bjob(0, 0, 0)
            load_bjob(0, 0, 1)
            for pair in range(4):
                stage_b(pair, (pair + 1) // 2, pair < 3)
            sp.wait_ge(by_stored[0], 16 * 32)
            sp.wait_ge(by_stored[1], 16 * 32)
            sp.sem_inc(b_over, 1)

            sp.dma_start(lng[:, :], bass.AP(tensor=ln_g.tensor, offset=0, ap=[[0, P], [1, D_MODEL]])).then_inc(ln_loaded, 16)
            sp.dma_start(lnb[:, :], bass.AP(tensor=ln_b.tensor, offset=0, ap=[[0, P], [1, D_MODEL]])).then_inc(ln_loaded, 16)
            n = 0
            for w, kts in ((w_out, KT), (w_gate, KT), (w_ple, 2)):
                for k in range(kts):
                    if n >= 2:
                        sp.wait_ge(cw_split, n - 1)
                    sp.dma_start(y_raw[:, n % 2, :, :].rearrange("p a b -> p (a b)"), w[k * P:k * P + P, :]
                                 ).then_inc(cw_loaded[n % 2], 16)
                    n += 1

            def load_tile(t, s):
                sp.dma_start(y_raw[:, s, :, :], y_d[:, bass.ds(t * P, P)].rearrange("(k p) t -> p k t", p=P)
                             ).then_inc(y_loaded[s], 16)
                sp.dma_start(p_raw[:, s, :, :], pT[:, bass.ds(t * P, P)].rearrange("(k p) t -> p k t", p=P)
                             ).then_inc(y_loaded[s], 16)

            def load_x(t):
                sp.dma_start(x_nat[:, :], x[bass.ds(t * P, P), :]).then_inc(xn_loaded, 16)

            def store_out(t, slot):
                sp.wait_ge(shifted, t + 1)
                sp.dma_start(out[bass.ds(t * P, P), :], h[:, slot, :]).then_inc(out_stored[slot], 16)

            sp.wait_ge(cw_split, n)
            load_tile(0, 0)
            load_tile(1, 1)
            load_x(0)

            def stage_c(t, i, more):
                if more > 1:
                    sp.wait_ge(y_split, t + 1)
                    load_tile(t + 2, i % 2)
                if more > 0:
                    sp.wait_ge(h_done, t + 1)
                    load_x(t + 1)
                store_out(t, i % 3)

            with sp.Fori(0, 5) as it:
                for i in range(6):
                    stage_c(6 * it + i, i, 2)
            stage_c(30, 0, 1)
            stage_c(31, 1, 0)
            for slot, count in ((0, 11), (1, 11), (2, 10)):
                sp.wait_ge(out_stored[slot], 16 * count + 16)

        @block.gpsimd
        def _(pool):
            pool.memset(ident[:, :], 0.0).then_inc(setup_step, 1)
            pool.wait_ge(setup_step, 1)
            pool.affine_select(out=ident[:, :], in_=ident[:, :], compare_op=ALU.not_equal, fill=1.0, base=0,
                               pattern=[[-1, P]], channel_multiplier=1).then_inc(ident_ready, 1)
            pool.memset(credit[:, 0:1], 0.0).then_inc(y_gated, 2)
            pool.memset(credit[:, 1:2], 0.0).then_inc(by_gated, 2)
            with pool.Fori(0, SEQ // TB * A_HEADS // 2) as it:
                for s in range(2):
                    pool.wait_ge(y_summed, 4 * it + 2 * s + 4)
                    pool.wait_ge(gate_loaded[s], 16 * it + 16)
                    pool.tensor_tensor(y_a[:, s, :], y_a[:, s, :], g_a[:, s, :], ALU.mult).then_inc(y_gated, 1)
            with pool.Fori(0, 32) as it:
                for s in range(2):
                    pool.wait_ge(by_summed, 2 * it + s + 2)
                    pool.wait_ge(bgate_loaded[s], 16 * it + 16)
                    yb = y_b[:, s, :, :, :].rearrange("p h c q -> p (h c q)")
                    pool.tensor_tensor(yb, yb, g_b[:, s, :, :].rearrange("p h t -> p (h t)"),
                                       ALU.mult).then_inc(by_gated, 1)
            pool.wait_ge(ln_loaded, 32)
            def scale_shift(t, slot):
                pool.wait_ge(normalized, t + 1)
                pool.tensor_tensor(h[:, slot, :], h[:, slot, :], lng[:, :], ALU.mult).then_inc(scaled, 1)
                pool.wait_ge(scaled, t + 1)
                pool.tensor_tensor(h[:, slot, :], h[:, slot, :], lnb[:, :], ALU.add).then_inc(shifted, 1)
            with pool.Fori(0, 10) as it:
                for i in range(3):
                    scale_shift(3 * it + i, i)
            scale_shift(30, 0)
            scale_shift(31, 1)

        @block.scalar
        def _(act):
            act.sem_inc(sig_done, 1)
            act.wait_ge(setup, 1)
            act.activation(swap[:, 1, :], work[:, 1, :], ACT.Sin)
            act.activation(swap[:, 0, :], work[:, 1, :], ACT.Sin, scale=0.5).then_inc(setup, 1)

            def split_w(panel, i, slot, width=PW):
                if i == 0:
                    act.wait_ge(w_loaded, 16 * (panel + 1))
                act.activation(w_hi[:, slot, 2 * i:2 * i + 2, 0:width], w_raw[:, 2 * i:2 * i + 2, 0:width],
                               ACT.Copy).then_inc(w_hi_done, 1)

            def split_x(half, c):
                act.wait_ge(x_loaded[c % 2], 16 * (half * 8 + c // 2 + 1))
                act.activation(x_hi[:, 2 * (c % 4):2 * (c % 4) + 2, (c // 4) * TB:(c // 4) * TB + TB],
                               x_raw[:, c % 2, :, :], ACT.Copy).then_inc(x_hi_done, 1)

            for i in range(4):
                split_w(0, i, 0)

            with act.Fori(0, 2) as half:
                base = half * UNITS
                pbase = half * PANELS
                for c in range(16):
                    split_x(half, c)

                def before(unit, slot):
                    act.wait_ge(acc_done, unit + 1)
                    act.wait_ge(unit_stored[slot], 8 * unit - 8 * slot + 16)

                def split_unit(unit, r):
                    before(unit, r % 2)
                    act.activation(stage_out[:, r % 2, 0, :].bitcast(f32r), psum[:, r % 8, :],
                                   ACT.Copy).then_inc(unit_act, 1)

                def panel(w, slot, units, next_width, unit_fn):
                    for r in range(units):
                        unit_fn(r)
                        if r < 4:
                            split_w(pbase + w + 1, r, 1 - slot, next_width)

                with act.Fori(0, 2) as it:
                    for s in range(2):
                        def fn(r):
                            split_unit(base + 16 * it + 8 * s + r, r)
                        panel(2 * it + s, s, 8, PW, fn)
                with act.Fori(0, 2) as it:
                    for s in range(2):
                        def fn(r):
                            unit = base + 32 + 16 * it + 8 * s + r
                            act.wait_ge(acc_done, unit + 1)
                            act.wait_ge(acc_free, unit + 7)
                            act.activation(work[:, r % 2, :], psum[:, r % 8, :], ACT.Sigmoid).then_inc(unit_act, 1)
                        panel(4 + 2 * it + s, s, 8, PW, fn)

                def rope_unit(unit, n, bank, slot):
                    rope = half * 20 + n
                    act.wait_ge(acc_done, unit + 1)
                    act.wait_ge(acc_free, unit + 7)
                    act.activation(work[:, slot, :], psum[:, bank, :], ACT.Copy).then_inc(rope_row, 1)
                    act.wait_ge(rope_done, rope + 2)
                    act.wait_ge(unit_stored[slot], 8 * unit - 8 * slot + 16)
                    act.wait_ge(bq_stored[slot], half * 128 + 8 * (min(n, 16 + slot) - slot) + 16)
                    act.activation(stage_out[:, slot, 0, :].bitcast(f32r), work[:, slot, :],
                                   ACT.Copy).then_inc(unit_act, 1)

                for w in range(2):
                    panel(8 + w, w, 8, PW if w == 0 else P,
                          lambda r: rope_unit(base + 64 + 8 * w + r, 8 * w + r, r % 8, r % 2))
                panel(10, 0, 4, P, lambda r: rope_unit(base + 80 + r, 16 + r, r, r % 2))

                def bv(r):
                    before(base + 84 + r, r % 2)
                    act.activation(stage_out[:, r % 2, 0, :].bitcast(f32r), psum[:, 4 + r, :],
                                   ACT.Copy).then_inc(unit_act, 1)
                panel(11, 1, 4, PW, bv)
                for w in range(2):
                    def av_unit(r):
                        before(base + 88 + 8 * w + r, r % 2)
                        dst = stage_out[:, r % 2, :, :].bitcast(f32r).rearrange("p t (h c d) -> p (t h) c d", c=2, d=HEAD)
                        act.activation(dst[:, :, 0, :], psum[:, r % 8, :].rearrange("p (h d) -> p h d", d=HEAD),
                                       ACT.Copy).then_inc(unit_act, 1)
                    panel(12 + w, w, 8, PW, av_unit)

            def a_step(u0, pair0, i, job_unit):
                if i < NT:
                    n = min(BAND, i + 1)
                    act.wait_ge(shift_ready, u0 + i + 1)
                    act.activation(prob[:, i % 4, NBW - n * P:NBW], prob[:, i % 4, NBW - n * P:NBW], ACT.Exp,
                                   bias=small[:, 4 + i % 4:5 + i % 4], scale=SCALE,
                                   accum_out=small[:, 8 + i % 4:9 + i % 4]).then_inc(exp_done, 1)
                t = i - 1
                if 0 <= t < NT and t % 2 == 0:
                    n = min(BAND, t + 1)
                    act.wait_ge(recip_ready, u0 + t + 1)
                    act.activation(prob[:, t % 4, NBW - n * P:NBW], prob[:, t % 4, NBW - n * P:NBW], ACT.Copy,
                                   scale=small[:, 12 + t % 4:13 + t % 4]).then_inc(normed[0], 1)
                t = i - 2
                if 0 <= t < NT:
                    n = min(BAND, t + 1)
                    e = t % 2
                    act.wait_ge(probsT_done, u0 + t + 1)
                    src = psum[:, 2 + 2 * e:4 + 2 * e, :].rearrange("p a b -> p (a b)")[:, 0:n * P]
                    act.activation(pt_hi[:, (t // 2) % 2, e + BAND - n:e + BAND, e * P:e * P + P],
                                   src.rearrange("p (j q) -> p j q", q=P), ACT.Copy).then_inc(probsT_hi, 1)
                t = i - 4
                if 0 <= t < NT and t % 2 == 1:
                    pr = t // 2
                    act.wait_ge(values_done, pair0 + pr + 1)
                    act.wait_ge(y_summed, pair0 + pr + 1)
                    act.activation(y_low[:, pr % 2, :], psum[HEAD:P, 6 + pr % 2, 0:2 * P],
                                   ACT.Copy).then_inc(y_low_ready, 1)

            with act.Fori(0, 4) as it:
                for s in range(2):
                    for i in range(NT + 4):
                        a_step(64 * it + 32 * s, 32 * it + 16 * s, i, None)

            def b_step(u0, pair, i):
                if i < B_UNITS:
                    act.wait_ge(bshift_ready, u0 + i + 1)
                    for c in range(4):
                        first = i == 0 and c == 0 and s == 0
                        lo = CHUNK if first else 0
                        act.activation(prob_b[:, i % 4, c, lo:P], psum[:, i % 2, c * P + lo:c * P + P], ACT.Exp,
                                       bias=small[:, 16 + 4 * (i % 4) + c:17 + 4 * (i % 4) + c], scale=SCALE,
                                       accum_out=small[:, 32 + 4 * (i % 4) + c:33 + 4 * (i % 4) + c])
                    act.activation(small[:, 48 + 4 * (i % 4):52 + 4 * (i % 4)],
                                   small[:, 16 + 4 * (i % 4):20 + 4 * (i % 4)], ACT.Exp,
                                   bias=sink_sb[:, 0, pair:pair + 1], scale=1.0).then_inc(bexp_done, 1)
                t = i - 2
                if 0 <= t < B_UNITS:
                    act.wait_ge(bprobsT_done, u0 + t + 1)
                    act.activation(ptb_hi[:, t % 2, :, :].rearrange("p c q -> p (c q)"), psum[:, 2 + t % 2, :],
                                   ACT.Copy).then_inc(bprobsT_hi, 1)
                t = i - 3
                if 0 <= t < B_UNITS:
                    act.wait_ge(bvalues_done, u0 + t + 1)
                    act.wait_ge(by_summed, u0 + t)
                    act.activation(yb_low[:, t % 2, :], psum[HEAD:P, 4 + t % 2, :], ACT.Copy).then_inc(by_low_ready, 1)
                if i < B_UNITS and i % 2 == 0:
                    act.wait_ge(bv_done, u0 + i + 1)
                    act.activation(v_b[:, i % 2, :, :].rearrange("p c d -> p (c d)"), psum[:, 7, :],
                                   ACT.Copy).then_inc(bv_ready, 1)

            act.wait_ge(a_over, 1)
            for pair in range(4):
                for s in range(2):
                    for i in range(B_UNITS + 3):
                        b_step(16 * pair + 8 * s, pair, i)

            act.wait_ge(b_over, 1)
            strips = ([(wo_hi, k) for k in range(KT)] + [(wg_hi, k) for k in range(KT)] + [(wp_hi, k) for k in range(2)])
            for n, (dst, k) in enumerate(strips):
                act.wait_ge(cw_loaded[n % 2], 16 * (n // 2 + 1))
                act.activation(dst[:, k, :], y_raw[:, n % 2, :, :].rearrange("p a b -> p (a b)"),
                               ACT.Copy).then_inc(cw_hi_done, 1)

            def y_tile_hi(t, s, first=False):
                act.wait_ge(y_loaded[s], 32 * (t // 2 + 1) if isinstance(t, int) else 16 * (t - s) + 32)
                if not first:
                    act.wait_ge(mix_done, t)
                act.activation(y_hi[:, :, :], y_raw[:, s, :, :], ACT.Copy)
                if not isinstance(t, int):
                    act.wait_ge(ple_done, t - 1)
                act.activation(p_hi[:, s, :, :], p_raw[:, s, :, :], ACT.Copy).then_inc(y_hi_done, 1)

            def hT_tile_hi(t):
                act.wait_ge(hT_done, t + 1)
                act.activation(hT_hi[:, :, :].rearrange("p k t -> p (k t)"),
                               psum[:, 2:4, :].rearrange("p a b -> p (a b)"), ACT.Copy).then_inc(hT_hi_done, 1)

            def sigmoid(t):
                act.wait_ge(gate_done, t + 1)
                act.wait_ge(h2_done, t + 1)
                act.activation(sg[:, :], psum[:, 4:6, :].rearrange("p a b -> p (a b)"), ACT.Sigmoid).then_inc(sig_done, 1)

            def root(t):
                act.wait_ge(inverse_done, t + 1)
                act.activation(small[:, 15:16], small[:, 14:15], ACT.Sqrt).then_inc(root_done, 1)

            y_tile_hi(0, 0, True)
            y_tile_hi(1, 1)
            hT_tile_hi(0)
            with act.Fori(0, 15) as it:
                for s in range(2):
                    t = 2 * it + s
                    y_tile_hi(t + 2, s)
                    sigmoid(t)
                    hT_tile_hi(t + 1)
                    root(t)
            sigmoid(30)
            hT_tile_hi(31)
            root(30)
            sigmoid(31)
            root(31)

        @block.vector
        def _(dve):
            dve.memset(credit[:, 2:3], 0.0).then_inc(acc_free, 8)
            dve.memset(credit[:, 3:4], 0.0).then_inc(x_split, 2)
            dve.memset(credit[:, 4:5], 0.0).then_inc(probsT_split, 2)
            dve.memset(credit[:, 5:6], 0.0).then_inc(y_summed, 2)
            dve.memset(credit[:, 6:7], 0.0).then_inc(by_summed, 1)
            for sm in (rope_done, scores_used, h2_done, ple_gated):
                dve.sem_inc(sm, 1)
            dve.memset(trig[:, :, 0, :], 1.0).then_inc(rope_step, 1)
            dve.memset(trig[:, :, 1, :], 0.0).then_inc(rope_step, 1)
            SET0 = 2

            step = [0]

            def chain(ins):
                step[0] += 1
                ins.then_inc(ln_step, 1)
                dve.wait_ge(ln_step, step[0])

            dve.wait_ge(consts_loaded, 16 * 12)
            chain(dve.tensor_copy(bias_row[:, 0:127], bias_row[:, 127:128].to_broadcast([A_HEADS, 127])))
            chain(dve.tensor_copy(small[0:A_HEADS, 0:1], bias_row[:, 127:128]))
            chain(dve.tensor_scalar(bias_row[:, :], bias_row[:, :], small[0:A_HEADS, 0:1], 1.0 / SCALE,
                                    ALU.subtract, ALU.mult))
            chain(dve.tensor_scalar(sink_sb[:, 1, :], sink_sb[:, 0, :], -1.0, None, ALU.mult))
            C1, C2 = 6.28125, 0.0019350051879882812
            C3 = 2 * np.pi - C1 - C2
            ang, kk, prod = work[:, 1, :], swap[:, 0, :], swap[:, 1, :]
            chain(dve.tensor_copy(kk, work[:, 0, :].bitcast(i32)))
            chain(dve.tensor_scalar(ang, kk, rope_c[:, 0:1], None, ALU.mult))
            ROUND = 12582912.0
            chain(dve.tensor_scalar(kk, ang, 1.0 / (2 * np.pi), None, ALU.mult))
            chain(dve.tensor_scalar(kk, kk, ROUND, None, ALU.add))
            chain(dve.tensor_scalar(kk, kk, ROUND, None, ALU.subtract))
            for c in (C1, C2, float(C3)):
                chain(dve.tensor_scalar(prod, kk, c, None, ALU.mult))
                chain(dve.tensor_tensor(ang, ang, prod, ALU.subtract))
            PI = 3.1415925
            dve.tensor_scalar(ang, ang, PI, -PI, ALU.min, ALU.max).then_inc(setup, 1)
            dve.wait_ge(setup, 2)
            chain(dve.tensor_tensor(swap[:, 0, :], swap[:, 0, :], swap[:, 0, :], ALU.mult))
            chain(dve.tensor_scalar(swap[:, 0, :], swap[:, 0, :], -2.0, 1.0, ALU.mult, ALU.add))
            dve.tensor_scalar(swap[:, 1, :], swap[:, 1, :], rope_c[:, 1:2], None, ALU.mult).then_inc(setup, 1)
            CHAINED = step[0]

            def split_w(panel, i, slot, width=PW):
                dve.wait_ge(w_hi_done, 4 * panel + i + 1)
                dve.tensor_tensor(w_lo[:, slot, 2 * i:2 * i + 2, 0:width], w_raw[:, 2 * i:2 * i + 2, 0:width],
                                  w_hi[:, slot, 2 * i:2 * i + 2, 0:width].bitcast(f32), ALU.subtract).then_inc(w_split, 1)

            def split_x(half, c):
                dve.wait_ge(x_hi_done, half * 16 + c + 1)
                at = (slice(None), slice(2 * (c % 4), 2 * (c % 4) + 2), slice((c // 4) * TB, (c // 4) * TB + TB))
                dve.tensor_tensor(x_lo[at], x_raw[:, c % 2, :, :], x_hi[at].bitcast(f32), ALU.subtract
                                  ).then_inc(x_split, 1)

            for i in range(4):
                split_w(0, i, 0)
            dve.wait_ge(setup_stored, 16 * 17)

            with dve.Fori(0, 2) as half:
                base = half * UNITS
                pbase = half * PANELS
                for c in range(16):
                    split_x(half, c)

                def split_unit(unit, bank, slot):
                    dve.wait_ge(unit_act, unit + 1)
                    dve.tensor_tensor(stage_out[:, slot, 1, :].bitcast(f32r), psum[:, bank, :],
                                      stage_out[:, slot, 0, :], ALU.subtract).then_inc(acc_free, 1)

                def panel(w, slot, units, next_width, unit_fn):
                    for r in range(units):
                        unit_fn(r)
                        if r < 4:
                            split_w(pbase + w + 1, r, 1 - slot, next_width)

                with dve.Fori(0, 2) as it:
                    for s in range(2):
                        def fn(r):
                            split_unit(base + 16 * it + 8 * s + r, r, r % 2)
                        panel(2 * it + s, s, 8, PW, fn)
                with dve.Fori(0, 2) as it:
                    for s in range(2):
                        def fn(r):
                            unit = base + 32 + 16 * it + 8 * s + r
                            dve.wait_ge(unit_act, unit + 1)
                            dve.wait_ge(unit_stored[r % 2], 8 * unit - 8 * (r % 2) + 16)
                            dve.tensor_tensor(stage_out[:, r % 2, 0, :], psum[:, r % 8, :], work[:, r % 2, :],
                                              ALU.mult).then_inc(acc_free, 1)
                        panel(4 + 2 * it + s, s, 8, PW, fn)

                def rope_unit(unit, rope, j, tl, slot):
                    row = work[:, slot, :]
                    dve.wait_ge(rope_row, rope + 1)
                    dve.wait_ge(trig_loaded[j % 2], 32 * (half * 6 + tl // 2 + 1))
                    dve.tensor_tensor(swap[:, 1, :], row, trig[:, j % 2, 0, :], ALU.mult).then_inc(rope_step, 1)
                    dve.stream_shuffle(swap[:, 0, :], row, [(i + 8) % 16 if i < 16 else i for i in range(32)]
                                       ).then_inc(rope_step, 1)
                    dve.wait_ge(rope_step, SET0 + 3 * rope + 2)
                    dve.tensor_tensor(swap[:, 0, :], swap[:, 0, :], trig[:, j % 2, 1, :], ALU.mult).then_inc(rope_step, 1)
                    dve.wait_ge(rope_step, SET0 + 3 * rope + 3)
                    dve.tensor_tensor(row, swap[:, 0, :], swap[:, 1, :], ALU.add).then_inc(rope_done, 1)
                    dve.wait_ge(unit_act, unit + 1)
                    dve.tensor_tensor(stage_out[:, slot, 1, :].bitcast(f32r), row, stage_out[:, slot, 0, :],
                                      ALU.subtract).then_inc(acc_free, 1)

                for w in range(2):
                    panel(8 + w, w, 8, PW if w == 0 else P,
                          lambda r: rope_unit(base + 64 + 8 * w + r, half * 20 + 8 * w + r, r // 2, 4 * w + r // 2, r % 2))
                panel(10, 0, 4, P, lambda r: rope_unit(base + 80 + r, half * 20 + 16 + r, r, 8 + r, r % 2))
                panel(11, 1, 4, PW, lambda r: split_unit(base + 84 + r, 4 + r, r % 2))
                for w in range(2):
                    def av_unit(r):
                        dve.wait_ge(unit_act, base + 88 + 8 * w + r + 1)
                        dst = stage_out[:, r % 2, :, :].rearrange("p t (h c d) -> p (t h) c d", c=2, d=HEAD)
                        dve.tensor_tensor(dst[:, :, 1, :].bitcast(f32r),
                                          psum[:, r % 8, :].rearrange("p (h d) -> p h d", d=HEAD),
                                          dst[:, :, 0, :], ALU.subtract).then_inc(acc_free, 1)
                    panel(12 + w, w, 8, PW, av_unit)

            dve.wait_ge(p_over, 1)
            for s in range(2):
                dve.memset(bias[:, s, 0:NBW - 256], 0.0).then_inc(ln_step, 1)
                dve.memset(bias[0:64, s, NBW - 64:NBW], MASKED).then_inc(ln_step, 1)
            dve.wait_ge(ln_step, CHAINED + 4)
            for s in range(2):
                dve.memset(bias[64:128, s, 0:64], MASKED).then_inc(ln_step, 1)
            dve.wait_ge(ln_step, CHAINED + 6)

            def a_step(u0, pair0, i, s, norms0):
                if i < NT:
                    n = min(BAND, i + 1)
                    if i == 0:
                        dve.wait_ge(job_loaded[s], 144 * (norms0 // 32) + 144 if isinstance(norms0, int) else job_wait)
                    dve.wait_ge(scores_done, u0 + i + 1)
                    dve.memset(credit[:, 7:8], 0.0)
                    dve.tensor_tensor_reduce(
                        out=prob[:, i % 4, NBW - n * P:NBW].rearrange("p (a b) -> p a b", a=2),
                        in0=psum[:, 0:2, 0:n * P // 2],
                        in1=bias[:, s, NBW - n * P:NBW].rearrange("p (a b) -> p a b", a=2),
                        scale=1.0, scalar=-3e38, op0=ALU.add, op1=ALU.max,
                        accum_out=small[:, i % 4:i % 4 + 1]).then_inc(scores_used, 1)
                    dve.wait_ge(scores_used, u0 + i + 2)
                    dve.tensor_scalar(small[:, 4 + i % 4:5 + i % 4], small[:, i % 4:i % 4 + 1], -SCALE, None,
                                      ALU.mult).then_inc(shift_ready, 1)
                t = i - 1
                if 0 <= t < NT:
                    n = min(BAND, t + 1)
                    dve.wait_ge(exp_done, u0 + t + 1)
                    dve.reciprocal(small[:, 12 + t % 4:13 + t % 4], small[:, 8 + t % 4:9 + t % 4]).then_inc(recip_ready, 1)
                    if t % 2 == 1:
                        dve.wait_ge(recip_ready, u0 + t + 1)
                        dve.tensor_scalar(prob[:, t % 4, NBW - n * P:NBW], prob[:, t % 4, NBW - n * P:NBW],
                                          small[:, 12 + t % 4:13 + t % 4], None, ALU.mult).then_inc(normed[1], 1)
                t = i - 2
                if 0 <= t < NT:
                    n = min(BAND, t + 1)
                    e = t % 2
                    dve.wait_ge(probsT_hi, u0 + t + 1)
                    at = (slice(None), (t // 2) % 2, slice(e + BAND - n, e + BAND), slice(e * P, e * P + P))
                    src = psum[:, 2 + 2 * e:4 + 2 * e, :].rearrange("p a b -> p (a b)")[:, 0:n * P]
                    dve.tensor_tensor(pt_lo[at], src.rearrange("p (j q) -> p j q", q=P), pt_hi[at].bitcast(f32),
                                      ALU.subtract).then_inc(probsT_split, 1)
                t = i - 4
                if 0 <= t < NT and t % 2 == 1:
                    pr = t // 2
                    dve.wait_ge(y_low_ready, pair0 + pr + 1)
                    if pr % 2 == 0:
                        dve.wait_ge(y_stored[(pr // 2) % 2], quad_wait + 16 * (pr // 4) + 16)
                    dve.tensor_tensor(y_a[:, (pr // 2) % 2, (pr % 2) * 2 * P:(pr % 2 + 1) * 2 * P],
                                      psum[0:HEAD, 6 + pr % 2, 0:2 * P], y_low[:, pr % 2, :], ALU.add).then_inc(y_summed, 1)

            with dve.Fori(0, 4) as it:
                for s in range(2):
                    job_wait = 144 * it + 144
                    quad_wait = 16 * (8 * it + 4 * s)
                    for i in range(NT + 4):
                        a_step(64 * it + 32 * s, 32 * it + 16 * s, i, s, it)

            dve.wait_ge(a_over, 1)
            dve.memset(bk[:, 0, 0:CHUNK].bitcast(f32), 0.0).then_inc(bden_step, 1)
            dve.memset(bvt[:, 0, 0:CHUNK], 0.0).then_inc(bden_step, 1)

            def b_step(u0, pair, i):
                if i < B_UNITS:
                    first = i == 0 and s == 0
                    q = i % 4
                    dve.wait_ge(bscores_done, u0 + i + 1)
                    sc = psum[:, i % 2, :].rearrange("p (c k) -> p c k", k=P)
                    mx = small[:, 4 * q:4 * q + 4]
                    if first:
                        dve.memset(prob_b[:, 0, 0, 0:CHUNK], 0.0)
                        dve.tensor_reduce(out=mx[:, 0:1], in_=sc[:, 0, CHUNK:P], op=ALU.max, axis=AX.X)
                        dve.tensor_reduce(out=mx[:, 1:4], in_=sc[:, 1:4, :], op=ALU.max, axis=AX.X).then_inc(bmax_done, 1)
                    else:
                        dve.tensor_reduce(out=mx, in_=sc, op=ALU.max, axis=AX.X).then_inc(bmax_done, 1)
                    dve.wait_ge(bmax_done, u0 + i + 1)
                    dve.tensor_scalar(small[:, 16 + 4 * q:20 + 4 * q], mx, -SCALE, sink_sb[:, 1, pair:pair + 1],
                                      ALU.mult, ALU.min).then_inc(bshift_ready, 1)
                t = i - 1
                if 0 <= t < B_UNITS:
                    q = t % 4
                    dve.wait_ge(bexp_done, u0 + t + 1)
                    den = small[:, 32 + 4 * q:36 + 4 * q]
                    dve.tensor_tensor(den, den, small[:, 48 + 4 * q:52 + 4 * q], ALU.add).then_inc(bden_step, 1)
                    dve.wait_ge(bden_step, 2 + 2 * (u0 + t) + 1)
                    dve.reciprocal(den, den).then_inc(bden_step, 1)
                    dve.wait_ge(bden_step, 2 + 2 * (u0 + t) + 2)
                    dve.tensor_tensor(prob_b[:, q, :, :], prob_b[:, q, :, :],
                                      den.unsqueeze(2).to_broadcast([P, 4, P]), ALU.mult).then_inc(bnormed, 1)
                t = i - 2
                if 0 <= t < B_UNITS:
                    dve.wait_ge(bprobsT_hi, u0 + t + 1)
                    dve.tensor_tensor(ptb_lo[:, t % 2, :, :].rearrange("p c q -> p (c q)"), psum[:, 2 + t % 2, :],
                                      ptb_hi[:, t % 2, :, :].rearrange("p c q -> p (c q)").bitcast(f32),
                                      ALU.subtract).then_inc(bprobsT_split, 1)
                t = i - 3
                if 0 <= t < B_UNITS:
                    dve.wait_ge(by_low_ready, u0 + t + 1)
                    dve.wait_ge(by_stored[t % 2], 8 * (u0 + t - t % 2))
                    dve.tensor_tensor(y_b[:, t % 2, :, :, :].rearrange("p h c q -> p c h q"),
                                      psum[0:HEAD, 4 + t % 2, :].rearrange("p (c h q) -> p c h q", c=4, h=2),
                                      yb_low[:, t % 2, :].rearrange("p (c h q) -> p c h q", c=4, h=2),
                                      ALU.add).then_inc(by_summed, 1)
                if i < B_UNITS and i % 2 == 1:
                    dve.wait_ge(bv_done, u0 + i + 1)
                    dve.tensor_copy(v_b[:, i % 2, :, :].rearrange("p c d -> p (c d)"), psum[:, 7, :]
                                    ).then_inc(bv_ready, 1)

            for pair in range(4):
                for s in range(2):
                    for i in range(B_UNITS + 3):
                        b_step(16 * pair + 8 * s, pair, i)

            dve.wait_ge(b_over, 1)
            strips = ([(wo_hi, wo_lo, k) for k in range(KT)] + [(wg_hi, wg_lo, k) for k in range(KT)]
                      + [(wp_hi, wp_lo, k) for k in range(2)])
            for n, (hi, lo, k) in enumerate(strips):
                dve.wait_ge(cw_hi_done, n + 1)
                dve.tensor_tensor(lo[:, k, :], y_raw[:, n % 2, :, :].rearrange("p a b -> p (a b)"),
                                  hi[:, k, :].bitcast(f32), ALU.subtract).then_inc(cw_split, 1)
            LN0 = CHAINED + 6
            LN_STEPS = 8

            def y_tile_lo(t, s):
                dve.wait_ge(y_hi_done, t + 1)
                dve.tensor_tensor(y_lo[:, :, :], y_raw[:, s, :, :], y_hi[:, :, :].bitcast(f32), ALU.subtract)
                dve.tensor_tensor(p_lo[:, s, :, :], p_raw[:, s, :, :], p_hi[:, s, :, :].bitcast(f32),
                                  ALU.subtract).then_inc(y_split, 1)

            def residual(t, slot, stored):
                dve.wait_ge(xn_loaded, 16 * t + 16)
                dve.wait_ge(mix_done, t + 1)
                if stored is not None:
                    dve.wait_ge(out_stored[slot], stored + 16)
                dve.scalar_tensor_tensor(h[:, slot, :], x_nat[:, :], ALPHA32,
                                         psum[:, 0:2, :].rearrange("p a b -> p (a b)"), ALU.mult, ALU.add
                                         ).then_inc(h_done, 1)

            def hT_tile_lo(t):
                dve.wait_ge(hT_hi_done, t + 1)
                dve.tensor_tensor(hT_lo[:, :, :].rearrange("p k t -> p (k t)"),
                                  psum[:, 2:4, :].rearrange("p a b -> p (a b)"),
                                  hT_hi[:, :, :].rearrange("p k t -> p (k t)").bitcast(f32),
                                  ALU.subtract).then_inc(hT_split, 1)

            def layer_norm(t, slot):
                hs = h[:, slot, :]
                dve.wait_ge(ple_done, t + 1)
                dve.wait_ge(sig_done, t + 2)
                dve.tensor_tensor(sg[:, :], sg[:, :], psum[:, 6:8, :].rearrange("p a b -> p (a b)"),
                                  ALU.mult).then_inc(ple_gated, 1)
                dve.wait_ge(ple_gated, t + 2)
                dve.tensor_tensor(hs, hs, sg[:, :], ALU.add).then_inc(h2_done, 1)
                dve.wait_ge(h2_done, t + 2)
                dve.bn_stats(small[:, 0:6], hs[:, 0:512]).then_inc(ln_step, 1)
                dve.bn_stats(small[:, 6:12], hs[:, 512:1024]).then_inc(ln_step, 1)
                dve.wait_ge(ln_step, LN0 + LN_STEPS * t + 2)
                dve.memset(credit[:, 7:8], 0.0)
                dve.bn_aggr(small[:, 12:14], small[:, 0:12]).then_inc(ln_step, 1)
                dve.wait_ge(ln_step, LN0 + LN_STEPS * t + 3)
                var, inv, root, tmp = (small[:, c:c + 1] for c in (13, 14, 15, 16))
                dve.tensor_scalar(var, var, LN_EPS, None, ALU.add).then_inc(ln_step, 1)
                dve.wait_ge(ln_step, LN0 + LN_STEPS * t + 4)
                dve.reciprocal(inv, var).then_inc(inverse_done, 1)
                dve.wait_ge(root_done, t + 1)
                dve.tensor_tensor(tmp, root, root, ALU.mult).then_inc(ln_step, 1)
                dve.wait_ge(ln_step, LN0 + LN_STEPS * t + 5)
                dve.tensor_tensor(tmp, tmp, var, ALU.mult).then_inc(ln_step, 1)
                dve.wait_ge(ln_step, LN0 + LN_STEPS * t + 6)
                dve.tensor_scalar(tmp, tmp, -0.5, 1.5, ALU.mult, ALU.add).then_inc(ln_step, 1)
                dve.wait_ge(ln_step, LN0 + LN_STEPS * t + 7)
                dve.tensor_tensor(tmp, tmp, root, ALU.mult).then_inc(ln_step, 1)
                dve.wait_ge(ln_step, LN0 + LN_STEPS * t + 8)
                dve.tensor_scalar(hs, hs, small[:, 12:13], tmp, ALU.subtract, ALU.mult).then_inc(normalized, 1)

            y_tile_lo(0, 0)
            residual(0, 0, None)
            y_tile_lo(1, 1)
            hT_tile_lo(0)
            def c_step(t, i, s, stored):
                y_tile_lo(t + 2, s)
                residual(t + 1, (i + 1) % 3, stored)
                hT_tile_lo(t + 1)
                layer_norm(t, i % 3)
            with dve.Fori(0, 5) as it:
                for i in range(6):
                    c_step(6 * it + i, i, i % 2, 16 * (2 * it + (i + 1) // 3))
            residual(31, 1, 16 * 10)
            hT_tile_lo(31)
            layer_norm(30, 0)
            layer_norm(31, 1)

        @block.tensor
        def _(pe):
            def mm(dst, lhs, rhs, start, stop):
                return pe.matmul(dst, lhs, rhs, start=start, stop=stop)

            with pe.Fori(0, 2) as half:
                base = half * UNITS
                pbase = half * PANELS

                def unit(number, bank, slot, c, j):
                    pe.wait_ge(acc_free, number + 1)
                    for k in range(KT):
                        wh, wl = (w[:, slot, k, c * P:c * P + P] for w in (w_hi, w_lo))
                        xh, xl = (t[:, k, j * TB:j * TB + TB] for t in (x_hi, x_lo))
                        mm(psum[:, bank, :], wh, xh, k == 0, False)
                        mm(psum[:, bank, :], wh, xl, False, False)
                        last = mm(psum[:, bank, :], wl, xh, False, k == KT - 1)
                    last.then_inc(acc_done, 1)

                with pe.Fori(0, 5) as it:
                    for s in range(2):
                        pe.wait_ge(w_split, 4 * (pbase + 2 * it + s + 1))
                        for r in range(8):
                            if s == 0 and r % 2 == 0:
                                pe.wait_ge(x_split, 16 * half + 4 * (r // 2 + 1) + 2)
                            unit(base + 16 * it + 8 * s + r, r, s, r % 2, r // 2)
                for w in range(2):
                    pe.wait_ge(w_split, 4 * (pbase + 11 + w))
                    for r in range(4):
                        unit(base + 80 + 4 * w + r, 4 * w + r, w, 0, r)
                for w in range(2):
                    pe.wait_ge(w_split, 4 * (pbase + 13 + w))
                    for r in range(8):
                        pe.wait_ge(acc_free, base + 88 + 8 * w + r + 1)
                        for tt in range(2):
                            tok = (2 * r + tt) * P
                            dst = psum[:, r, tt * PW:tt * PW + PW]
                            for k in range(KT):
                                xh, xl = (t[:, k, tok:tok + P] for t in (x_hi, x_lo))
                                wh, wl = (t[:, w, k, :] for t in (w_hi, w_lo))
                                mm(dst, xh, wh, k == 0, False)
                                mm(dst, xh, wl, False, False)
                                last = mm(dst, xl, wh, False, k == KT - 1)
                        last.then_inc(acc_done, 1)

            pe.wait_ge(ident_ready, 1)

            def a_scores(u0, t, s):
                n = min(BAND, t + 1)
                w = n * P // 2
                k0 = (t + 1 - n) * P
                pe.wait_ge(scores_used, u0 + t + 1)
                for q in (aq_hi, aq_lo):
                    for a in range(2):
                        last = mm(psum[:, a, 0:w], q[:, s, t * P:t * P + P], ak[:, s, k0 + a * w:k0 + a * w + w],
                                  q is aq_hi, q is aq_lo)
                last.then_inc(scores_done, 1)

            def a_transpose(u0, t, n0):
                n = min(BAND, t + 1)
                e = t % 2
                pe.wait_ge(normed[e], n0 + t // 2 + 1)
                pe.wait_ge(probsT_split, u0 + t + 1)
                for j in range(n):
                    b = 2 + 2 * e + j // 4
                    last = pe.transpose(psum[:, b, (j % 4) * P:(j % 4) * P + P],
                                        prob[:, t % 4, NBW - (n - j) * P:NBW - (n - j - 1) * P], ident[:, :])
                last.then_inc(probsT_done, 1)

            def a_values(u0, pair0, pr, s):
                pe.wait_ge(probsT_split, u0 + 2 * pr + 4)
                pe.wait_ge(y_summed, pair0 + pr + 1)
                first_tile = 2 * pr - (BAND - 1)
                order = [i for i in range(1, BAND) if first_tile + i >= 0]
                order += [i for i in (0, BAND) if first_tile + i >= 0]
                for m, i in enumerate(order):
                    c0, c1 = (0, P) if i == 0 else (P, 2 * P) if i == BAND else (0, 2 * P)
                    for pt in (pt_hi, pt_lo):
                        last = mm(psum[:, 6 + pr % 2, c0:c1], av[:, s, first_tile + i, :], pt[:, pr % 2, i, c0:c1],
                                  m == 0 and pt is pt_hi, m == len(order) - 1 and pt is pt_lo)
                last.then_inc(values_done, 1)

            with pe.Fori(0, 4) as it:
                for s in range(2):
                    u0, pair0 = 64 * it + 32 * s, 32 * it + 16 * s
                    pe.wait_ge(job_loaded[s], 144 * it + 144)
                    a_scores(u0, 0, s)
                    for i in range(NT + 4):
                        if i + 1 < NT:
                            a_scores(u0, i + 1, s)
                        if 0 <= i - 1 < NT:
                            a_transpose(u0, i - 1, pair0)
                        if 0 <= i - 3 < NT and (i - 3) % 2 == 1:
                            a_values(u0, pair0, (i - 3) // 2, s)

            def b_scores(u0, i, s):
                if u0 + i >= 2:
                    pe.wait_ge(bexp_done, u0 + i - 1)
                for c in range(4):
                    t = (4 * i + c) * CHUNK
                    for q in (bq_hi, bq_lo):
                        last = mm(psum[:, i % 2, c * P:c * P + P], q[:, s, 2 * t:2 * t + P], bk[:, s, t:t + P],
                                  q is bq_hi, q is bq_lo)
                last.then_inc(bscores_done, 1)

            def b_v(u0, i, s):
                if u0 + i >= 1:
                    pe.wait_ge(bv_ready, u0 + i)
                if u0 + i >= 2:
                    pe.wait_ge(bvalues_done, u0 + i - 1)
                for c in range(4):
                    t = (4 * i + c) * CHUNK
                    last = pe.transpose(psum[:, 7, c * P:c * P + P], bvt[:, s, t:t + P], ident[:, :])
                last.then_inc(bv_done, 1)

            def b_transpose(u0, t):
                pe.wait_ge(bnormed, u0 + t + 1)
                if u0 + t >= 2:
                    pe.wait_ge(bprobsT_split, u0 + t - 1)
                for c in range(4):
                    last = pe.transpose(psum[:, 2 + t % 2, c * P:c * P + P], prob_b[:, t % 4, c, :], ident[:, :])
                last.then_inc(bprobsT_done, 1)

            def b_values(u0, t, s):
                pe.wait_ge(bprobsT_split, u0 + t + 1)
                pe.wait_ge(bv_ready, u0 + t + 1)
                if u0 + t >= 1:
                    pe.wait_ge(by_summed, u0 + t)
                for c in range(4):
                    for pt in (ptb_hi, ptb_lo):
                        last = mm(psum[:, 4 + t % 2, c * P:c * P + P], v_b[:, t % 2, c, :], pt[:, t % 2, c, :],
                                  pt is ptb_hi, pt is ptb_lo)
                last.then_inc(bvalues_done, 1)

            pe.wait_ge(bden_step, 2)
            for pair in range(4):
                for s in range(2):
                    u0 = 16 * pair + 8 * s
                    pe.wait_ge(bjob_loaded[s], 128 * (pair + 1))
                    b_scores(u0, 0, s)
                    for i in range(B_UNITS + 3):
                        if i + 1 < B_UNITS:
                            b_scores(u0, i + 1, s)
                        if 0 <= i - 1 < B_UNITS:
                            b_transpose(u0, i - 1)
                        if 0 <= i - 2 < B_UNITS:
                            b_values(u0, i - 2, s)
                        if i < B_UNITS:
                            b_v(u0, i, s)

            def product(bank, l_hi, l_lo, r_hi, r_lo, kts):
                for n in range(2):
                    cols = slice(n * 512, n * 512 + 512)
                    dst = psum[:, bank + n, :]
                    for k in range(kts):
                        mm(dst, l_hi[:, k, :], r_hi[:, k, cols], k == 0, False)
                        mm(dst, l_hi[:, k, :], r_lo[:, k, cols], False, False)
                        last = mm(dst, l_lo[:, k, :], r_hi[:, k, cols], False, k == kts - 1)
                return last

            def mix(t):
                pe.wait_ge(y_split, t + 1)
                pe.wait_ge(h_done, t)
                product(0, y_hi, y_lo, wo_hi, wo_lo, KT).then_inc(mix_done, 1)

            def ple(t, s):
                pe.wait_ge(ple_gated, t + 1)
                product(6, p_hi[:, s, :, :], p_lo[:, s, :, :], wp_hi, wp_lo, 2).then_inc(ple_done, 1)

            def gate(t):
                pe.wait_ge(hT_split, t + 1)
                pe.wait_ge(sig_done, t + 1)
                product(4, hT_hi, hT_lo, wg_hi, wg_lo, KT).then_inc(gate_done, 1)

            def transpose_h(t, slot):
                pe.wait_ge(h_done, t + 1)
                for k in range(KT):
                    last = pe.transpose(psum[:, 2 + k // 4, (k % 4) * P:(k % 4) * P + P], h[:, slot, k * P:k * P + P],
                                        ident[:, :])
                last.then_inc(hT_done, 1)

            pe.wait_ge(cw_split, 2 * KT + 2)
            mix(0)
            transpose_h(0, 0)
            with pe.Fori(0, 5) as it:
                for i in range(6):
                    t = 6 * it + i
                    mix(t + 1)
                    ple(t, i % 2)
                    gate(t)
                    transpose_h(t + 1, (i + 1) % 3)
            mix(31)
            ple(30, 0)
            gate(30)
            transpose_h(31, 1)
            ple(31, 1)
            gate(31)


def _rope_const():
    half = ROT // 2
    inv = np.float32(THETA) ** (-np.arange(half, dtype=np.float32) / np.float32(half))
    c = np.zeros((P, 2), np.float32)
    r = np.arange(P) % ROT
    c[:, 0] = inv[r % half]
    c[:, 1] = np.where(r < half, -1.0, 1.0)
    return c


def kernel(x, p, positions, w_in, rel_bias, sinks, w_out, ln_g, ln_b, w_ple_proj, w_ple_gate):
    import concourse.bacc as bacc
    from concourse.bass_utils import run_bass_kernel_spmd

    x, p, positions, w_in, rel_bias, sinks, w_out, ln_g, ln_b, w_ple_proj, w_ple_gate = (
        np.asarray(a) for a in (x, p, positions, w_in, rel_bias, sinks, w_out, ln_g, ln_b, w_ple_proj, w_ple_gate))
    w = w_in[0]
    aq, ak, av, ag, bq, bk, bv, bg = np.split(w, np.cumsum([D_A, D_A, D_A, D_A, D_B, D_KV, D_KV]).tolist(), axis=1)
    arrays = {
        "xT": np.ascontiguousarray(x[0].T),
        "x": np.ascontiguousarray(x[0]),
        "pT": np.ascontiguousarray(p[0, 0].T),
        "pos": np.ascontiguousarray(positions),
        "w_in": np.concatenate([aq, ak, ag, bg, bq, bk, bv, av], axis=1),
        "rel_rev": np.ascontiguousarray(rel_bias[0][:, ::-1]),
        "sinks": np.ascontiguousarray(sinks[0].reshape(B_HEADS // 2, 2).T),
        "w_out": np.ascontiguousarray(w_out[0]),
        "w_gate": np.ascontiguousarray(w_ple_gate[0]),
        "w_ple": np.ascontiguousarray(w_ple_proj[0]),
        "ln_g": np.ascontiguousarray(ln_g),
        "ln_b": np.ascontiguousarray(ln_b),
        "rope_const": _rope_const(),
    }
    nc = bacc.Bacc("TRN2", target_bir_lowering=False, num_devices=1)
    aps = {n: nc.dram_tensor("in_" + n, list(a.shape), mybir.dt.from_np(a.dtype), kind="ExternalInput").ap()
           for n, a in arrays.items()}
    out = nc.dram_tensor("out", [SEQ, D_MODEL], mybir.dt.float32, kind="ExternalOutput").ap()
    build(nc, out=out, **aps)
    r = run_bass_kernel_spmd(nc, [{"in_" + n: a for n, a in arrays.items()}], core_ids=[0])
    return r.results[0]["out"].reshape(1, SEQ, D_MODEL)
```

```python
import numpy as np
import concourse.bass as bass
from concourse import mybir
from contextlib import ExitStack

D_MODEL, SEQ, CHUNK, HEAD = 1024, 4096, 64, 64
A_HEADS, A_LEFT, REL_CLIP = 8, 8, 128
B_HEADS, B_KV = 8, 2
THETA, ROT = 500000.0, 16
PLE = 256
LN_EPS = 1e-5
ALPHA = 2.0 ** 0.25
SCALE = HEAD ** -0.5
MASKED = -1e30

P = 128
KT = D_MODEL // P
TB = 512
HALF = SEQ // 2
JB = HALF // TB
D_A, D_B, D_KV = A_HEADS * HEAD, B_HEADS * HEAD, B_KV * HEAD
COL_QK, COL_G, COL_BQ, COL_BK, COL_BV, COL_AV = 0, 1024, 2048, 2560, 2688, 2816
D_IN = COL_AV + D_A
PW = 256
PANELS = 14
UNITS = 104
ROW_BK, ROW_BV = 1024, 1152
ROWS = 1280

NT = SEQ // P
BAND = A_LEFT // 2 + 1
NBW = BAND * P
QUADS = SEQ // TB
PARTS = 8
PART = NT // PARTS
RING = 8
A_TURN = 2 * NT
A_DRAIN = 9

B_HALF = SEQ // 2
B_UNITS = B_HALF // (4 * CHUNK)
B_ALL = B_HEADS * B_UNITS
STRIPS = 7
B_DRAIN = 9

X_CHUNKS = 4 * JB
X_RING = 3

ALPHA32 = float(np.float32(ALPHA))


def b_unit(u):
    job = u // B_UNITS
    return 2 * (job // 4) + job % 2, job // 2 % 2, u % B_UNITS


def a_unit(turn, i, lag):
    v = i - lag
    if v >= A_TURN or (v < 0 and isinstance(turn, int) and turn == 0):
        return None
    return A_TURN * turn + v, v % A_TURN // NT, v % NT


def build(nc, xT, x, pT, pos, w_in, rel_rev, sinks, w_out, w_gate, w_ple, ln_g, ln_b, rope_const, out):
    f32, f32r, i32 = mybir.dt.float32, mybir.dt.float32r, mybir.dt.int32
    ALU, ACT, AX = mybir.AluOpType, mybir.ActivationFunctionType, mybir.AxisListType

    ctx = ExitStack()
    with ctx:
        def sem(name):
            return ctx.enter_context(nc.semaphore(name))

        def scratch(name, shape):
            return nc.dram_tensor(name, shape, f32, kind="Internal").ap()

        qk_d = scratch("qk_d", [2, ROWS, SEQ])
        bq_d = scratch("bq_d", [B_HEADS // 2, HEAD, SEQ // TB, 2, TB // CHUNK, 2, CHUNK])
        g_d = scratch("g_d", [D_A + D_B, SEQ])
        v_d = scratch("v_d", [SEQ, A_HEADS, 2, HEAD])
        y_d = scratch("y_d", [D_A + D_B, SEQ])
        trig_d = scratch("trig_d", [2, ROT, SEQ])
        bias_d = scratch("bias_d", [A_HEADS, 384])
        bias_q_d = scratch("bias_q_d", [A_HEADS * P, 256])

        psum = ctx.enter_context(nc.psum_tensor("psum", [P, 8, 512], f32))

        ident = ctx.enter_context(nc.sbuf_tensor("ident", [P, P], f32))
        sink_sb = ctx.enter_context(nc.sbuf_tensor("sink_sb", [P, 2, 4], f32))
        small = ctx.enter_context(nc.sbuf_tensor("small", [P, 64], f32))
        credit = ctx.enter_context(nc.sbuf_tensor("credit", [P, 8], f32))
        A_MAX, A_SHIFT, A_SUM, A_RECIP = (small[:, RING * c:RING * c + RING] for c in range(4))

        def a_col(group, r):
            return group[:, r:r + 1]

        stage = ExitStack()

        def sb(name, shape, dt=f32):
            return stage.enter_context(nc.sbuf_tensor(name, shape, dt))

        x_hi, x_lo = (sb(n, [P, KT, HALF], f32r) for n in ("x_hi", "x_lo"))
        x_raw = sb("x_raw", [P, X_RING, 2, TB])
        w_raw = sb("w_raw", [P, KT, PW])
        w_hi, w_lo = (sb(n, [P, 2, KT, PW], f32r) for n in ("w_hi", "w_lo"))
        stage_out = sb("stage_out", [P, 2, 2, TB])
        work = sb("work", [P, 2, TB])
        trig = sb("trig", [P, 2, 2, TB])
        swap = sb("swap", [P, 2, TB])
        bias_row = sb("bias_row", [A_HEADS, 384])
        rope_c = sb("rope_c", [P, 2])
        stage.close()

        aq_hi, aq_lo = (sb(n, [P, 2, SEQ], f32r) for n in ("aq_hi", "aq_lo"))
        ak = sb("ak", [P, 2, SEQ], f32r)
        av = sb("av", [P, 2, NT, P], f32r)
        prob = sb("prob", [P, RING, NBW])
        pt_hi, pt_lo = (sb(n, [P, 2, BAND + 1, 2 * P], f32r) for n in ("pt_hi", "pt_lo"))
        bias = sb("bias", [P, 2, NBW])
        y_low = sb("y_low", [HEAD, 2, 2 * P])
        y_a = sb("y_a", [HEAD, 2, TB])
        g_a = sb("g_a", [HEAD, 2, TB])
        stage.close()

        bq = sb("bq", [P, 2, 2 * B_HALF], f32r)
        bk_hi, bk_lo = (sb(n, [P, 2, SEQ], f32r) for n in ("bk_hi", "bk_lo"))
        bvt = sb("bvt", [P, 2, SEQ])
        prob_b = sb("prob_b", [P, 4, 4, P])
        ptb_hi, ptb_lo = (sb(n, [P, 4, 4, P], f32r) for n in ("ptb_hi", "ptb_lo"))
        v_b = sb("v_b", [P, 4, 4, P], f32r)
        yb_low = sb("yb_low", [HEAD, 2, 4 * P])
        y_b = sb("y_b", [HEAD, 2, 2, 4, CHUNK])
        g_b = sb("g_b", [HEAD, 2, 2, 4 * CHUNK])
        stage.close()

        wo_hi, wo_lo = (sb(n, [P, KT, D_MODEL], f32r) for n in ("wo_hi", "wo_lo"))
        wg_hi, wg_lo = (sb(n, [P, KT, D_MODEL], f32r) for n in ("wg_hi", "wg_lo"))
        wp_hi, wp_lo = (sb(n, [P, 2, D_MODEL], f32r) for n in ("wp_hi", "wp_lo"))
        y_raw = sb("y_raw", [P, 2, KT, P])
        p_raw = sb("p_raw", [P, 2, 2, P])
        y_hi, y_lo = (sb(n, [P, KT, P], f32r) for n in ("y_hi", "y_lo"))
        p_hi, p_lo = (sb(n, [P, 2, 2, P], f32r) for n in ("p_hi", "p_lo"))
        hT_hi, hT_lo = (sb(n, [P, KT, P], f32r) for n in ("hT_hi", "hT_lo"))
        above = ExitStack()
        strip = above.enter_context(nc.sbuf_tensor("strip", [P, STRIPS, D_MODEL], f32))
        above.close()
        x_nat = sb("x_nat", [P, D_MODEL])
        h = sb("h", [P, 3, D_MODEL])
        sg = sb("sg", [P, D_MODEL])
        lng, lnb = (sb(n, [P, D_MODEL]) for n in ("lng", "lnb"))
        stage.close()

        setup = sem("setup")
        ident_ready = sem("ident_ready")
        consts_loaded = sem("consts_loaded")
        setup_stored = sem("setup_stored")
        setup_step = sem("setup_step")
        bias_stored = sem("bias_stored")

        p_over, a_over, b_over = sem("p_over"), sem("a_over"), sem("b_over")

        x_loaded = [sem(f"x_loaded{i}") for i in range(X_RING)]
        x_hi_done, x_split = sem("x_hi_done"), sem("x_split")
        w_loaded = sem("w_loaded")
        w_hi_done, w_split = sem("w_hi_done"), sem("w_split")
        acc_done, acc_free = sem("acc_done"), sem("acc_free")
        unit_act = sem("unit_act")
        unit_stored = [sem(f"unit_stored{i}") for i in range(2)]
        bq_stored = [sem(f"bq_stored{i}") for i in range(2)]
        rope_row, rope_step, rope_done = sem("rope_row"), sem("rope_step"), sem("rope_done")
        trig_loaded = [sem(f"trig_loaded{i}") for i in range(2)]

        first_loaded = [sem(f"first_loaded{i}") for i in range(PARTS)]
        job_loaded = [sem(f"job_loaded{i}") for i in range(2)]
        scores_done, scores_used = sem("scores_done"), sem("scores_used")
        shift_ready, exp_done, recip_ready = sem("shift_ready"), sem("exp_done"), sem("recip_ready")
        normed = [sem(f"normed{i}") for i in range(2)]
        probsT_done, probsT_hi, probsT_split = sem("probsT_done"), sem("probsT_hi"), sem("probsT_split")
        values_done, y_low_ready, y_summed = sem("values_done"), sem("y_low_ready"), sem("y_summed")
        y_gated = sem("y_gated")
        gate_loaded = [sem(f"gate_loaded{i}") for i in range(2)]
        y_stored = [sem(f"y_stored{i}") for i in range(2)]

        bq_loaded, bk_loaded, bv_loaded = ([sem(f"{n}_loaded{i}") for i in range(2)] for n in ("bq", "bk", "bv"))
        bscores_done, bmax_done, bshift_ready = sem("bscores_done"), sem("bmax_done"), sem("bshift_ready")
        bexp_done, bden_step, bnormed = sem("bexp_done"), sem("bden_step"), sem("bnormed")
        bprobsT_done, bprobsT_hi, bprobsT_split = sem("bprobsT_done"), sem("bprobsT_hi"), sem("bprobsT_split")
        bv_done = sem("bv_done")
        bv_ready = [sem(f"bv_ready{i}") for i in range(2)]
        bvalues_done, by_low_ready, by_summed = sem("bvalues_done"), sem("by_low_ready"), sem("by_summed")
        by_gated = sem("by_gated")
        bgate_loaded = [sem(f"bgate_loaded{i}") for i in range(2)]
        by_stored = [sem(f"by_stored{i}") for i in range(2)]

        cw_loaded = [sem(f"cw_loaded{i}") for i in range(STRIPS)]
        cw_hi_done, cw_split = sem("cw_hi_done"), sem("cw_split")
        ln_loaded = sem("ln_loaded")
        y_loaded = [sem(f"y_loaded{i}") for i in range(2)]
        xn_loaded = sem("xn_loaded")
        y_hi_done, y_split = sem("y_hi_done"), sem("y_split")
        mix_done, h_done = sem("mix_done"), sem("h_done")
        hT_done, hT_hi_done, hT_split = sem("hT_done"), sem("hT_hi_done"), sem("hT_split")
        ple_done, gate_done, sig_done = sem("ple_done"), sem("gate_done"), sem("sig_done")
        ple_gated, h2_done = sem("ple_gated"), sem("h2_done")
        ln_step, normalized, scaled = sem("ln_step"), sem("normalized"), sem("scaled")
        shifted = sem("shifted")
        inverse_done, root_done = sem("inverse_done"), sem("root_done")
        out_stored = [sem(f"out_stored{i}") for i in range(3)]

        def split_after(r, units):
            return range(2 * r, 2 * r + 2) if units == 4 and r < 2 else range(r, r + 1) if units == 8 and r < 4 else ()

        def x_after(r):
            return range(2 * (r - 1), 2 * r + (2 if r == 7 else 0)) if r > 0 else ()

        def wait_head(eng, turn, s, t):
            if isinstance(turn, int) and turn == 0 and s == 0:
                if t % PART == 0:
                    eng.wait_ge(first_loaded[t // PART], 16 * (9 if t == 0 else 7))
            elif t == 0:
                eng.wait_ge(job_loaded[s], 144 * (turn + s))

        block = ctx.enter_context(nc.Block())

        @block.sync
        def _(sp):
            for sm in (*unit_stored, *bq_stored, *y_stored, *by_stored, *out_stored):
                sp.sem_inc(sm, 16)
            def load_panel(col, width):
                sp.dma_start(w_raw[:, :, 0:width],
                             w_in[:, bass.ds(col, width)].rearrange("(k p) n -> p k n", p=P)).then_inc(w_loaded, 16)

            load_panel(COL_QK, PW)
            def store_unit(unit, slot, dst, n=2):
                sp.wait_ge(acc_free, unit + 9)
                src = stage_out[:, slot, 0:n, :]
                if n == 1:
                    src = stage_out[:, slot, 0, :]
                sp.dma_start(dst, src).then_inc(unit_stored[slot], 16)

            def load_x_piece(half, c):
                j, kp = c // 4, c % 4
                sp.wait_ge(x_split, half * X_CHUNKS + max(c - X_RING + 1, 0) + 2)
                sp.dma_start(x_raw[:, c % X_RING, :, :],
                             xT[2 * kp * P:2 * kp * P + 2 * P, half * HALF + j * TB:half * HALF + j * TB + TB]
                             .rearrange("(k p) t -> p k t", p=P)).then_inc(x_loaded[c % X_RING], 16)

            for half in range(2):
                base = half * UNITS
                tok = half * HALF
                if half == 0:
                    for c in range(X_CHUNKS):
                        load_x_piece(0, c)

                def next_panel(panel, col, width):
                    sp.wait_ge(w_split, 4 * (half * PANELS + panel))
                    load_panel(col, width)

                def rows(row, j):
                    return qk_d[:, bass.ds(row, P), bass.ds(tok + j * TB, TB)].rearrange("c p t -> p c t")

                with sp.Fori(0, 2) as it:
                    for s in range(2):
                        next_panel(2 * it + s + 1, COL_QK + (2 * it + s + 1) * PW, PW)
                        for r in range(8):
                            store_unit(base + 16 * it + 8 * s + r, r % 2,
                                       rows((2 * it + s) * PW + (r % 2) * P, r // 2))
                with sp.Fori(0, 2) as it:
                    for s in range(2):
                        next_panel(5 + 2 * it + s, COL_G + (2 * it + s + 1) * PW, PW)
                        for r in range(8):
                            store_unit(base + 32 + 16 * it + 8 * s + r, r % 2,
                                       g_d[bass.ds((2 * it + s) * PW + (r % 2) * P, P),
                                           bass.ds(tok + (r // 2) * TB, TB)], 1)

                def load_trig(n):
                    j = n % JB
                    earlier = 0 if n < 2 else 2 * (n - 1) if n <= 9 else n + 7
                    sp.wait_ge(rope_done, half * 20 + earlier + 1)
                    for r0 in (0, HEAD):
                        sp.dma_start(trig[r0:r0 + ROT, j % 2, :, :],
                                     trig_d[:, :, bass.ds(tok + j * TB, TB)].rearrange("c r t -> r c t")
                                     ).then_inc(trig_loaded[j % 2], 16)
                sp.wait_ge(setup_stored, 16 * 17)
                sp.wait_ge(rope_step, 2)
                load_trig(0)
                load_trig(1)
                for w in range(2):
                    if w == 0:
                        next_panel(9, COL_BQ + PW, PW)
                    else:
                        next_panel(10, COL_BK, P)
                    for j in range(JB):
                        for c in range(2):
                            sp.wait_ge(acc_free, base + 64 + 8 * w + 2 * j + c + 9)
                            for hd, stored in ((0, unit_stored), (1, bq_stored)):
                                sp.dma_start(
                                    bq_d[2 * w + c, :, bass.ds(half * JB + j, 1), :, :, hd, :]
                                    .rearrange("d b c n q -> d (b c n) q"),
                                    stage_out[hd * HEAD:hd * HEAD + HEAD, c, :, :]
                                    .rearrange("d c (n q) -> d (c n) q", q=CHUNK)).then_inc(stored[c], 16)
                        load_trig(4 * w + j + 2)
                next_panel(11, COL_BV, P)
                for j in range(JB):
                    store_unit(base + 80 + j, j % 2, rows(ROW_BK, j))
                    if j < 2:
                        load_trig(10 + j)
                    if j == 1:
                        next_panel(12, COL_AV, PW)
                for j in range(JB):
                    store_unit(base + 84 + j, j % 2, rows(ROW_BV, j))
                    if j == 1:
                        next_panel(13, COL_AV + PW, PW)
                for w in range(2):
                    if w == 1:
                        if half == 0:
                            next_panel(14, COL_QK, PW)
                    x_next = w == 1 and half == 0
                    if x_next:
                        for c in range(X_RING):
                            load_x_piece(1, c)
                    for r in range(8):
                        store_unit(base + 88 + 8 * w + r, r % 2,
                                   v_d[bass.ds(tok + r * 2 * P, 2 * P), 4 * w:4 * w + 4, :, :]
                                   .rearrange("(t p) h c d -> p t (h c d)", p=P))
                        if x_next:
                            for c in range(X_RING + 2 * (r - 1), X_RING + 2 * r):
                                if X_RING <= c < X_CHUNKS:
                                    load_x_piece(1, c)

            sp.wait_ge(acc_free, 8 + 2 * UNITS)
            sp.wait_ge(w_split, 4 * 2 * PANELS)
            sp.wait_ge(unit_stored[0], 16 * UNITS)
            sp.wait_ge(unit_stored[1], 16 * UNITS)
            sp.wait_ge(bias_stored, 16)

            def load_bq(job, parts=(0, 1)):
                pair, s, i = b_unit(job * B_UNITS)
                for c in parts:
                    sp.dma_start(bq[c * HEAD:c * HEAD + HEAD, job % 2, :].bitcast(f32)
                                 .rearrange("d (b n) -> d b n", n=2 * TB),
                                 bq_d[pair, :, s * JB:(s + 1) * JB, c, :, :, :]
                                 .rearrange("d b n h q -> d b (n h q)")).then_inc(bq_loaded[job % 2], 16)

            def kv_rows(row, kv, s, c):
                lo_tok, c0, n = (0, CHUNK, B_HALF) if s == 0 else (B_HALF - CHUNK, 0, B_HALF + CHUNK)
                return slice(c0, c0 + n), qk_d[c, row + kv * HEAD:row + kv * HEAD + HEAD, lo_tok:lo_tok + n]

            def load_bk(kv, s, parts=(0, 1)):
                for dst, c in ((bk_hi, 0), (bk_lo, 1)):
                    if c not in parts:
                        continue
                    cols, src = kv_rows(ROW_BK, kv, s, c)
                    for r0 in (0, HEAD):
                        sp.dma_start(dst[r0:r0 + HEAD, s, cols].bitcast(f32), src).then_inc(bk_loaded[s], 16)

            def load_bv(kv, s):
                for c in range(2):
                    cols, src = kv_rows(ROW_BV, kv, s, c)
                    sp.dma_start(bvt[c * HEAD:c * HEAD + HEAD, s, cols], src).then_inc(bv_loaded[s], 16)

            def load_bias(head, s, done):
                for r0, n in ((0, 192), (64, 256)):
                    sp.dma_start(bias[r0:r0 + 64, s, NBW - 256:NBW - 256 + n],
                                 bias_q_d[bass.ds(head * P + r0, 64), 0:n]).then_inc(done, 16)

            def load_job(head, s, piece, done, t0=0, t1=NT):
                cols = slice(t0 * P, t1 * P)
                if piece < 4:
                    dst, c, r0 = ((aq_hi, 0, 0), (aq_hi, 0, HEAD), (aq_lo, 1, 0), (aq_lo, 1, HEAD))[piece]
                    sp.dma_start(dst[r0:r0 + HEAD, s, cols].bitcast(f32), qk_d[c, bass.ds(head * HEAD, HEAD), cols]
                                 ).then_inc(done, 16)
                elif piece < 6:
                    c = piece - 4
                    sp.dma_start(ak[c * HEAD:c * HEAD + HEAD, s, cols].bitcast(f32),
                                 qk_d[c, bass.ds(D_A + head * HEAD, HEAD), cols]).then_inc(done, 16)
                else:
                    sp.dma_start(av[:, s, t0:t1, :].bitcast(f32),
                                 v_d[cols, bass.ds(head, 1), :, :].rearrange("(t p) h c d -> p t (h c d)", p=P)
                                 ).then_inc(done, 16)

            def load_gate(head, q):
                sp.dma_start(g_a[:, q % 2, :], g_d[bass.ds(head * HEAD, HEAD), q * TB:q * TB + TB]
                             ).then_inc(gate_loaded[q % 2], 16)

            def stage_a(it, load_next):
                for s in range(2):
                    quad0 = 16 * it + 8 * s
                    head = 2 * it + s
                    more = load_next or s == 0
                    for q in range(QUADS):
                        sp.wait_ge(y_gated, quad0 + q + 3)
                        sp.dma_start(y_d[bass.ds(head * HEAD, HEAD), q * TB:q * TB + TB], y_a[:, q % 2, :]
                                     ).then_inc(y_stored[q % 2], 16)
                        if q + 2 < QUADS:
                            load_gate(head, q + 2)
                        elif more:
                            load_gate(head + 1, q + 2 - QUADS)
                        if q == 0 and more:
                            load_job(head + 1, 1 - s, 4, job_loaded[1 - s])
                            load_job(head + 1, 1 - s, 5, job_loaded[1 - s])
                        if q == 1 and more:
                            load_job(head + 1, 1 - s, 6, job_loaded[1 - s])
                        if q == QUADS - 2 and load_next:
                            sp.wait_ge(scores_used, A_TURN * it + NT * s + NT + 1)
                            load_job(head + 2, s, 0, job_loaded[s])
                            load_job(head + 2, s, 1, job_loaded[s])
                        if q == QUADS - 1 and load_next:
                            load_job(head + 2, s, 2, job_loaded[s])
                            load_job(head + 2, s, 3, job_loaded[s])
                            load_bias(head + 2, s, job_loaded[s])
                        if not more:
                            if q == 0:
                                load_bq(0)
                            if q == 1:
                                load_bk(0, 0)
                            if q == 2:
                                load_bv(0, 0)

            def first_qk(part):
                for piece in range(6):
                    load_job(0, 0, piece, first_loaded[part], part * PART, (part + 1) * PART)

            def first_v(part):
                load_job(0, 0, 6, first_loaded[part], part * PART, (part + 1) * PART)

            first_qk(0)
            load_bias(0, 0, first_loaded[0])
            for i in range(2):
                sp.wait_ge(unit_stored[i], 16 * UNITS + 16)
                sp.wait_ge(bq_stored[i], 16 * 17)
            first_v(0)
            sp.sem_inc(p_over, 1)
            load_gate(0, 0)
            load_gate(0, 1)
            for part in range(1, PARTS):
                first_qk(part)
                first_v(part)
            for piece in range(4):
                load_job(1, 1, piece, job_loaded[1])
            load_bias(1, 1, job_loaded[1])
            with sp.Fori(0, 3) as it:
                stage_a(it, True)
            stage_a(3, False)
            sp.wait_ge(y_stored[0], 16 * 33)
            sp.wait_ge(y_stored[1], 16 * 33)
            sp.sem_inc(a_over, 1)

            def gated_rows(t, u):
                pair, s, i = b_unit(u)
                t0 = s * B_HALF + i * 4 * CHUNK
                return (t[D_A + pair * P:D_A + pair * P + P, t0:t0 + 4 * CHUNK].rearrange("(h d) t -> d h t", h=2))

            def load_bgate(u):
                sp.wait_ge(by_gated, u + 1)
                sp.dma_start(g_b[:, u % 2, :, :], gated_rows(g_d, u)).then_inc(bgate_loaded[u % 2], 16)

            load_bgate(0)
            load_bq(1)
            load_bk(0, 1)
            load_bv(0, 1)
            strips = ([w_out[k * P:k * P + P, :] for k in range(KT)] + [w_ple[k * P:k * P + P, :] for k in range(2)]
                      + [w_gate[k * P:k * P + P, :] for k in range(KT)])

            def load_strip(n):
                sp.dma_start(strip[:, n % STRIPS, :], strips[n]).then_inc(cw_loaded[n % STRIPS], 16)

            JOBS = B_ALL // B_UNITS
            for step in range(B_ALL + B_DRAIN - 1):
                job, since = (step + 1) // B_UNITS - 1, (step + 1) % B_UNITS
                if job >= 0:
                    half_done = job % 2 == 1 and job < JOBS // 2
                    if since == 0 and job < JOBS:
                        sp.wait_ge(bscores_done, B_UNITS * (job + 1))
                    if since < 2 and job + 2 < JOBS:
                        load_bq(job + 2, (since,))
                    if since in (2, 3) and half_done:
                        load_bk(1, job // 2, (since - 2,))
                    if since == 5 and half_done:
                        sp.wait_ge(bv_done, B_UNITS * (job + 1))
                        load_bv(1, job // 2)
                    if job == JOBS - 3 and since >= 2 or job == JOBS - 2 and since < STRIPS - B_UNITS + 2:
                        load_strip(since - 2 if job == JOBS - 3 else since + B_UNITS - 2)
                u = step - B_DRAIN + 1
                if u >= 0:
                    if u + 1 < B_ALL:
                        load_bgate(u + 1)
                    sp.wait_ge(by_gated, u + 3)
                    sp.dma_start(gated_rows(y_d, u), y_b[:, u % 2, :, :, :].rearrange("p h c q -> p h (c q)")
                                 ).then_inc(by_stored[u % 2], 16)
            sp.wait_ge(by_stored[0], 16 * 33)
            sp.wait_ge(by_stored[1], 16 * 33)
            sp.sem_inc(b_over, 1)

            def load_tile(t, s):
                sp.dma_start(y_raw[:, s, :, :], y_d[:, bass.ds(t * P, P)].rearrange("(k p) t -> p k t", p=P)
                             ).then_inc(y_loaded[s], 16)
                sp.dma_start(p_raw[:, s, :, :], pT[:, bass.ds(t * P, P)].rearrange("(k p) t -> p k t", p=P)
                             ).then_inc(y_loaded[s], 16)

            def load_x(t):
                sp.dma_start(x_nat[:, :], x[bass.ds(t * P, P), :]).then_inc(xn_loaded, 16)

            def store_out(t, slot):
                sp.wait_ge(shifted, t + 1)
                sp.dma_start(out[bass.ds(t * P, P), :], h[:, slot, :]).then_inc(out_stored[slot], 16)

            load_tile(0, 0)
            load_tile(1, 1)
            for n in range(STRIPS, len(strips)):
                sp.wait_ge(cw_split, n - STRIPS + 1)
                load_strip(n)
            sp.wait_ge(cw_split, len(strips))
            load_x(0)
            for dst, src in ((lng, ln_g), (lnb, ln_b)):
                sp.dma_start(dst[:, :], bass.AP(tensor=src.tensor, offset=0, ap=[[0, P], [1, D_MODEL]])
                             ).then_inc(ln_loaded, 16)

            def stage_c(t, i, more):
                if more > 1:
                    sp.wait_ge(y_split, t + 1)
                    load_tile(t + 2, i % 2)
                if more > 0:
                    sp.wait_ge(h_done, t + 1)
                    load_x(t + 1)
                store_out(t, i % 3)

            with sp.Fori(0, 5) as it:
                for i in range(6):
                    stage_c(6 * it + i, i, 2)
            stage_c(30, 0, 1)
            stage_c(31, 1, 0)
            for slot, count in ((0, 11), (1, 11), (2, 10)):
                sp.wait_ge(out_stored[slot], 16 * count + 16)

        @block.gpsimd
        def _(pool):
            pool.memset(ident[:, :], 0.0).then_inc(setup_step, 1)
            pool.wait_ge(setup_step, 1)
            pool.affine_select(out=ident[:, :], in_=ident[:, :], compare_op=ALU.not_equal, fill=1.0, base=0,
                               pattern=[[-1, P]], channel_multiplier=1).then_inc(ident_ready, 1)
            pool.dma_start(rope_c[:, :], rope_const).then_inc(consts_loaded, 16)
            for g in range(SEQ // TB):
                pool.dma_start(work[ROT * g:ROT * g + ROT, 0, :].bitcast(i32),
                               bass.AP(tensor=pos.tensor, offset=TB * g, ap=[[0, ROT], [1, TB]])
                               ).then_inc(consts_loaded, 16)
            pool.dma_start(bias_row[:, 127:384], rel_rev).then_inc(consts_loaded, 16)
            for hd in range(2):
                pool.dma_start(sink_sb[64 * hd:64 * hd + 64, 0, :],
                               bass.AP(tensor=sinks.tensor, offset=4 * hd, ap=[[0, 64], [1, 4]]),
                               ).then_inc(consts_loaded, 16)
            pool.wait_ge(setup, 3)
            for g in range(8):
                for c in range(2):
                    pool.dma_start(trig_d[c, :, TB * g:TB * g + TB], swap[16 * g:16 * g + 16, c, :]
                                   ).then_inc(setup_stored, 16)
            pool.dma_start(bias_d[:, 0:384], bias_row[:, :]).then_inc(setup_stored, 16)
            pool.wait_ge(setup_stored, 16 * 17)
            pool.dma_start(bias_q_d.rearrange("(h q) c -> h q c", q=P),
                           bass.AP(tensor=bias_d.tensor, offset=127, ap=[[384, A_HEADS], [-1, P], [1, 256]])
                           ).then_inc(bias_stored, 16)
            pool.memset(credit[:, 0:1], 0.0).then_inc(y_gated, 2)
            pool.memset(credit[:, 1:2], 0.0).then_inc(by_gated, 2)
            with pool.Fori(0, SEQ // TB * A_HEADS // 2) as it:
                for s in range(2):
                    pool.wait_ge(y_summed, 4 * it + 2 * s + 4)
                    pool.wait_ge(gate_loaded[s], 16 * it + 16)
                    pool.tensor_tensor(y_a[:, s, :], y_a[:, s, :], g_a[:, s, :], ALU.mult).then_inc(y_gated, 1)
            with pool.Fori(0, 32) as it:
                for s in range(2):
                    pool.wait_ge(by_summed, 2 * it + s + 3)
                    pool.wait_ge(bgate_loaded[s], 16 * it + 16)
                    yb = y_b[:, s, :, :, :].rearrange("p h c q -> p (h c q)")
                    pool.tensor_tensor(yb, yb, g_b[:, s, :, :].rearrange("p h t -> p (h t)"),
                                       ALU.mult).then_inc(by_gated, 1)
            pool.wait_ge(ln_loaded, 32)
            def scale_shift(t, slot):
                pool.wait_ge(normalized, t + 1)
                pool.tensor_tensor(h[:, slot, :], h[:, slot, :], lng[:, :], ALU.mult).then_inc(scaled, 1)
                pool.wait_ge(scaled, t + 1)
                pool.tensor_tensor(h[:, slot, :], h[:, slot, :], lnb[:, :], ALU.add).then_inc(shifted, 1)
            with pool.Fori(0, 10) as it:
                for i in range(3):
                    scale_shift(3 * it + i, i)
            scale_shift(30, 0)
            scale_shift(31, 1)

        @block.scalar
        def _(act):
            act.sem_inc(sig_done, 1)

            def split_w(panel, i, slot, width=PW):
                if i == 0:
                    act.wait_ge(w_loaded, 16 * (panel + 1))
                act.activation(w_hi[:, slot, 2 * i:2 * i + 2, 0:width], w_raw[:, 2 * i:2 * i + 2, 0:width],
                               ACT.Copy).then_inc(w_hi_done, 1)

            def split_x(half, c):
                slot = c % X_RING
                in_half = len(range(slot, X_CHUNKS, X_RING))
                act.wait_ge(x_loaded[slot], 16 * (half * in_half + c // X_RING + 1))
                act.activation(x_hi[:, 2 * (c % 4):2 * (c % 4) + 2, (c // 4) * TB:(c // 4) * TB + TB],
                               x_raw[:, slot, :, :], ACT.Copy).then_inc(x_hi_done, 1)

            for i in range(4):
                split_w(0, i, 0)
            for half in range(2):
                base = half * UNITS
                pbase = half * PANELS
                if half == 0:
                    for c in range(X_CHUNKS):
                        split_x(0, c)
                    act.wait_ge(setup, 1)
                    act.activation(swap[:, 1, :], work[:, 1, :], ACT.Sin)
                    act.activation(swap[:, 0, :], work[:, 1, :], ACT.Sin, scale=0.5).then_inc(setup, 1)

                def before(unit, slot):
                    act.wait_ge(acc_done, unit + 1)
                    act.wait_ge(unit_stored[slot], 8 * unit - 8 * slot + 16)

                def split_unit(unit, r):
                    before(unit, r % 2)
                    act.activation(stage_out[:, r % 2, 0, :].bitcast(f32r), psum[:, r % 8, :],
                                   ACT.Copy).then_inc(unit_act, 1)

                def panel(w, slot, units, next_width, unit_fn, last=False):
                    for r in range(units):
                        unit_fn(r)
                        for i in split_after(r, units):
                            if not last or half == 0:
                                split_w(pbase + w + 1, i, 1 - slot, next_width)
                        if last and half == 0:
                            for c in x_after(r):
                                split_x(1, c)

                with act.Fori(0, 2) as it:
                    for s in range(2):
                        def fn(r):
                            split_unit(base + 16 * it + 8 * s + r, r)
                        panel(2 * it + s, s, 8, PW, fn)
                with act.Fori(0, 2) as it:
                    for s in range(2):
                        def fn(r):
                            unit = base + 32 + 16 * it + 8 * s + r
                            act.wait_ge(acc_done, unit + 1)
                            act.wait_ge(acc_free, unit + 7)
                            act.activation(work[:, r % 2, :], psum[:, r % 8, :], ACT.Sigmoid).then_inc(unit_act, 1)
                        panel(4 + 2 * it + s, s, 8, PW, fn)

                def rope_unit(unit, n, bank, slot):
                    rope = half * 20 + n
                    act.wait_ge(acc_done, unit + 1)
                    act.wait_ge(acc_free, unit + 7)
                    act.activation(work[:, slot, :], psum[:, bank, :], ACT.Copy).then_inc(rope_row, 1)
                    act.wait_ge(rope_done, rope + 2)
                    act.wait_ge(unit_stored[slot], 8 * unit - 8 * slot + 16)
                    act.wait_ge(bq_stored[slot], half * 128 + 8 * (min(n, 16 + slot) - slot) + 16)
                    act.activation(stage_out[:, slot, 0, :].bitcast(f32r), work[:, slot, :],
                                   ACT.Copy).then_inc(unit_act, 1)

                for w in range(2):
                    panel(8 + w, w, 8, PW if w == 0 else P,
                          lambda r: rope_unit(base + 64 + 8 * w + r, 8 * w + r, r % 8, r % 2))
                panel(10, 0, 4, P, lambda r: rope_unit(base + 80 + r, 16 + r, r, r % 2))

                def bv(r):
                    before(base + 84 + r, r % 2)
                    act.activation(stage_out[:, r % 2, 0, :].bitcast(f32r), psum[:, 4 + r, :],
                                   ACT.Copy).then_inc(unit_act, 1)
                panel(11, 1, 4, PW, bv)
                for w in range(2):
                    def av_unit(r):
                        before(base + 88 + 8 * w + r, r % 2)
                        dst = stage_out[:, r % 2, :, :].bitcast(f32r).rearrange("p t (h c d) -> p (t h) c d", c=2, d=HEAD)
                        act.activation(dst[:, :, 0, :], psum[:, r % 8, :].rearrange("p (h d) -> p h d", d=HEAD),
                                       ACT.Copy).then_inc(unit_act, 1)
                    panel(12 + w, w, 8, PW, av_unit, w == 1)

            def a_step(it, i):
                unit = a_unit(it, i, 1)
                if unit:
                    u, s, t = unit
                    n, r = min(BAND, t + 1), t % RING
                    act.wait_ge(shift_ready, u + 1)
                    act.activation(prob[:, r, NBW - n * P:NBW], prob[:, r, NBW - n * P:NBW], ACT.Exp,
                                   bias=a_col(A_SHIFT, r), scale=SCALE, accum_out=a_col(A_SUM, r)).then_inc(exp_done, 1)
                unit = a_unit(it, i, 7)
                if unit and unit[2] % 2 == 1:
                    u, s, t = unit
                    pr = t // 2
                    act.wait_ge(values_done, (A_TURN // 2) * it + (i - 7) // 2 + 1)
                    act.wait_ge(y_summed, (A_TURN // 2) * it + (i - 7) // 2 + 1)
                    act.activation(y_low[:, pr % 2, :], psum[HEAD:P, 6 + pr % 2, 0:2 * P],
                                   ACT.Copy).then_inc(y_low_ready, 1)
                unit = a_unit(it, i, 4)
                if unit:
                    u, s, t = unit
                    n, e = min(BAND, t + 1), t % 2
                    act.wait_ge(probsT_done, u + 1)
                    src = psum[:, 2 + 2 * e:4 + 2 * e, :].rearrange("p a b -> p (a b)")[:, 0:n * P]
                    act.activation(pt_hi[:, (t // 2) % 2, e + BAND - n:e + BAND, e * P:e * P + P],
                                   src.rearrange("p (j q) -> p j q", q=P), ACT.Copy).then_inc(probsT_hi, 1)

                unit = a_unit(it, i, 2)
                if unit and unit[2] % 2 == 0:
                    u, s, t = unit
                    n, r = min(BAND, t + 1), t % RING
                    act.wait_ge(recip_ready, u + 1)
                    act.activation(prob[:, r, NBW - n * P:NBW], prob[:, r, NBW - n * P:NBW], ACT.Copy,
                                   scale=a_col(A_RECIP, r)).then_inc(normed[0], 1)

            for i in range(A_TURN):
                a_step(0, i)
            with act.Fori(1, A_HEADS // 2) as it:
                for i in range(A_TURN):
                    a_step(it, i)
            for i in range(A_TURN, A_TURN + A_DRAIN):
                a_step(A_HEADS // 2 - 1, i)

            def b_step(step):
                u = step - 7
                if 0 <= u < B_ALL:
                    act.wait_ge(bvalues_done, u + 1)
                    act.wait_ge(by_summed, u + 1)
                    act.activation(yb_low[:, u % 2, :], psum[HEAD:P, 4 + u % 2, :], ACT.Copy).then_inc(by_low_ready, 1)
                u = step - 1
                if 0 <= u < B_ALL:
                    act.wait_ge(bshift_ready, u + 1)
                    pair, s, i = b_unit(u)
                    q = u % 4
                    for c in range(4):
                        lo = CHUNK if s == 0 and i == 0 and c == 0 else 0
                        act.activation(prob_b[:, q, c, lo:P], psum[:, u % 2, c * P + lo:c * P + P], ACT.Exp,
                                       bias=small[:, 16 + 4 * q + c:17 + 4 * q + c], scale=SCALE,
                                       accum_out=small[:, 32 + 4 * q + c:33 + 4 * q + c])
                    act.activation(small[:, 48 + 4 * q:52 + 4 * q], small[:, 16 + 4 * q:20 + 4 * q], ACT.Exp,
                                   bias=sink_sb[:, 0, pair:pair + 1], scale=1.0).then_inc(bexp_done, 1)
                u = step - 4
                if 0 <= u < B_ALL:
                    act.wait_ge(bprobsT_done, u + 1)
                    act.activation(ptb_hi[:, u % 4, :, :].rearrange("p c q -> p (c q)"), psum[:, 2 + u % 2, :],
                                   ACT.Copy).then_inc(bprobsT_hi, 1)

                u = step - 4
                if 0 <= u < B_ALL and u % 2 == 0:
                    act.wait_ge(bv_done, u + 1)
                    act.activation(v_b[:, u % 4, :, :].rearrange("p c d -> p (c d)"), psum[:, 6, :],
                                   ACT.Copy).then_inc(bv_ready[0], 1)
            act.wait_ge(a_over, 1)
            for step in range(B_ALL + B_DRAIN):
                b_step(step)

            act.wait_ge(b_over, 1)
            strips = ([(wo_hi, k) for k in range(KT)] + [(wp_hi, k) for k in range(2)] + [(wg_hi, k) for k in range(KT)])

            def strip_hi(n):
                dst, k = strips[n]
                act.wait_ge(cw_loaded[n % STRIPS], 16 * (n // STRIPS + 1))
                act.activation(dst[:, k, :], strip[:, n % STRIPS, :], ACT.Copy).then_inc(cw_hi_done, 1)

            def y_tile_hi(t, s, first=False):
                act.wait_ge(y_loaded[s], 32 * (t // 2 + 1) if isinstance(t, int) else 16 * (t - s) + 32)
                if not first:
                    act.wait_ge(mix_done, t)
                act.activation(y_hi[:, :, :], y_raw[:, s, :, :], ACT.Copy)
                if not isinstance(t, int):
                    act.wait_ge(ple_done, t - 1)
                act.activation(p_hi[:, s, :, :], p_raw[:, s, :, :], ACT.Copy).then_inc(y_hi_done, 1)

            def hT_tile_hi(t):
                act.wait_ge(hT_done, t + 1)
                act.activation(hT_hi[:, :, :].rearrange("p k t -> p (k t)"),
                               psum[:, 2:4, :].rearrange("p a b -> p (a b)"), ACT.Copy).then_inc(hT_hi_done, 1)

            def sigmoid(t):
                act.wait_ge(gate_done, t + 1)
                act.wait_ge(h2_done, t + 1)
                act.activation(sg[:, :], psum[:, 4:6, :].rearrange("p a b -> p (a b)"), ACT.Sigmoid).then_inc(sig_done, 1)

            def root(t):
                act.wait_ge(inverse_done, t + 1)
                act.activation(small[:, 15:16], small[:, 14:15], ACT.Sqrt).then_inc(root_done, 1)

            strip_hi(0)
            y_tile_hi(0, 0, True)
            for n in range(1, len(strips)):
                strip_hi(n)
            y_tile_hi(1, 1)
            hT_tile_hi(0)
            with act.Fori(0, 15) as it:
                for s in range(2):
                    t = 2 * it + s
                    y_tile_hi(t + 2, s)
                    sigmoid(t)
                    hT_tile_hi(t + 1)
                    root(t)
            sigmoid(30)
            hT_tile_hi(31)
            root(30)
            sigmoid(31)
            root(31)

        @block.vector
        def _(dve):
            dve.memset(credit[:, 2:3], 0.0).then_inc(acc_free, 8)
            dve.memset(credit[:, 3:4], 0.0).then_inc(x_split, 2)
            dve.memset(credit[:, 4:5], 0.0).then_inc(probsT_split, 2)
            dve.memset(credit[:, 5:6], 0.0).then_inc(y_summed, 2)
            dve.memset(credit[:, 6:7], 0.0).then_inc(by_summed, 2)
            for sm in (rope_done, scores_used, h2_done, ple_gated):
                dve.sem_inc(sm, 1)
            dve.memset(trig[:, :, 0, :], 1.0).then_inc(rope_step, 1)
            dve.memset(trig[:, :, 1, :], 0.0).then_inc(rope_step, 1)
            SET0 = 2

            def split_w(panel, i, slot, width=PW):
                dve.wait_ge(w_hi_done, 4 * panel + i + 1)
                dve.tensor_tensor(w_lo[:, slot, 2 * i:2 * i + 2, 0:width], w_raw[:, 2 * i:2 * i + 2, 0:width],
                                  w_hi[:, slot, 2 * i:2 * i + 2, 0:width].bitcast(f32), ALU.subtract).then_inc(w_split, 1)


            step = [0]

            def chain(ins):
                step[0] += 1
                ins.then_inc(ln_step, 1)
                dve.wait_ge(ln_step, step[0])

            def tables():

                dve.wait_ge(consts_loaded, 16 * 12)
                chain(dve.tensor_copy(bias_row[:, 0:127], bias_row[:, 127:128].to_broadcast([A_HEADS, 127])))
                chain(dve.tensor_copy(small[0:A_HEADS, 0:1], bias_row[:, 127:128]))
                chain(dve.tensor_scalar(bias_row[:, :], bias_row[:, :], small[0:A_HEADS, 0:1], 1.0 / SCALE,
                                        ALU.subtract, ALU.mult))
                chain(dve.tensor_scalar(sink_sb[:, 1, :], sink_sb[:, 0, :], -1.0, None, ALU.mult))
                C1, C2 = 6.28125, 0.0019350051879882812
                C3 = 2 * np.pi - C1 - C2
                ang, kk, prod = work[:, 1, :], swap[:, 0, :], swap[:, 1, :]
                chain(dve.tensor_copy(kk, work[:, 0, :].bitcast(i32)))
                chain(dve.tensor_scalar(ang, kk, rope_c[:, 0:1], None, ALU.mult))
                ROUND = 12582912.0
                chain(dve.tensor_scalar(kk, ang, 1.0 / (2 * np.pi), None, ALU.mult))
                chain(dve.tensor_scalar(kk, kk, ROUND, None, ALU.add))
                chain(dve.tensor_scalar(kk, kk, ROUND, None, ALU.subtract))
                for c in (C1, C2, float(C3)):
                    chain(dve.tensor_scalar(prod, kk, c, None, ALU.mult))
                    chain(dve.tensor_tensor(ang, ang, prod, ALU.subtract))
                PI = 3.1415925
                dve.tensor_scalar(ang, ang, PI, -PI, ALU.min, ALU.max).then_inc(setup, 1)
                dve.wait_ge(setup, 2)
                chain(dve.tensor_tensor(swap[:, 0, :], swap[:, 0, :], swap[:, 0, :], ALU.mult))
                chain(dve.tensor_scalar(swap[:, 0, :], swap[:, 0, :], -2.0, 1.0, ALU.mult, ALU.add))
                dve.tensor_scalar(swap[:, 1, :], swap[:, 1, :], rope_c[:, 1:2], None, ALU.mult).then_inc(setup, 1)

            for i in range(4):
                split_w(0, i, 0)

            def split_x(half, c):
                dve.wait_ge(x_hi_done, half * 16 + c + 1)
                at = (slice(None), slice(2 * (c % 4), 2 * (c % 4) + 2), slice((c // 4) * TB, (c // 4) * TB + TB))
                dve.tensor_tensor(x_lo[at], x_raw[:, c % X_RING, :, :], x_hi[at].bitcast(f32), ALU.subtract
                                  ).then_inc(x_split, 1)


            for half in range(2):
                base = half * UNITS
                pbase = half * PANELS
                if half == 0:
                    for c in range(X_CHUNKS):
                        split_x(0, c)
                    tables()

                def split_unit(unit, bank, slot):
                    dve.wait_ge(unit_act, unit + 1)
                    dve.tensor_tensor(stage_out[:, slot, 1, :].bitcast(f32r), psum[:, bank, :],
                                      stage_out[:, slot, 0, :], ALU.subtract).then_inc(acc_free, 1)

                def panel(w, slot, units, next_width, unit_fn, last=False):
                    for r in range(units):
                        unit_fn(r)
                        for i in split_after(r, units):
                            if not last or half == 0:
                                split_w(pbase + w + 1, i, 1 - slot, next_width)
                        if last and half == 0:
                            for c in x_after(r):
                                split_x(1, c)

                with dve.Fori(0, 2) as it:
                    for s in range(2):
                        def fn(r):
                            split_unit(base + 16 * it + 8 * s + r, r, r % 2)
                        panel(2 * it + s, s, 8, PW, fn)
                dve.wait_ge(setup_stored, 16 * 17)
                with dve.Fori(0, 2) as it:
                    for s in range(2):
                        def fn(r):
                            unit = base + 32 + 16 * it + 8 * s + r
                            dve.wait_ge(unit_act, unit + 1)
                            dve.wait_ge(unit_stored[r % 2], 8 * unit - 8 * (r % 2) + 16)
                            dve.tensor_tensor(stage_out[:, r % 2, 0, :], psum[:, r % 8, :], work[:, r % 2, :],
                                              ALU.mult).then_inc(acc_free, 1)
                        panel(4 + 2 * it + s, s, 8, PW, fn)

                def rope_unit(unit, rope, j, tl, slot):
                    row = work[:, slot, :]
                    dve.wait_ge(rope_row, rope + 1)
                    dve.wait_ge(trig_loaded[j % 2], 32 * (half * 6 + tl // 2 + 1))
                    dve.tensor_tensor(swap[:, 1, :], row, trig[:, j % 2, 0, :], ALU.mult).then_inc(rope_step, 1)
                    dve.stream_shuffle(swap[:, 0, :], row, [(i + 8) % 16 if i < 16 else i for i in range(32)]
                                       ).then_inc(rope_step, 1)
                    dve.wait_ge(rope_step, SET0 + 3 * rope + 2)
                    dve.tensor_tensor(swap[:, 0, :], swap[:, 0, :], trig[:, j % 2, 1, :], ALU.mult).then_inc(rope_step, 1)
                    dve.wait_ge(rope_step, SET0 + 3 * rope + 3)
                    dve.tensor_tensor(row, swap[:, 0, :], swap[:, 1, :], ALU.add).then_inc(rope_done, 1)
                    dve.wait_ge(unit_act, unit + 1)
                    dve.tensor_tensor(stage_out[:, slot, 1, :].bitcast(f32r), row, stage_out[:, slot, 0, :],
                                      ALU.subtract).then_inc(acc_free, 1)

                for w in range(2):
                    panel(8 + w, w, 8, PW if w == 0 else P,
                          lambda r: rope_unit(base + 64 + 8 * w + r, half * 20 + 8 * w + r, r // 2, 4 * w + r // 2, r % 2))
                panel(10, 0, 4, P, lambda r: rope_unit(base + 80 + r, half * 20 + 16 + r, r, 8 + r, r % 2))
                panel(11, 1, 4, PW, lambda r: split_unit(base + 84 + r, 4 + r, r % 2))
                for w in range(2):
                    def av_unit(r):
                        dve.wait_ge(unit_act, base + 88 + 8 * w + r + 1)
                        dst = stage_out[:, r % 2, :, :].rearrange("p t (h c d) -> p (t h) c d", c=2, d=HEAD)
                        dve.tensor_tensor(dst[:, :, 1, :].bitcast(f32r),
                                          psum[:, r % 8, :].rearrange("p (h d) -> p h d", d=HEAD),
                                          dst[:, :, 0, :], ALU.subtract).then_inc(acc_free, 1)
                    panel(12 + w, w, 8, PW, av_unit, w == 1)

            CHAINED = step[0]

            dve.wait_ge(p_over, 1)
            for s in range(2):
                dve.memset(bias[:, s, 0:NBW - 256], 0.0).then_inc(ln_step, 1)
                dve.memset(bias[0:64, s, NBW - 64:NBW], MASKED).then_inc(ln_step, 1)
            dve.wait_ge(ln_step, CHAINED + 4)
            for s in range(2):
                dve.memset(bias[64:128, s, 0:64], MASKED).then_inc(ln_step, 1)
            dve.wait_ge(ln_step, CHAINED + 6)

            def a_step(it, i):
                unit = a_unit(it, i, 5)
                if unit:
                    u, s, t = unit
                    n, e = min(BAND, t + 1), t % 2
                    dve.wait_ge(probsT_hi, u + 1)
                    at = (slice(None), (t // 2) % 2, slice(e + BAND - n, e + BAND), slice(e * P, e * P + P))
                    src = psum[:, 2 + 2 * e:4 + 2 * e, :].rearrange("p a b -> p (a b)")[:, 0:n * P]
                    dve.tensor_tensor(pt_lo[at], src.rearrange("p (j q) -> p j q", q=P), pt_hi[at].bitcast(f32),
                                      ALU.subtract).then_inc(probsT_split, 1)
                unit = a_unit(it, i, 0)
                if unit:
                    u, s, t = unit
                    n, r = min(BAND, t + 1), t % RING
                    if t == 0:
                        wait_head(dve, it, s, t)
                    dve.wait_ge(scores_done, u + 1)
                    dve.memset(credit[:, 7:8], 0.0)
                    dve.tensor_tensor_reduce(
                        out=prob[:, r, NBW - n * P:NBW].rearrange("p (a b) -> p a b", a=2),
                        in0=psum[:, 0:2, 0:n * P // 2],
                        in1=bias[:, s, NBW - n * P:NBW].rearrange("p (a b) -> p a b", a=2),
                        scale=1.0, scalar=-3e38, op0=ALU.add, op1=ALU.max,
                        accum_out=a_col(A_MAX, r)).then_inc(scores_used, 1)
                unit = a_unit(it, i, 2)
                if unit:
                    u, s, t = unit
                    dve.wait_ge(exp_done, u + 1)
                    dve.reciprocal(a_col(A_RECIP, t % RING), a_col(A_SUM, t % RING)).then_inc(recip_ready, 1)
                unit = a_unit(it, i, 0)
                if unit:
                    u, s, t = unit
                    dve.wait_ge(scores_used, u + 2)
                    dve.tensor_scalar(a_col(A_SHIFT, t % RING), a_col(A_MAX, t % RING), -SCALE, None,
                                      ALU.mult).then_inc(shift_ready, 1)
                unit = a_unit(it, i, 2)
                if unit and unit[2] % 2 == 1:
                    u, s, t = unit
                    n, r = min(BAND, t + 1), t % RING
                    dve.wait_ge(recip_ready, u + 1)
                    dve.tensor_scalar(prob[:, r, NBW - n * P:NBW], prob[:, r, NBW - n * P:NBW],
                                      a_col(A_RECIP, r), None, ALU.mult).then_inc(normed[1], 1)
                unit = a_unit(it, i, A_DRAIN - 1)
                if unit and unit[2] % 2 == 1:
                    u, s, t = unit
                    pr = t // 2
                    dve.wait_ge(y_low_ready, (A_TURN // 2) * it + (i - A_DRAIN + 1) // 2 + 1)
                    if pr % 2 == 0:
                        quad = (i - A_DRAIN + 1) // 4
                        dve.wait_ge(y_stored[(pr // 2) % 2], 16 * (8 * it + quad // 2 + 1))
                    dve.tensor_tensor(y_a[:, (pr // 2) % 2, (pr % 2) * 2 * P:(pr % 2 + 1) * 2 * P],
                                      psum[0:HEAD, 6 + pr % 2, 0:2 * P], y_low[:, pr % 2, :], ALU.add).then_inc(y_summed, 1)

            for i in range(A_TURN):
                a_step(0, i)
            with dve.Fori(1, A_HEADS // 2) as it:
                for i in range(A_TURN):
                    a_step(it, i)
            for i in range(A_TURN, A_TURN + A_DRAIN):
                a_step(A_HEADS // 2 - 1, i)

            dve.wait_ge(a_over, 1)
            dve.memset(bk_hi[:, 0, 0:CHUNK].bitcast(f32), 0.0).then_inc(bden_step, 1)
            dve.memset(bk_lo[:, 0, 0:CHUNK].bitcast(f32), 0.0).then_inc(bden_step, 1)
            dve.memset(bvt[:, 0, 0:CHUNK], 0.0).then_inc(bden_step, 1)

            BDEN0 = 3

            def b_step(step):
                u = step - 8
                if 0 <= u < B_ALL:
                    dve.wait_ge(by_low_ready, u + 1)
                    dve.wait_ge(by_stored[u % 2], 16 * (u // 2 + 1))
                    dve.tensor_tensor(y_b[:, u % 2, :, :, :].rearrange("p h c q -> p c h q"),
                                      psum[0:HEAD, 4 + u % 2, :].rearrange("p (c h q) -> p c h q", c=4, h=2),
                                      yb_low[:, u % 2, :].rearrange("p (c h q) -> p c h q", c=4, h=2),
                                      ALU.add).then_inc(by_summed, 1)
                u = step - 5
                if 0 <= u < B_ALL:
                    dve.wait_ge(bprobsT_hi, u + 1)
                    dve.tensor_tensor(ptb_lo[:, u % 4, :, :].rearrange("p c q -> p (c q)"), psum[:, 2 + u % 2, :],
                                      ptb_hi[:, u % 4, :, :].rearrange("p c q -> p (c q)").bitcast(f32),
                                      ALU.subtract).then_inc(bprobsT_split, 1)
                u = step
                if u < B_ALL:
                    pair, s, i = b_unit(u)
                    dve.wait_ge(bscores_done, u + 1)
                    sc = psum[:, u % 2, :].rearrange("p (c k) -> p c k", k=P)
                    mx = small[:, 4 * (u % 4):4 * (u % 4) + 4]
                    if s == 0 and i == 0:
                        if u >= 4:
                            dve.wait_ge(bprobsT_done, u - 3)
                        dve.memset(prob_b[:, 0, 0, 0:CHUNK], 0.0)
                        dve.tensor_reduce(out=mx[:, 0:1], in_=sc[:, 0, CHUNK:P], op=ALU.max, axis=AX.X)
                        dve.tensor_reduce(out=mx[:, 1:4], in_=sc[:, 1:4, :], op=ALU.max, axis=AX.X).then_inc(bmax_done, 1)
                    else:
                        dve.tensor_reduce(out=mx, in_=sc, op=ALU.max, axis=AX.X).then_inc(bmax_done, 1)
                u = step - 2
                den = small[:, 32 + 4 * (u % 4):36 + 4 * (u % 4)]
                if 0 <= u < B_ALL:
                    dve.wait_ge(bexp_done, u + 1)
                    dve.tensor_tensor(den, den, small[:, 48 + 4 * (u % 4):52 + 4 * (u % 4)], ALU.add).then_inc(bden_step, 1)
                u = step
                if u < B_ALL:
                    dve.wait_ge(bmax_done, u + 1)
                    dve.tensor_scalar(small[:, 16 + 4 * (u % 4):20 + 4 * (u % 4)], small[:, 4 * (u % 4):4 * (u % 4) + 4],
                                      -SCALE, sink_sb[:, 1, pair:pair + 1], ALU.mult, ALU.min).then_inc(bshift_ready, 1)
                u = step - 2
                if 0 <= u < B_ALL:
                    dve.wait_ge(bden_step, BDEN0 + 2 * u + 1)
                    dve.reciprocal(den, den).then_inc(bden_step, 1)
                u = step - 2
                if 0 <= u < B_ALL:
                    dve.wait_ge(bden_step, BDEN0 + 2 * u + 2)
                    dve.tensor_tensor(prob_b[:, u % 4, :, :], prob_b[:, u % 4, :, :],
                                      den.unsqueeze(2).to_broadcast([P, 4, P]), ALU.mult).then_inc(bnormed, 1)
                u = step - 4
                if 0 <= u < B_ALL and u % 2 == 1:
                    dve.wait_ge(bv_done, u + 1)
                    dve.tensor_copy(v_b[:, u % 4, :, :].rearrange("p c d -> p (c d)"), psum[:, 7, :]
                                    ).then_inc(bv_ready[1], 1)

            for step in range(B_ALL + B_DRAIN):
                b_step(step)

            dve.wait_ge(b_over, 1)
            strips = ([(wo_hi, wo_lo, k) for k in range(KT)] + [(wp_hi, wp_lo, k) for k in range(2)]
                      + [(wg_hi, wg_lo, k) for k in range(KT)])

            def strip_lo(n):
                hi, lo, k = strips[n]
                dve.wait_ge(cw_hi_done, n + 1)
                dve.tensor_tensor(lo[:, k, :], strip[:, n % STRIPS, :], hi[:, k, :].bitcast(f32),
                                  ALU.subtract).then_inc(cw_split, 1)
            LN0 = CHAINED + 6
            LN_STEPS = 8

            def y_tile_lo(t, s):
                dve.wait_ge(y_hi_done, t + 1)
                dve.tensor_tensor(y_lo[:, :, :], y_raw[:, s, :, :], y_hi[:, :, :].bitcast(f32), ALU.subtract)
                dve.tensor_tensor(p_lo[:, s, :, :], p_raw[:, s, :, :], p_hi[:, s, :, :].bitcast(f32),
                                  ALU.subtract).then_inc(y_split, 1)

            def residual(t, slot, stored):
                dve.wait_ge(xn_loaded, 16 * t + 16)
                dve.wait_ge(mix_done, t + 1)
                if stored is not None:
                    dve.wait_ge(out_stored[slot], stored + 16)
                dve.scalar_tensor_tensor(h[:, slot, :], x_nat[:, :], ALPHA32,
                                         psum[:, 0:2, :].rearrange("p a b -> p (a b)"), ALU.mult, ALU.add
                                         ).then_inc(h_done, 1)

            def hT_tile_lo(t):
                dve.wait_ge(hT_hi_done, t + 1)
                dve.tensor_tensor(hT_lo[:, :, :].rearrange("p k t -> p (k t)"),
                                  psum[:, 2:4, :].rearrange("p a b -> p (a b)"),
                                  hT_hi[:, :, :].rearrange("p k t -> p (k t)").bitcast(f32),
                                  ALU.subtract).then_inc(hT_split, 1)

            def layer_norm(t, slot):
                hs = h[:, slot, :]
                dve.wait_ge(ple_done, t + 1)
                dve.wait_ge(sig_done, t + 2)
                dve.tensor_tensor(sg[:, :], sg[:, :], psum[:, 6:8, :].rearrange("p a b -> p (a b)"),
                                  ALU.mult).then_inc(ple_gated, 1)
                dve.wait_ge(ple_gated, t + 2)
                dve.tensor_tensor(hs, hs, sg[:, :], ALU.add).then_inc(h2_done, 1)
                dve.wait_ge(h2_done, t + 2)
                dve.bn_stats(small[:, 0:6], hs[:, 0:512]).then_inc(ln_step, 1)
                dve.bn_stats(small[:, 6:12], hs[:, 512:1024]).then_inc(ln_step, 1)
                dve.wait_ge(ln_step, LN0 + LN_STEPS * t + 2)
                dve.memset(credit[:, 7:8], 0.0)
                dve.bn_aggr(small[:, 12:14], small[:, 0:12]).then_inc(ln_step, 1)
                dve.wait_ge(ln_step, LN0 + LN_STEPS * t + 3)
                var, inv, root, tmp = (small[:, c:c + 1] for c in (13, 14, 15, 16))
                dve.tensor_scalar(var, var, LN_EPS, None, ALU.add).then_inc(ln_step, 1)
                dve.wait_ge(ln_step, LN0 + LN_STEPS * t + 4)
                dve.reciprocal(inv, var).then_inc(inverse_done, 1)
                dve.wait_ge(root_done, t + 1)
                dve.tensor_tensor(tmp, root, root, ALU.mult).then_inc(ln_step, 1)
                dve.wait_ge(ln_step, LN0 + LN_STEPS * t + 5)
                dve.tensor_tensor(tmp, tmp, var, ALU.mult).then_inc(ln_step, 1)
                dve.wait_ge(ln_step, LN0 + LN_STEPS * t + 6)
                dve.tensor_scalar(tmp, tmp, -0.5, 1.5, ALU.mult, ALU.add).then_inc(ln_step, 1)
                dve.wait_ge(ln_step, LN0 + LN_STEPS * t + 7)
                dve.tensor_tensor(tmp, tmp, root, ALU.mult).then_inc(ln_step, 1)
                dve.wait_ge(ln_step, LN0 + LN_STEPS * t + 8)
                dve.tensor_scalar(hs, hs, small[:, 12:13], tmp, ALU.subtract, ALU.mult).then_inc(normalized, 1)

            strip_lo(0)
            y_tile_lo(0, 0)
            for n in range(1, len(strips)):
                strip_lo(n)
            residual(0, 0, None)
            y_tile_lo(1, 1)
            hT_tile_lo(0)
            def c_step(t, i, s, stored):
                y_tile_lo(t + 2, s)
                residual(t + 1, (i + 1) % 3, stored)
                hT_tile_lo(t + 1)
                layer_norm(t, i % 3)
            with dve.Fori(0, 5) as it:
                for i in range(6):
                    c_step(6 * it + i, i, i % 2, 16 * (2 * it + (i + 1) // 3))
            residual(31, 1, 16 * 10)
            hT_tile_lo(31)
            layer_norm(30, 0)
            layer_norm(31, 1)

        @block.tensor
        def _(pe):
            def mm(dst, lhs, rhs, start, stop):
                return pe.matmul(dst, lhs, rhs, start=start, stop=stop)

            for half in range(2):
                base = half * UNITS
                pbase = half * PANELS

                def unit(number, bank, slot, c, j):
                    pe.wait_ge(acc_free, number + 1)
                    for k in range(KT):
                        wh, wl = (w[:, slot, k, c * P:c * P + P] for w in (w_hi, w_lo))
                        xh, xl = (t[:, k, j * TB:j * TB + TB] for t in (x_hi, x_lo))
                        mm(psum[:, bank, :], wh, xh, k == 0, False)
                        mm(psum[:, bank, :], wh, xl, False, False)
                        last = mm(psum[:, bank, :], wl, xh, False, k == KT - 1)
                    last.then_inc(acc_done, 1)

                with pe.Fori(0, 5) as it:
                    for s in range(2):
                        pe.wait_ge(w_split, 4 * (pbase + 2 * it + s + 1))
                        for r in range(8):
                            if s == 0 and r % 2 == 0:
                                pe.wait_ge(x_split, 16 * half + 4 * (r // 2 + 1) + 2)
                            unit(base + 16 * it + 8 * s + r, r, s, r % 2, r // 2)
                for w in range(2):
                    pe.wait_ge(w_split, 4 * (pbase + 11 + w))
                    for r in range(4):
                        unit(base + 80 + 4 * w + r, 4 * w + r, w, 0, r)
                for w in range(2):
                    pe.wait_ge(w_split, 4 * (pbase + 13 + w))
                    for r in range(8):
                        pe.wait_ge(acc_free, base + 88 + 8 * w + r + 1)
                        for tt in range(2):
                            tok = (2 * r + tt) * P
                            dst = psum[:, r, tt * PW:tt * PW + PW]
                            for k in range(KT):
                                xh, xl = (t[:, k, tok:tok + P] for t in (x_hi, x_lo))
                                wh, wl = (t[:, w, k, :] for t in (w_hi, w_lo))
                                mm(dst, xh, wh, k == 0, False)
                                mm(dst, xh, wl, False, False)
                                last = mm(dst, xl, wh, False, k == KT - 1)
                        last.then_inc(acc_done, 1)

            pe.wait_ge(ident_ready, 1)

            def a_scores(u, s, t):
                n = min(BAND, t + 1)
                w = n * P // 2
                k0 = (t + 1 - n) * P
                pe.wait_ge(scores_used, u + 1)
                for q in (aq_hi, aq_lo):
                    for a in range(2):
                        last = mm(psum[:, a, 0:w], q[:, s, t * P:t * P + P], ak[:, s, k0 + a * w:k0 + a * w + w],
                                  q is aq_hi, q is aq_lo)
                last.then_inc(scores_done, 1)

            def a_transpose(u, t, norms):
                n = min(BAND, t + 1)
                e = t % 2
                pe.wait_ge(normed[e], norms)
                pe.wait_ge(probsT_split, u + 1)
                for j in range(n):
                    b = 2 + 2 * e + j // 4
                    last = pe.transpose(psum[:, b, (j % 4) * P:(j % 4) * P + P],
                                        prob[:, t % RING, NBW - (n - j) * P:NBW - (n - j - 1) * P], ident[:, :])
                last.then_inc(probsT_done, 1)

            def a_values(u, pair, s, pr):
                pe.wait_ge(probsT_split, u + 3)
                pe.wait_ge(y_summed, pair + 1)
                first_tile = 2 * pr - (BAND - 1)
                order = [i for i in range(1, BAND) if first_tile + i >= 0]
                order += [i for i in (0, BAND) if first_tile + i >= 0]
                for m, i in enumerate(order):
                    c0, c1 = (0, P) if i == 0 else (P, 2 * P) if i == BAND else (0, 2 * P)
                    for pt in (pt_hi, pt_lo):
                        last = mm(psum[:, 6 + pr % 2, c0:c1], av[:, s, first_tile + i, :], pt[:, pr % 2, i, c0:c1],
                                  m == 0 and pt is pt_hi, m == len(order) - 1 and pt is pt_lo)
                last.then_inc(values_done, 1)

            def a_step(it, i):
                unit = a_unit(it, i, 6)
                if unit and unit[2] % 2 == 1:
                    u, s, t = unit
                    a_values(u, (A_TURN // 2) * it + (i - 6) // 2, s, t // 2)
                unit = a_unit(it, i, 3)
                if unit:
                    u, s, t = unit
                    a_transpose(u, t, (A_TURN // 2) * it + (i - 3) // 2 + 1)

                unit = a_unit(it, i, -1)
                if unit:
                    u, s, t = unit
                    wait_head(pe, it, s, t)
                    a_scores(u, s, t)
            for i in range(-1, A_TURN - 1):
                a_step(0, i)
            with pe.Fori(1, A_HEADS // 2) as it:
                for i in range(-1, A_TURN - 1):
                    a_step(it, i)
            for i in range(A_TURN - 1, A_TURN + A_DRAIN):
                a_step(A_HEADS // 2 - 1, i)

            def b_scores(u):
                pair, s, i = b_unit(u)
                job = u // B_UNITS
                if i == 0:
                    pe.wait_ge(bq_loaded[job % 2], 32 * (job // 2 + 1))
                    pe.wait_ge(bk_loaded[s], 64 * (pair // 2 + 1))
                if u >= 2:
                    pe.wait_ge(bexp_done, u - 1)
                for c in range(4):
                    t = (4 * i + c) * CHUNK
                    for bk in (bk_hi, bk_lo):
                        last = mm(psum[:, u % 2, c * P:c * P + P], bq[:, job % 2, 2 * t:2 * t + P], bk[:, s, t:t + P],
                                  bk is bk_hi, bk is bk_lo)
                last.then_inc(bscores_done, 1)

            def b_v(u):
                pair, s, i = b_unit(u)
                if i == 0:
                    pe.wait_ge(bv_loaded[s], 32 * (pair // 2 + 1))
                if u >= 2:
                    pe.wait_ge(bv_ready[u % 2], u // 2)
                for c in range(4):
                    t = (4 * i + c) * CHUNK
                    last = pe.transpose(psum[:, 6 + u % 2, c * P:c * P + P], bvt[:, s, t:t + P], ident[:, :])
                last.then_inc(bv_done, 1)

            def b_transpose(u):
                pe.wait_ge(bnormed, u + 1)
                if u >= 2:
                    pe.wait_ge(bprobsT_split, u - 1)
                for c in range(4):
                    last = pe.transpose(psum[:, 2 + u % 2, c * P:c * P + P], prob_b[:, u % 4, c, :], ident[:, :])
                last.then_inc(bprobsT_done, 1)

            def b_values(u):
                pe.wait_ge(bprobsT_split, u + 1)
                pe.wait_ge(bv_ready[u % 2], u // 2 + 1)
                pe.wait_ge(by_summed, u + 1)
                for c in range(4):
                    for pt in (ptb_hi, ptb_lo):
                        last = mm(psum[:, 4 + u % 2, c * P:c * P + P], v_b[:, u % 4, c, :], pt[:, u % 4, c, :],
                                  pt is ptb_hi, pt is ptb_lo)
                last.then_inc(bvalues_done, 1)

            pe.wait_ge(bden_step, 3)
            for step in range(-1, B_ALL + B_DRAIN):
                for fn, lag in ((b_values, 6), (b_transpose, 3), (b_v, 3), (b_scores, -1)):
                    if 0 <= step - lag < B_ALL:
                        fn(step - lag)

            def product(bank, l_hi, l_lo, r_hi, r_lo, kts, split0=None):
                for n in range(2):
                    cols = slice(n * 512, n * 512 + 512)
                    dst = psum[:, bank + n, :]
                    for k in range(kts):
                        if split0 is not None and n == 0:
                            pe.wait_ge(cw_split, split0 + k + 1)
                        mm(dst, l_hi[:, k, :], r_hi[:, k, cols], k == 0, False)
                        mm(dst, l_hi[:, k, :], r_lo[:, k, cols], False, False)
                        last = mm(dst, l_lo[:, k, :], r_hi[:, k, cols], False, k == kts - 1)
                return last

            def mix(t, split0=None):
                pe.wait_ge(y_split, t + 1)
                if split0 is None:
                    pe.wait_ge(h_done, t)
                product(0, y_hi, y_lo, wo_hi, wo_lo, KT, split0).then_inc(mix_done, 1)

            def ple(t, s):
                pe.wait_ge(ple_gated, t + 1)
                product(6, p_hi[:, s, :, :], p_lo[:, s, :, :], wp_hi, wp_lo, 2).then_inc(ple_done, 1)

            def gate(t):
                pe.wait_ge(hT_split, t + 1)
                pe.wait_ge(sig_done, t + 1)
                product(4, hT_hi, hT_lo, wg_hi, wg_lo, KT).then_inc(gate_done, 1)

            def transpose_h(t, slot):
                pe.wait_ge(h_done, t + 1)
                for k in range(KT):
                    last = pe.transpose(psum[:, 2 + k // 4, (k % 4) * P:(k % 4) * P + P], h[:, slot, k * P:k * P + P],
                                        ident[:, :])
                last.then_inc(hT_done, 1)

            mix(0, 0)
            pe.wait_ge(cw_split, 2 * KT + 2)
            transpose_h(0, 0)
            with pe.Fori(0, 5) as it:
                for i in range(6):
                    t = 6 * it + i
                    mix(t + 1)
                    ple(t, i % 2)
                    gate(t)
                    transpose_h(t + 1, (i + 1) % 3)
            mix(31)
            ple(30, 0)
            gate(30)
            transpose_h(31, 1)
            ple(31, 1)
            gate(31)


def _rope_const():
    half = ROT // 2
    inv = np.float32(THETA) ** (-np.arange(half, dtype=np.float32) / np.float32(half))
    c = np.zeros((P, 2), np.float32)
    r = np.arange(P) % ROT
    c[:, 0] = inv[r % half]
    c[:, 1] = np.where(r < half, -1.0, 1.0)
    return c


def kernel(x, p, positions, w_in, rel_bias, sinks, w_out, ln_g, ln_b, w_ple_proj, w_ple_gate):
    import concourse.bacc as bacc
    from concourse.bass_utils import run_bass_kernel_spmd

    x, p, positions, w_in, rel_bias, sinks, w_out, ln_g, ln_b, w_ple_proj, w_ple_gate = (
        np.asarray(a) for a in (x, p, positions, w_in, rel_bias, sinks, w_out, ln_g, ln_b, w_ple_proj, w_ple_gate))
    w = w_in[0]
    aq, ak, av, ag, bq, bk, bv, bg = np.split(w, np.cumsum([D_A, D_A, D_A, D_A, D_B, D_KV, D_KV]).tolist(), axis=1)
    arrays = {
        "xT": np.ascontiguousarray(x[0].T),
        "x": np.ascontiguousarray(x[0]),
        "pT": np.ascontiguousarray(p[0, 0].T),
        "pos": np.ascontiguousarray(positions),
        "w_in": np.concatenate([aq, ak, ag, bg, bq, bk, bv, av], axis=1),
        "rel_rev": np.ascontiguousarray(rel_bias[0][:, ::-1]),
        "sinks": np.ascontiguousarray(sinks[0].reshape(B_HEADS // 2, 2).T),
        "w_out": np.ascontiguousarray(w_out[0]),
        "w_gate": np.ascontiguousarray(w_ple_gate[0]),
        "w_ple": np.ascontiguousarray(w_ple_proj[0]),
        "ln_g": np.ascontiguousarray(ln_g),
        "ln_b": np.ascontiguousarray(ln_b),
        "rope_const": _rope_const(),
    }
    nc = bacc.Bacc("TRN2", target_bir_lowering=False, num_devices=1)
    aps = {n: nc.dram_tensor("in_" + n, list(a.shape), mybir.dt.from_np(a.dtype), kind="ExternalInput").ap()
           for n, a in arrays.items()}
    out = nc.dram_tensor("out", [SEQ, D_MODEL], mybir.dt.float32, kind="ExternalOutput").ap()
    build(nc, out=out, **aps)
    r = run_bass_kernel_spmd(nc, [{"in_" + n: a for n, a in arrays.items()}], core_ids=[0])
    return r.results[0]["out"].reshape(1, SEQ, D_MODEL)
```

```python
import numpy as np
import concourse.bass as bass
from concourse import mybir
from contextlib import ExitStack

D_MODEL, SEQ, CHUNK, HEAD = 1024, 4096, 64, 64
A_HEADS, A_LEFT, REL_CLIP = 8, 8, 128
B_HEADS, B_KV = 8, 2
THETA, ROT = 500000.0, 16
PLE = 256
LN_EPS = 1e-5
ALPHA = 2.0 ** 0.25
SCALE = HEAD ** -0.5
MASKED = -1e30

P = 128
KT = D_MODEL // P
TB = 512
HALF = SEQ // 2
JB = HALF // TB
D_A, D_B, D_KV = A_HEADS * HEAD, B_HEADS * HEAD, B_KV * HEAD
COL_QK, COL_G, COL_BQ, COL_BK, COL_BV, COL_AV = 0, 1024, 2048, 2560, 2688, 2816
D_IN = COL_AV + D_A
PW = 256
PANELS = 14
UNITS = 104
ROW_BK, ROW_BV = 1024, 1152
ROWS = 1280

NT = SEQ // P
BAND = A_LEFT // 2 + 1
NBW = BAND * P
QUADS = SEQ // TB
PARTS = 8
PART = NT // PARTS
VECTOR_NORMS = (1, 3, 5)
QSLOTS = 4
RING = 8
A_TURN = 2 * NT
A_DRAIN = 10

B_HALF = SEQ // 2
B_UNITS = B_HALF // (4 * CHUNK)
B_ALL = B_HEADS * B_UNITS
DRAIN_STRIPS = 7
DRAIN_LOADS = 4
STRIPS = 7
B_DRAIN = 9

X_CHUNKS = 4 * JB
X_RING = 3

ALPHA32 = float(np.float32(ALPHA))


def norms(v, by_vector):
    n = (v + 1) // 8 * len(VECTOR_NORMS) + sum(t < (v + 1) % 8 for t in VECTOR_NORMS)
    return n if by_vector else v + 1 - n


def b_unit(u):
    kv, half, i = u // (4 * B_UNITS), u // (2 * B_UNITS) % 2, u // 2 % B_UNITS
    return 2 * kv + u % 2, half, i


def a_unit(turn, i, lag):
    v = i - lag
    if v >= A_TURN or (v < 0 and isinstance(turn, int) and turn == 0):
        return None
    return A_TURN * turn + v, v % A_TURN // NT, v % NT


def build(nc, xT, x, pT, pos, w_in, rel_rev, sinks, w_out, w_gate, w_ple, ln_g, ln_b, rope_const, out):
    f32, f32r, i32 = mybir.dt.float32, mybir.dt.float32r, mybir.dt.int32
    ALU, ACT, AX = mybir.AluOpType, mybir.ActivationFunctionType, mybir.AxisListType

    ctx = ExitStack()
    with ctx:
        def sem(name):
            return ctx.enter_context(nc.semaphore(name))

        def scratch(name, shape):
            return nc.dram_tensor(name, shape, f32, kind="Internal").ap()

        qk_d = scratch("qk_d", [2, ROWS, SEQ])
        bq_d = scratch("bq_d", [B_HEADS // 2, HEAD, SEQ // TB, 2, TB // CHUNK, 2, CHUNK])
        g_d = scratch("g_d", [D_A + D_B, SEQ])
        v_d = scratch("v_d", [SEQ, A_HEADS, 2, HEAD])
        y_d = scratch("y_d", [D_A + D_B, SEQ])
        trig_d = scratch("trig_d", [2, ROT, SEQ])
        bias_d = scratch("bias_d", [A_HEADS, 384])
        bias_q_d = scratch("bias_q_d", [A_HEADS * P, 256])

        psum = ctx.enter_context(nc.psum_tensor("psum", [P, 8, 512], f32))

        ident = ctx.enter_context(nc.sbuf_tensor("ident", [P, P], f32))
        sink_sb = ctx.enter_context(nc.sbuf_tensor("sink_sb", [P, 2, 4], f32))
        small = ctx.enter_context(nc.sbuf_tensor("small", [P, 64], f32))
        credit = ctx.enter_context(nc.sbuf_tensor("credit", [P, 8], f32))
        A_MAX, A_SHIFT, A_SUM, A_RECIP = (small[:, RING * c:RING * c + RING] for c in range(4))

        def a_col(group, r):
            return group[:, r:r + 1]

        stage = ExitStack()

        def sb(name, shape, dt=f32):
            return stage.enter_context(nc.sbuf_tensor(name, shape, dt))

        x_hi, x_lo = (sb(n, [P, KT, HALF], f32r) for n in ("x_hi", "x_lo"))
        x_raw = sb("x_raw", [P, X_RING, 2, TB])
        w_raw = sb("w_raw", [P, KT, PW])
        w_hi, w_lo = (sb(n, [P, 2, KT, PW], f32r) for n in ("w_hi", "w_lo"))
        stage_out = sb("stage_out", [P, 2, 2, TB])
        work = sb("work", [P, 2, TB])
        trig = sb("trig", [P, 2, 2, TB])
        swap = sb("swap", [P, 2, TB])
        bias_row = sb("bias_row", [A_HEADS, 384])
        rope_c = sb("rope_c", [P, 2])
        stage.close()

        aq_hi, aq_lo = (sb(n, [P, 2, SEQ], f32r) for n in ("aq_hi", "aq_lo"))
        ak = sb("ak", [P, 2, SEQ], f32r)
        av = sb("av", [P, 2, NT, P], f32r)
        prob = sb("prob", [P, RING, NBW])
        pt_hi, pt_lo = (sb(n, [P, 2, BAND + 1, 2 * P], f32r) for n in ("pt_hi", "pt_lo"))
        y_low = sb("y_low", [HEAD, 2, 2 * P])
        y_a = sb("y_a", [HEAD, QSLOTS, TB])
        g_a = sb("g_a", [HEAD, QSLOTS, TB])
        bias = sb("bias", [P, 2, NBW])
        stage.close()

        bq = sb("bq", [P, 2, 2 * B_HALF], f32r)
        bk_hi, bk_lo = (sb(n, [P, 2, SEQ], f32r) for n in ("bk_hi", "bk_lo"))
        bvt = sb("bvt", [P, 2, SEQ])
        prob_b = sb("prob_b", [P, 4, 4, P])
        ptb_hi, ptb_lo = (sb(n, [P, 4, 4, P], f32r) for n in ("ptb_hi", "ptb_lo"))
        v_b = sb("v_b", [P, 4, 4, P], f32r)
        yb_low = sb("yb_low", [HEAD, 2, 4 * P])
        y_b = sb("y_b", [HEAD, 2, 2, 4, CHUNK])
        g_b = sb("g_b", [HEAD, 2, 2, 4 * CHUNK])
        stage.close()

        wo_hi, wo_lo = (sb(n, [P, KT, D_MODEL], f32r) for n in ("wo_hi", "wo_lo"))
        wg_hi, wg_lo = (sb(n, [P, KT, D_MODEL], f32r) for n in ("wg_hi", "wg_lo"))
        wp_hi, wp_lo = (sb(n, [P, 2, D_MODEL], f32r) for n in ("wp_hi", "wp_lo"))
        y_raw = sb("y_raw", [P, 2, KT, P])
        p_raw = sb("p_raw", [P, 2, 2, P])
        y_hi, y_lo = (sb(n, [P, KT, P], f32r) for n in ("y_hi", "y_lo"))
        p_hi, p_lo = (sb(n, [P, 2, 2, P], f32r) for n in ("p_hi", "p_lo"))
        hT_hi = sb("hT_hi", [P, KT, P], f32r)
        x_nat = sb("x_nat", [P, D_MODEL])
        above = ExitStack()
        strip = above.enter_context(nc.sbuf_tensor("strip", [P, STRIPS, D_MODEL], f32))
        above.close()
        hT_lo = sb("hT_lo", [P, KT, P], f32r)
        sg = sb("sg", [P, D_MODEL])
        lng, lnb = (sb(n, [P, D_MODEL]) for n in ("lng", "lnb"))
        h = sb("h", [P, 3, D_MODEL])
        stage.close()

        setup = sem("setup")
        ident_ready = sem("ident_ready")
        consts_loaded = sem("consts_loaded")
        setup_stored = sem("setup_stored")
        setup_step = sem("setup_step")
        bias_stored = sem("bias_stored")

        p_over, b_over = sem("p_over"), sem("b_over")

        x_loaded = [sem(f"x_loaded{i}") for i in range(X_RING)]
        x_hi_done, x_split = sem("x_hi_done"), sem("x_split")
        w_loaded = sem("w_loaded")
        w_hi_done, w_split = sem("w_hi_done"), sem("w_split")
        acc_done, acc_free = sem("acc_done"), sem("acc_free")
        unit_act = sem("unit_act")
        unit_stored = [sem(f"unit_stored{i}") for i in range(2)]
        bq_stored = [sem(f"bq_stored{i}") for i in range(2)]
        rope_row, rope_step, rope_done = sem("rope_row"), sem("rope_step"), sem("rope_done")
        trig_loaded = [sem(f"trig_loaded{i}") for i in range(2)]

        first_loaded = [sem(f"first_loaded{i}") for i in range(PARTS)]
        job_loaded = [sem(f"job_loaded{i}") for i in range(2)]
        scores_done, scores_used = sem("scores_done"), sem("scores_used")
        shift_ready, exp_done, recip_ready = sem("shift_ready"), sem("exp_done"), sem("recip_ready")
        normed = [sem(f"normed{i}") for i in range(2)]
        probsT_done, probsT_hi, probsT_split = sem("probsT_done"), sem("probsT_hi"), sem("probsT_split")
        values_done, y_low_ready, y_summed = sem("values_done"), sem("y_low_ready"), sem("y_summed")
        y_gated = sem("y_gated")
        gate_loaded = [sem(f"gate_loaded{i}") for i in range(QSLOTS)]
        y_stored = [sem(f"y_stored{i}") for i in range(QSLOTS)]

        bq_loaded = [sem(f"bq_loaded{i}") for i in range(JB)]
        bk_loaded, bv_loaded = ([sem(f"{n}_loaded{i}") for i in range(2)] for n in ("bk", "bv"))
        bscores_done, bmax_done, bshift_ready = sem("bscores_done"), sem("bmax_done"), sem("bshift_ready")
        bexp_done, bden_step, bnormed = sem("bexp_done"), sem("bden_step"), sem("bnormed")
        bprobsT_done, bprobsT_hi, bprobsT_split = sem("bprobsT_done"), sem("bprobsT_hi"), sem("bprobsT_split")
        bv_done = sem("bv_done")
        bv_ready = sem("bv_ready")
        bvalues_done, by_low_ready, by_summed = sem("bvalues_done"), sem("by_low_ready"), sem("by_summed")
        by_gated = sem("by_gated")
        bgate_loaded = [sem(f"bgate_loaded{i}") for i in range(2)]
        by_stored = [sem(f"by_stored{i}") for i in range(2)]

        cw_loaded = [sem(f"cw_loaded{i}") for i in range(STRIPS)]
        cw_hi_done, cw_split = sem("cw_hi_done"), sem("cw_split")
        ln_loaded = sem("ln_loaded")
        y_loaded, p_loaded = ([sem(f"{n}_loaded{i}") for i in range(2)] for n in ("y", "p"))
        xn_loaded = sem("xn_loaded")
        y_hi_done, y_split = sem("y_hi_done"), sem("y_split")
        p_hi_done, p_split = sem("p_hi_done"), sem("p_split")
        mix_done, h_done = sem("mix_done"), sem("h_done")
        hT_done, hT_hi_done, hT_split = sem("hT_done"), sem("hT_hi_done"), sem("hT_split")
        ple_done, gate_done, sig_done = sem("ple_done"), sem("gate_done"), sem("sig_done")
        ple_gated, h2_done = sem("ple_gated"), sem("h2_done")
        ln_step, normalized, scaled = sem("ln_step"), sem("normalized"), sem("scaled")
        shifted = sem("shifted")
        last_scaled, last_shifted = sem("last_scaled"), sem("last_shifted")
        inverse_done, root_done = sem("inverse_done"), sem("root_done")
        out_stored = [sem(f"out_stored{i}") for i in range(3)]

        def split_after(r, units):
            return range(2 * r, 2 * r + 2) if units == 4 and r < 2 else range(r, r + 1) if units == 8 and r < 4 else ()

        def x_after(r):
            return range(2 * (r - 1), 2 * r + (2 if r == 7 else 0)) if r > 0 else ()

        def wait_head(eng, turn, s, t):
            if isinstance(turn, int) and turn == 0 and s == 0:
                if t % PART == 0:
                    eng.wait_ge(first_loaded[t // PART], 16 * (9 if t == 0 else 7))
            elif t == 0:
                eng.wait_ge(job_loaded[s], 144 * (turn + s))

        block = ctx.enter_context(nc.Block())

        @block.sync
        def _(sp):
            for sm in (*unit_stored, *bq_stored, *y_stored, *by_stored, *out_stored):
                sp.sem_inc(sm, 16)

            def load_panel(col, width):
                sp.dma_start(w_raw[:, :, 0:width],
                             w_in[:, bass.ds(col, width)].rearrange("(k p) n -> p k n", p=P)).then_inc(w_loaded, 16)

            load_panel(COL_QK, PW)

            def store_unit(unit, slot, dst, n=2):
                sp.wait_ge(acc_free, unit + 9)
                src = stage_out[:, slot, 0:n, :]
                if n == 1:
                    src = stage_out[:, slot, 0, :]
                sp.dma_start(dst, src).then_inc(unit_stored[slot], 16)

            def load_x_piece(half, c):
                j, kp = c // 4, c % 4
                sp.wait_ge(x_split, half * X_CHUNKS + max(c - X_RING + 1, 0) + 2)
                sp.dma_start(x_raw[:, c % X_RING, :, :],
                             xT[2 * kp * P:2 * kp * P + 2 * P, half * HALF + j * TB:half * HALF + j * TB + TB]
                             .rearrange("(k p) t -> p k t", p=P)).then_inc(x_loaded[c % X_RING], 16)

            def load_bias(head, s, done):
                for r0, n in ((0, 192), (64, 256)):
                    sp.dma_start(bias[r0:r0 + 64, s, NBW - 256:NBW - 256 + n],
                                 bias_q_d[bass.ds(head * P + r0, 64), 0:n]).then_inc(done, 16)

            def load_job(head, s, piece, done, t0=0, t1=NT):
                cols = slice(t0 * P, t1 * P)
                if piece < 4:
                    dst, c, r0 = ((aq_hi, 0, 0), (aq_hi, 0, HEAD), (aq_lo, 1, 0), (aq_lo, 1, HEAD))[piece]
                    sp.dma_start(dst[r0:r0 + HEAD, s, cols].bitcast(f32), qk_d[c, bass.ds(head * HEAD, HEAD), cols]
                                 ).then_inc(done, 16)
                elif piece < 6:
                    c = piece - 4
                    sp.dma_start(ak[c * HEAD:c * HEAD + HEAD, s, cols].bitcast(f32),
                                 qk_d[c, bass.ds(D_A + head * HEAD, HEAD), cols]).then_inc(done, 16)
                else:
                    sp.dma_start(av[:, s, t0:t1, :].bitcast(f32),
                                 v_d[cols, bass.ds(head, 1), :, :].rearrange("(t p) h c d -> p t (h c d)", p=P)
                                 ).then_inc(done, 16)

            def first_head(part):
                for piece in range(7):
                    load_job(0, 0, piece, first_loaded[part], part * PART, (part + 1) * PART)

            for half in range(2):
                base = half * UNITS
                tok = half * HALF
                if half == 0:
                    for c in range(X_CHUNKS):
                        load_x_piece(0, c)

                def next_panel(panel, col, width):
                    sp.wait_ge(w_split, 4 * (half * PANELS + panel))
                    load_panel(col, width)

                def rows(row, j):
                    return qk_d[:, bass.ds(row, P), bass.ds(tok + j * TB, TB)].rearrange("c p t -> p c t")

                with sp.Fori(0, 2) as it:
                    for s in range(2):
                        next_panel(2 * it + s + 1, COL_QK + (2 * it + s + 1) * PW, PW)
                        for r in range(8):
                            store_unit(base + 16 * it + 8 * s + r, r % 2,
                                       rows((2 * it + s) * PW + (r % 2) * P, r // 2))
                with sp.Fori(0, 2) as it:
                    for s in range(2):
                        next_panel(5 + 2 * it + s, COL_G + (2 * it + s + 1) * PW, PW)
                        for r in range(8):
                            store_unit(base + 32 + 16 * it + 8 * s + r, r % 2,
                                       g_d[bass.ds((2 * it + s) * PW + (r % 2) * P, P),
                                           bass.ds(tok + (r // 2) * TB, TB)], 1)

                def load_trig(n):
                    j = n % JB
                    earlier = 0 if n < 2 else 2 * (n - 1) if n <= 9 else n + 7
                    sp.wait_ge(rope_done, half * 20 + earlier + 1)
                    for r0 in (0, HEAD):
                        sp.dma_start(trig[r0:r0 + ROT, j % 2, :, :],
                                     trig_d[:, :, bass.ds(tok + j * TB, TB)].rearrange("c r t -> r c t")
                                     ).then_inc(trig_loaded[j % 2], 16)
                sp.wait_ge(setup_stored, 16 * 17)
                sp.wait_ge(rope_step, 2)
                load_trig(0)
                load_trig(1)
                for w in range(2):
                    if w == 0:
                        next_panel(9, COL_BQ + PW, PW)
                    else:
                        next_panel(10, COL_BK, P)
                    for j in range(JB):
                        for c in range(2):
                            sp.wait_ge(acc_free, base + 64 + 8 * w + 2 * j + c + 9)
                            for hd, stored in ((0, unit_stored), (1, bq_stored)):
                                sp.dma_start(
                                    bq_d[2 * w + c, :, bass.ds(half * JB + j, 1), :, :, hd, :]
                                    .rearrange("d b c n q -> d (b c n) q"),
                                    stage_out[hd * HEAD:hd * HEAD + HEAD, c, :, :]
                                    .rearrange("d c (n q) -> d (c n) q", q=CHUNK)).then_inc(stored[c], 16)
                        load_trig(4 * w + j + 2)
                next_panel(11, COL_BV, P)
                for j in range(JB):
                    store_unit(base + 80 + j, j % 2, rows(ROW_BK, j))
                    if j < 2:
                        load_trig(10 + j)
                    if j == 1:
                        next_panel(12, COL_AV, PW)
                for j in range(JB):
                    store_unit(base + 84 + j, j % 2, rows(ROW_BV, j))
                    if j == 1:
                        next_panel(13, COL_AV + PW, PW)
                for w in range(2):
                    if w == 1:
                        if half == 0:
                            next_panel(14, COL_QK, PW)
                    x_next = w == 1 and half == 0
                    a_next = w == 1 and half == 1
                    if a_next:
                        for i in range(2):
                            sp.wait_ge(unit_stored[i], 16 * ((base + 96) // 2 + 1))
                        sp.wait_ge(bias_stored, 16)
                        load_bias(0, 0, first_loaded[0])
                    if x_next:
                        for c in range(X_RING):
                            load_x_piece(1, c)
                    for r in range(8):
                        store_unit(base + 88 + 8 * w + r, r % 2,
                                   v_d[bass.ds(tok + r * 2 * P, 2 * P), 4 * w:4 * w + 4, :, :]
                                   .rearrange("(t p) h c d -> p t (h c d)", p=P))
                        if x_next:
                            for c in range(X_RING + 2 * (r - 1), X_RING + 2 * r):
                                if X_RING <= c < X_CHUNKS:
                                    load_x_piece(1, c)
                        if a_next and r % 2 == 1:
                            first_head(r // 2)

            sp.wait_ge(acc_free, 8 + 2 * UNITS)
            sp.wait_ge(w_split, 4 * 2 * PANELS)

            def load_bq(group, block, which):
                pair, s, _ = b_unit(2 * B_UNITS * group)
                for c in range(2):
                    sp.dma_start(bq[c * HEAD:c * HEAD + HEAD, which, block * 2 * TB:(block + 1) * 2 * TB].bitcast(f32),
                                 bq_d[pair + which, :, s * JB + block, c, :, :, :].rearrange("d n h q -> d (n h q)")
                                 ).then_inc(bq_loaded[block], 16)

            def kv_rows(row, kv, s, c):
                lo_tok, c0, n = (0, CHUNK, B_HALF) if s == 0 else (B_HALF - CHUNK, 0, B_HALF + CHUNK)
                return slice(c0, c0 + n), qk_d[c, row + kv * HEAD:row + kv * HEAD + HEAD, lo_tok:lo_tok + n]

            def load_bk(kv, s, parts=(0, 1)):
                for dst, c in ((bk_hi, 0), (bk_lo, 1)):
                    if c not in parts:
                        continue
                    cols, src = kv_rows(ROW_BK, kv, s, c)
                    for r0 in (0, HEAD):
                        sp.dma_start(dst[r0:r0 + HEAD, s, cols].bitcast(f32), src).then_inc(bk_loaded[s], 16)

            def load_bv(kv, s):
                for c in range(2):
                    cols, src = kv_rows(ROW_BV, kv, s, c)
                    sp.dma_start(bvt[c * HEAD:c * HEAD + HEAD, s, cols], src).then_inc(bv_loaded[s], 16)

            def load_gate(head, q):
                sp.dma_start(g_a[:, q % QSLOTS, :], g_d[bass.ds(head * HEAD, HEAD), q * TB:q * TB + TB]
                             ).then_inc(gate_loaded[q % QSLOTS], 16)

            def stage_a(it, load_next):
                for s in range(2):
                    quad0 = 16 * it + 8 * s
                    head = 2 * it + s
                    more = load_next or s == 0
                    for q in range(QUADS):
                        sp.wait_ge(y_gated, quad0 + q + 1)
                        sp.dma_start(y_d[bass.ds(head * HEAD, HEAD), q * TB:q * TB + TB], y_a[:, q % QSLOTS, :]
                                     ).then_inc(y_stored[q % QSLOTS], 16)
                        if q + QSLOTS < QUADS:
                            load_gate(head, q + QSLOTS)
                        elif more:
                            load_gate(head + 1, q + QSLOTS - QUADS)
                        if q == 0 and more:
                            load_job(head + 1, 1 - s, 4, job_loaded[1 - s])
                            load_job(head + 1, 1 - s, 5, job_loaded[1 - s])
                        if q == 1 and more:
                            load_job(head + 1, 1 - s, 6, job_loaded[1 - s])
                        if q == QUADS - 2 and load_next:
                            sp.wait_ge(scores_used, A_TURN * it + NT * s + NT + 1)
                            load_job(head + 2, s, 0, job_loaded[s])
                            load_job(head + 2, s, 1, job_loaded[s])
                        if q == QUADS - 1 and load_next:
                            load_job(head + 2, s, 2, job_loaded[s])
                            load_job(head + 2, s, 3, job_loaded[s])
                            load_bias(head + 2, s, job_loaded[s])
                        if not more:
                            if q < JB:
                                load_bq(0, q, 0)
                            if q in (1, 2):
                                load_bk(0, 0, (q - 1,))
                            if q == 3:
                                load_bv(0, 0)
                            if q == QUADS - 2:
                                sp.wait_ge(scores_used, A_HEADS * NT + 1)
                                for block in range(JB):
                                    load_bq(0, block, 1)

            for i in range(2):
                sp.wait_ge(unit_stored[i], 16 * UNITS + 16)
                sp.wait_ge(bq_stored[i], 16 * 17)
            sp.sem_inc(p_over, 1)
            for q in range(QSLOTS):
                load_gate(0, q)
            for part in range(JB, PARTS):
                first_head(part)
            for piece in range(4):
                load_job(1, 1, piece, job_loaded[1])
            load_bias(1, 1, job_loaded[1])
            with sp.Fori(0, 3) as it:
                stage_a(it, True)
            stage_a(3, False)
            for stored in y_stored:
                sp.wait_ge(stored, 16 * (A_HEADS * QUADS // QSLOTS + 1))

            def gated_rows(t, u):
                pair, s, i = b_unit(u)
                t0 = s * B_HALF + i * 4 * CHUNK
                return (t[D_A + pair * P:D_A + pair * P + P, t0:t0 + 4 * CHUNK].rearrange("(h d) t -> d h t", h=2))

            def load_bgate(u):
                sp.wait_ge(by_gated, u + 1)
                sp.dma_start(g_b[:, u % 2, :, :], gated_rows(g_d, u)).then_inc(bgate_loaded[u % 2], 16)

            load_bgate(0)
            load_bk(0, 1)
            load_bv(0, 1)
            strips = ([w_out[k * P:k * P + P, :] for k in range(KT)] + [w_gate[k * P:k * P + P, :] for k in range(KT)]
                      + [w_ple[k * P:k * P + P, :] for k in range(2)])

            def load_strip(n):
                sp.dma_start(strip[:, n % STRIPS, :], strips[n]).then_inc(cw_loaded[n % STRIPS], 16)

            def load_tile(t, s):
                sp.dma_start(y_raw[:, s, :, :], y_d[:, bass.ds(t * P, P)].rearrange("(k p) t -> p k t", p=P)
                             ).then_inc(y_loaded[s], 16)
                sp.dma_start(p_raw[:, s, :, :], pT[:, bass.ds(t * P, P)].rearrange("(k p) t -> p k t", p=P)
                             ).then_inc(p_loaded[s], 16)

            def load_x(t):
                sp.dma_start(x_nat[:, :], x[bass.ds(t * P, P), :]).then_inc(xn_loaded, 16)

            def more_strips(n0, count):
                for n in range(n0, n0 + count):
                    sp.wait_ge(cw_split, n - STRIPS + 1)
                    load_strip(n)

            GROUP = 2 * B_UNITS
            strip_steps = [step for step in range(5 * B_ALL // 8, B_ALL) if step % 4 in (1, 2)][:STRIPS]
            for step in range(B_ALL + B_DRAIN - 1):
                group, since = step // GROUP, step % GROUP
                if step % 4 == 3 and group + 1 < 4:
                    sp.wait_ge(bscores_done, step + 1)
                    load_bq(group + 1, since // 4, 0)
                if step % 4 == 0 and 0 < step < 3 * GROUP + 1:
                    load_bq((step - 1) // GROUP + 1, (step - 1) % GROUP // 4, 1)
                if group in (1, 2) and since in (1, 2):
                    load_bk(1, group - 1, (since - 1,))
                if group in (1, 2) and since == 5:
                    sp.wait_ge(bv_done, B_UNITS * group)
                    load_bv(1, group - 1)
                if step in strip_steps:
                    load_strip(strip_steps.index(step))
                u = step - B_DRAIN + 1
                if u == B_ALL - 3:
                    sp.wait_ge(bvalues_done, B_ALL)
                    for stored in by_stored:
                        sp.wait_ge(stored, 16 * (3 * GROUP // 2 + 1))
                    load_tile(0, 0)
                if u == B_ALL - 2:
                    more_strips(STRIPS + DRAIN_LOADS, 2)
                if u >= 0:
                    if u + 1 < B_ALL:
                        load_bgate(u + 1)
                    sp.wait_ge(by_gated, u + 3)
                    sp.dma_start(gated_rows(y_d, u), y_b[:, u % 2, :, :, :].rearrange("p h c q -> p h (c q)")
                                 ).then_inc(by_stored[u % 2], 16)
                n = step - B_ALL + STRIPS
                if STRIPS <= n < STRIPS + DRAIN_LOADS:
                    more_strips(n, 1)
            def store_out(t, slot, done=None):
                sp.wait_ge(done or shifted, 1 if done else t + 1)
                sp.dma_start(out[bass.ds(t * P, P), :], h[:, slot, :]).then_inc(out_stored[slot], 16)

            load_x(0)
            more_strips(STRIPS + DRAIN_LOADS + 2, 1)
            load_tile(1, 1)
            more_strips(STRIPS + DRAIN_LOADS + 3, len(strips) - STRIPS - DRAIN_LOADS - 3)
            sp.wait_ge(by_stored[0], 16 * 33)
            sp.wait_ge(by_stored[1], 16 * 33)
            sp.sem_inc(b_over, 1)
            sp.wait_ge(cw_split, len(strips))
            for dst, src in ((lng, ln_g), (lnb, ln_b)):
                sp.dma_start(dst[:, :], bass.AP(tensor=src.tensor, offset=0, ap=[[0, P], [1, D_MODEL]])
                             ).then_inc(ln_loaded, 16)

            def stage_c(t, i, more=True):
                if more:
                    sp.wait_ge(p_split, t + 1)
                    load_tile(t + 2, i % 2)
                sp.wait_ge(h_done, t + 1)
                load_x(t + 1)
                store_out(t, i % 3)

            with sp.Fori(0, 5) as it:
                for i in range(6):
                    stage_c(6 * it + i, i)
            stage_c(30, 0, False)
            store_out(31, 1, last_shifted)
            for slot, count in ((0, 11), (1, 11), (2, 10)):
                sp.wait_ge(out_stored[slot], 16 * count + 16)

        @block.gpsimd
        def _(pool):
            pool.memset(ident[:, :], 0.0).then_inc(setup_step, 1)
            pool.wait_ge(setup_step, 1)
            pool.affine_select(out=ident[:, :], in_=ident[:, :], compare_op=ALU.not_equal, fill=1.0, base=0,
                               pattern=[[-1, P]], channel_multiplier=1).then_inc(ident_ready, 1)
            pool.dma_start(rope_c[:, :], rope_const).then_inc(consts_loaded, 16)
            for g in range(SEQ // TB):
                pool.dma_start(work[ROT * g:ROT * g + ROT, 0, :].bitcast(i32),
                               bass.AP(tensor=pos.tensor, offset=TB * g, ap=[[0, ROT], [1, TB]])
                               ).then_inc(consts_loaded, 16)
            pool.dma_start(bias_row[:, 127:384], rel_rev).then_inc(consts_loaded, 16)
            for hd in range(2):
                pool.dma_start(sink_sb[64 * hd:64 * hd + 64, 0, :],
                               bass.AP(tensor=sinks.tensor, offset=4 * hd, ap=[[0, 64], [1, 4]]),
                               ).then_inc(consts_loaded, 16)
            pool.wait_ge(setup, 3)
            for g in range(8):
                for c in range(2):
                    pool.dma_start(trig_d[c, :, TB * g:TB * g + TB], swap[16 * g:16 * g + 16, c, :]
                                   ).then_inc(setup_stored, 16)
            pool.dma_start(bias_d[:, 0:384], bias_row[:, :]).then_inc(setup_stored, 16)
            pool.wait_ge(setup_stored, 16 * 17)
            pool.dma_start(bias_q_d.rearrange("(h q) c -> h q c", q=P),
                           bass.AP(tensor=bias_d.tensor, offset=127, ap=[[384, A_HEADS], [-1, P], [1, 256]])
                           ).then_inc(bias_stored, 16)
            pool.memset(credit[:, 1:2], 0.0).then_inc(by_gated, 2)
            with pool.Fori(0, QUADS * A_HEADS // QSLOTS) as it:
                for s in range(QSLOTS):
                    pool.wait_ge(y_summed, 2 * QSLOTS * it + 2 * s + 4)
                    pool.wait_ge(gate_loaded[s], 16 * it + 16)
                    pool.tensor_tensor(y_a[:, s, :], y_a[:, s, :], g_a[:, s, :], ALU.mult).then_inc(y_gated, 1)
            with pool.Fori(0, 32) as it:
                for s in range(2):
                    pool.wait_ge(by_summed, 2 * it + s + 4)
                    pool.wait_ge(bgate_loaded[s], 16 * it + 16)
                    yb = y_b[:, s, :, :, :].rearrange("p h c q -> p (h c q)")
                    pool.tensor_tensor(yb, yb, g_b[:, s, :, :].rearrange("p h t -> p (h t)"),
                                       ALU.mult).then_inc(by_gated, 1)
            pool.wait_ge(ln_loaded, 32)
            def scale_shift(t, slot):
                pool.wait_ge(normalized, t + 1)
                pool.tensor_tensor(h[:, slot, :], h[:, slot, :], lng[:, :], ALU.mult).then_inc(scaled, 1)
                pool.wait_ge(scaled, t + 1)
                pool.tensor_tensor(h[:, slot, :], h[:, slot, :], lnb[:, :], ALU.add).then_inc(shifted, 1)
            with pool.Fori(0, 10) as it:
                for i in range(3):
                    scale_shift(3 * it + i, i)
            scale_shift(30, 0)

        @block.scalar
        def _(act):
            act.sem_inc(sig_done, 1)

            def split_w(panel, i, slot, width=PW):
                if i == 0:
                    act.wait_ge(w_loaded, 16 * (panel + 1))
                act.activation(w_hi[:, slot, 2 * i:2 * i + 2, 0:width], w_raw[:, 2 * i:2 * i + 2, 0:width],
                               ACT.Copy).then_inc(w_hi_done, 1)

            def split_x(half, c):
                slot = c % X_RING
                in_half = len(range(slot, X_CHUNKS, X_RING))
                act.wait_ge(x_loaded[slot], 16 * (half * in_half + c // X_RING + 1))
                act.activation(x_hi[:, 2 * (c % 4):2 * (c % 4) + 2, (c // 4) * TB:(c // 4) * TB + TB],
                               x_raw[:, slot, :, :], ACT.Copy).then_inc(x_hi_done, 1)

            for i in range(4):
                split_w(0, i, 0)
            for half in range(2):
                base = half * UNITS
                pbase = half * PANELS
                if half == 0:
                    for c in range(X_CHUNKS):
                        split_x(0, c)
                    act.wait_ge(setup, 1)
                    act.activation(swap[:, 1, :], work[:, 1, :], ACT.Sin)
                    act.activation(swap[:, 0, :], work[:, 1, :], ACT.Sin, scale=0.5).then_inc(setup, 1)

                def before(unit, slot):
                    act.wait_ge(acc_done, unit + 1)
                    act.wait_ge(unit_stored[slot], 8 * unit - 8 * slot + 16)

                def split_unit(unit, r):
                    before(unit, r % 2)
                    act.activation(stage_out[:, r % 2, 0, :].bitcast(f32r), psum[:, r % 8, :],
                                   ACT.Copy).then_inc(unit_act, 1)

                def panel(w, slot, units, next_width, unit_fn, last=False):
                    for r in range(units):
                        unit_fn(r)
                        for i in split_after(r, units):
                            if not last or half == 0:
                                split_w(pbase + w + 1, i, 1 - slot, next_width)
                        if last and half == 0:
                            for c in x_after(r):
                                split_x(1, c)

                with act.Fori(0, 2) as it:
                    for s in range(2):
                        def fn(r):
                            split_unit(base + 16 * it + 8 * s + r, r)
                        panel(2 * it + s, s, 8, PW, fn)
                with act.Fori(0, 2) as it:
                    for s in range(2):
                        def fn(r):
                            unit = base + 32 + 16 * it + 8 * s + r
                            act.wait_ge(acc_done, unit + 1)
                            act.wait_ge(acc_free, unit + 7)
                            act.activation(work[:, r % 2, :], psum[:, r % 8, :], ACT.Sigmoid).then_inc(unit_act, 1)
                        panel(4 + 2 * it + s, s, 8, PW, fn)

                def rope_unit(unit, n, bank, slot):
                    rope = half * 20 + n
                    act.wait_ge(acc_done, unit + 1)
                    act.wait_ge(acc_free, unit + 7)
                    act.activation(work[:, slot, :], psum[:, bank, :], ACT.Copy).then_inc(rope_row, 1)
                    act.wait_ge(rope_done, rope + 2)
                    act.wait_ge(unit_stored[slot], 8 * unit - 8 * slot + 16)
                    act.wait_ge(bq_stored[slot], half * 128 + 8 * (min(n, 16 + slot) - slot) + 16)
                    act.activation(stage_out[:, slot, 0, :].bitcast(f32r), work[:, slot, :],
                                   ACT.Copy).then_inc(unit_act, 1)

                for w in range(2):
                    panel(8 + w, w, 8, PW if w == 0 else P,
                          lambda r: rope_unit(base + 64 + 8 * w + r, 8 * w + r, r % 8, r % 2))
                panel(10, 0, 4, P, lambda r: rope_unit(base + 80 + r, 16 + r, r, r % 2))

                def bv(r):
                    before(base + 84 + r, r % 2)
                    act.activation(stage_out[:, r % 2, 0, :].bitcast(f32r), psum[:, 4 + r, :],
                                   ACT.Copy).then_inc(unit_act, 1)
                panel(11, 1, 4, PW, bv)
                for w in range(2):
                    def av_unit(r):
                        before(base + 88 + 8 * w + r, r % 2)
                        dst = stage_out[:, r % 2, :, :].bitcast(f32r).rearrange("p t (h c d) -> p (t h) c d", c=2, d=HEAD)
                        act.activation(dst[:, :, 0, :], psum[:, r % 8, :].rearrange("p (h d) -> p h d", d=HEAD),
                                       ACT.Copy).then_inc(unit_act, 1)
                    panel(12 + w, w, 8, PW, av_unit, w == 1)

            def a_step(it, i):
                unit = a_unit(it, i, 1)
                if unit:
                    u, s, t = unit
                    n, r = min(BAND, t + 1), t % RING
                    act.wait_ge(shift_ready, u + 1)
                    act.activation(prob[:, r, NBW - n * P:NBW], prob[:, r, NBW - n * P:NBW], ACT.Exp,
                                   bias=a_col(A_SHIFT, r), scale=SCALE, accum_out=a_col(A_SUM, r)).then_inc(exp_done, 1)
                unit = a_unit(it, i, 8)
                if unit and unit[2] % 2 == 1:
                    u, s, t = unit
                    pr = t // 2
                    act.wait_ge(values_done, (A_TURN // 2) * it + (i - 8) // 2 + 1)
                    act.wait_ge(y_summed, (A_TURN // 2) * it + (i - 8) // 2 + 1)
                    act.activation(y_low[:, pr % 2, :], psum[HEAD:P, 6 + pr % 2, 0:2 * P],
                                   ACT.Copy).then_inc(y_low_ready, 1)
                unit = a_unit(it, i, 5)
                if unit:
                    u, s, t = unit
                    n, e = min(BAND, t + 1), t % 2
                    act.wait_ge(probsT_done, u + 1)
                    src = psum[:, 2 + 2 * e:4 + 2 * e, :].rearrange("p a b -> p (a b)")[:, 0:n * P]
                    act.activation(pt_hi[:, (t // 2) % 2, e + BAND - n:e + BAND, e * P:e * P + P],
                                   src.rearrange("p (j q) -> p j q", q=P), ACT.Copy).then_inc(probsT_hi, 1)

                unit = a_unit(it, i, 3)
                if unit and unit[2] % 8 not in VECTOR_NORMS:
                    u, s, t = unit
                    n, r = min(BAND, t + 1), t % RING
                    act.wait_ge(recip_ready, u + 1)
                    act.activation(prob[:, r, NBW - n * P:NBW], prob[:, r, NBW - n * P:NBW], ACT.Copy,
                                   scale=a_col(A_RECIP, r)).then_inc(normed[0], 1)

            for i in range(A_TURN):
                a_step(0, i)
            with act.Fori(1, A_HEADS // 2) as it:
                for i in range(A_TURN):
                    a_step(it, i)
            for i in range(A_TURN, A_TURN + A_DRAIN):
                a_step(A_HEADS // 2 - 1, i)

            def b_step(step):
                u = step - 1
                if 0 <= u < B_ALL:
                    act.wait_ge(bshift_ready, u + 1)
                    pair, s, i = b_unit(u)
                    q = u % 4
                    for c in range(4):
                        lo = CHUNK if s == 0 and i == 0 and c == 0 else 0
                        act.activation(prob_b[:, q, c, lo:P], psum[:, u % 2, c * P + lo:c * P + P], ACT.Exp,
                                       bias=small[:, 16 + 4 * q + c:17 + 4 * q + c], scale=SCALE,
                                       accum_out=small[:, 32 + 4 * q + c:33 + 4 * q + c])
                    act.activation(small[:, 48 + 4 * q:52 + 4 * q], small[:, 16 + 4 * q:20 + 4 * q], ACT.Exp,
                                   bias=sink_sb[:, 0, pair:pair + 1], scale=1.0).then_inc(bexp_done, 1)
                u = step - 4
                if 0 <= u < B_ALL:
                    act.wait_ge(bprobsT_done, u + 1)
                    act.activation(ptb_hi[:, u % 4, :, :].rearrange("p c q -> p (c q)"), psum[:, 2 + u % 2, :],
                                   ACT.Copy).then_inc(bprobsT_hi, 1)

                u = step - 4
                if 0 <= u < B_ALL and u % 2 == 0:
                    act.wait_ge(bv_done, u // 2 + 1)
                    act.activation(v_b[:, u // 2 % 4, :, :].rearrange("p c d -> p (c d)"), psum[:, 7, :],
                                   ACT.Copy).then_inc(bv_ready, 1)
                u = step - 7
                if 0 <= u < B_ALL:
                    act.wait_ge(bvalues_done, u + 1)
                    act.wait_ge(by_summed, u + 2)
                    act.activation(yb_low[:, u % 2, :], psum[HEAD:P, 4 + u % 3, :], ACT.Copy).then_inc(by_low_ready, 1)

            strips = ([(wo_hi, k) for k in range(KT)] + [(wg_hi, k) for k in range(KT)] + [(wp_hi, k) for k in range(2)])

            def strip_hi(n):
                dst, k = strips[n]
                act.wait_ge(cw_loaded[n % STRIPS], 16 * (n // STRIPS + 1))
                if n == KT:
                    act.wait_ge(bv_done, B_ALL // 2)
                act.activation(dst[:, k, :], strip[:, n % STRIPS, :], ACT.Copy).then_inc(cw_hi_done, 1)

            for step in range(B_ALL + B_DRAIN):
                b_step(step)
                if B_ALL <= step < B_ALL + DRAIN_STRIPS:
                    strip_hi(step - B_ALL)

            def y_tile_hi(t, s, first=False):
                act.wait_ge(y_loaded[s], 8 * (t - s) + 16)
                if not first:
                    act.wait_ge(mix_done, t)
                act.activation(y_hi[:, :, :], y_raw[:, s, :, :], ACT.Copy).then_inc(y_hi_done, 1)

            def p_tile_hi(t, s, first=False):
                act.wait_ge(p_loaded[s], 8 * (t - s) + 16)
                if not first:
                    act.wait_ge(ple_done, t - 1)
                act.activation(p_hi[:, s, :, :], p_raw[:, s, :, :], ACT.Copy).then_inc(p_hi_done, 1)

            def hT_tile_hi(t):
                act.wait_ge(hT_done, t + 1)
                act.activation(hT_hi[:, :, :].rearrange("p k t -> p (k t)"),
                               psum[:, 2:4, :].rearrange("p a b -> p (a b)"), ACT.Copy).then_inc(hT_hi_done, 1)

            def sigmoid(t):
                act.wait_ge(gate_done, t + 1)
                act.wait_ge(h2_done, t + 1)
                act.activation(sg[:, :], psum[:, 4:6, :].rearrange("p a b -> p (a b)"), ACT.Sigmoid).then_inc(sig_done, 1)

            def root(t):
                act.wait_ge(inverse_done, t + 1)
                act.activation(small[:, 15:16], small[:, 14:15], ACT.Sqrt).then_inc(root_done, 1)

            y_tile_hi(0, 0, True)
            for n in range(DRAIN_STRIPS, 14):
                strip_hi(n)
            y_tile_hi(1, 1)
            for n in range(14, len(strips)):
                strip_hi(n)
            act.wait_ge(b_over, 1)
            p_tile_hi(0, 0, True)
            p_tile_hi(1, 1, True)
            hT_tile_hi(0)
            with act.Fori(0, 15) as it:
                for s in range(2):
                    t = 2 * it + s
                    y_tile_hi(t + 2, s)
                    p_tile_hi(t + 2, s)
                    sigmoid(t)
                    hT_tile_hi(t + 1)
                    root(t)
            sigmoid(30)
            hT_tile_hi(31)
            root(30)
            sigmoid(31)
            root(31)

        @block.vector
        def _(dve):
            dve.memset(credit[:, 2:3], 0.0).then_inc(acc_free, 8)
            dve.memset(credit[:, 3:4], 0.0).then_inc(x_split, 2)
            dve.memset(credit[:, 4:5], 0.0).then_inc(probsT_split, 2)
            dve.memset(credit[:, 5:6], 0.0).then_inc(y_summed, 2)
            dve.memset(credit[:, 6:7], 0.0).then_inc(by_summed, 3)
            for sm in (rope_done, scores_used, h2_done, ple_gated):
                dve.sem_inc(sm, 1)
            dve.memset(trig[:, :, 0, :], 1.0).then_inc(rope_step, 1)
            dve.memset(trig[:, :, 1, :], 0.0).then_inc(rope_step, 1)
            SET0 = 2

            def split_w(panel, i, slot, width=PW):
                dve.wait_ge(w_hi_done, 4 * panel + i + 1)
                dve.tensor_tensor(w_lo[:, slot, 2 * i:2 * i + 2, 0:width], w_raw[:, 2 * i:2 * i + 2, 0:width],
                                  w_hi[:, slot, 2 * i:2 * i + 2, 0:width].bitcast(f32), ALU.subtract).then_inc(w_split, 1)


            step = [0]

            def chain(ins):
                step[0] += 1
                ins.then_inc(ln_step, 1)
                dve.wait_ge(ln_step, step[0])

            def tables():

                dve.wait_ge(consts_loaded, 16 * 12)
                chain(dve.tensor_copy(bias_row[:, 0:127], bias_row[:, 127:128].to_broadcast([A_HEADS, 127])))
                chain(dve.tensor_copy(small[0:A_HEADS, 0:1], bias_row[:, 127:128]))
                chain(dve.tensor_scalar(bias_row[:, :], bias_row[:, :], small[0:A_HEADS, 0:1], 1.0 / SCALE,
                                        ALU.subtract, ALU.mult))
                chain(dve.tensor_scalar(sink_sb[:, 1, :], sink_sb[:, 0, :], -1.0, None, ALU.mult))
                C1, C2 = 6.28125, 0.0019350051879882812
                C3 = 2 * np.pi - C1 - C2
                ang, kk, prod = work[:, 1, :], swap[:, 0, :], swap[:, 1, :]
                chain(dve.tensor_copy(kk, work[:, 0, :].bitcast(i32)))
                chain(dve.tensor_scalar(ang, kk, rope_c[:, 0:1], None, ALU.mult))
                ROUND = 12582912.0
                chain(dve.tensor_scalar(kk, ang, 1.0 / (2 * np.pi), None, ALU.mult))
                chain(dve.tensor_scalar(kk, kk, ROUND, None, ALU.add))
                chain(dve.tensor_scalar(kk, kk, ROUND, None, ALU.subtract))
                for c in (C1, C2, float(C3)):
                    chain(dve.tensor_scalar(prod, kk, c, None, ALU.mult))
                    chain(dve.tensor_tensor(ang, ang, prod, ALU.subtract))
                PI = 3.1415925
                dve.tensor_scalar(ang, ang, PI, -PI, ALU.min, ALU.max).then_inc(setup, 1)
                dve.wait_ge(setup, 2)
                chain(dve.tensor_tensor(swap[:, 0, :], swap[:, 0, :], swap[:, 0, :], ALU.mult))
                chain(dve.tensor_scalar(swap[:, 0, :], swap[:, 0, :], -2.0, 1.0, ALU.mult, ALU.add))
                dve.tensor_scalar(swap[:, 1, :], swap[:, 1, :], rope_c[:, 1:2], None, ALU.mult).then_inc(setup, 1)

            for i in range(4):
                split_w(0, i, 0)

            def split_x(half, c):
                dve.wait_ge(x_hi_done, half * 16 + c + 1)
                at = (slice(None), slice(2 * (c % 4), 2 * (c % 4) + 2), slice((c // 4) * TB, (c // 4) * TB + TB))
                dve.tensor_tensor(x_lo[at], x_raw[:, c % X_RING, :, :], x_hi[at].bitcast(f32), ALU.subtract
                                  ).then_inc(x_split, 1)


            for half in range(2):
                base = half * UNITS
                pbase = half * PANELS
                if half == 0:
                    for c in range(X_CHUNKS):
                        split_x(0, c)
                    tables()

                def split_unit(unit, bank, slot):
                    dve.wait_ge(unit_act, unit + 1)
                    dve.tensor_tensor(stage_out[:, slot, 1, :].bitcast(f32r), psum[:, bank, :],
                                      stage_out[:, slot, 0, :], ALU.subtract).then_inc(acc_free, 1)

                def panel(w, slot, units, next_width, unit_fn, last=False):
                    for r in range(units):
                        unit_fn(r)
                        for i in split_after(r, units):
                            if not last or half == 0:
                                split_w(pbase + w + 1, i, 1 - slot, next_width)
                        if last and half == 0:
                            for c in x_after(r):
                                split_x(1, c)

                with dve.Fori(0, 2) as it:
                    for s in range(2):
                        def fn(r):
                            split_unit(base + 16 * it + 8 * s + r, r, r % 2)
                        panel(2 * it + s, s, 8, PW, fn)
                dve.wait_ge(setup_stored, 16 * 17)
                with dve.Fori(0, 2) as it:
                    for s in range(2):
                        def fn(r):
                            unit = base + 32 + 16 * it + 8 * s + r
                            dve.wait_ge(unit_act, unit + 1)
                            dve.wait_ge(unit_stored[r % 2], 8 * unit - 8 * (r % 2) + 16)
                            dve.tensor_tensor(stage_out[:, r % 2, 0, :], psum[:, r % 8, :], work[:, r % 2, :],
                                              ALU.mult).then_inc(acc_free, 1)
                        panel(4 + 2 * it + s, s, 8, PW, fn)

                def rope_unit(unit, rope, j, tl, slot):
                    row = work[:, slot, :]
                    dve.wait_ge(rope_row, rope + 1)
                    dve.wait_ge(trig_loaded[j % 2], 32 * (half * 6 + tl // 2 + 1))
                    dve.tensor_tensor(swap[:, 1, :], row, trig[:, j % 2, 0, :], ALU.mult).then_inc(rope_step, 1)
                    dve.stream_shuffle(swap[:, 0, :], row, [(i + 8) % 16 if i < 16 else i for i in range(32)]
                                       ).then_inc(rope_step, 1)
                    dve.wait_ge(rope_step, SET0 + 3 * rope + 2)
                    dve.tensor_tensor(swap[:, 0, :], swap[:, 0, :], trig[:, j % 2, 1, :], ALU.mult).then_inc(rope_step, 1)
                    dve.wait_ge(rope_step, SET0 + 3 * rope + 3)
                    dve.tensor_tensor(row, swap[:, 0, :], swap[:, 1, :], ALU.add).then_inc(rope_done, 1)
                    dve.wait_ge(unit_act, unit + 1)
                    dve.tensor_tensor(stage_out[:, slot, 1, :].bitcast(f32r), row, stage_out[:, slot, 0, :],
                                      ALU.subtract).then_inc(acc_free, 1)

                for w in range(2):
                    panel(8 + w, w, 8, PW if w == 0 else P,
                          lambda r: rope_unit(base + 64 + 8 * w + r, half * 20 + 8 * w + r, r // 2, 4 * w + r // 2, r % 2))
                panel(10, 0, 4, P, lambda r: rope_unit(base + 80 + r, half * 20 + 16 + r, r, 8 + r, r % 2))
                panel(11, 1, 4, PW, lambda r: split_unit(base + 84 + r, 4 + r, r % 2))
                for w in range(2):
                    if w == 1 and half == 1:
                        for s in range(2):
                            dve.memset(bias[:, s, 0:NBW - 256], 0.0).then_inc(ln_step, 1)
                            dve.memset(bias[0:64, s, NBW - 64:NBW], MASKED).then_inc(ln_step, 1)
                        dve.wait_ge(ln_step, step[0] + 4)
                        for s in range(2):
                            dve.memset(bias[64:128, s, 0:64], MASKED).then_inc(ln_step, 1)
                        dve.wait_ge(ln_step, step[0] + 6)
                    def av_unit(r):
                        dve.wait_ge(unit_act, base + 88 + 8 * w + r + 1)
                        dst = stage_out[:, r % 2, :, :].rearrange("p t (h c d) -> p (t h) c d", c=2, d=HEAD)
                        dve.tensor_tensor(dst[:, :, 1, :].bitcast(f32r),
                                          psum[:, r % 8, :].rearrange("p (h d) -> p h d", d=HEAD),
                                          dst[:, :, 0, :], ALU.subtract).then_inc(acc_free, 1)
                    panel(12 + w, w, 8, PW, av_unit, w == 1)

            CHAINED = step[0]

            def a_step(it, i):
                unit = a_unit(it, i, 6)
                if unit:
                    u, s, t = unit
                    n, e = min(BAND, t + 1), t % 2
                    dve.wait_ge(probsT_hi, u + 1)
                    at = (slice(None), (t // 2) % 2, slice(e + BAND - n, e + BAND), slice(e * P, e * P + P))
                    src = psum[:, 2 + 2 * e:4 + 2 * e, :].rearrange("p a b -> p (a b)")[:, 0:n * P]
                    dve.tensor_tensor(pt_lo[at], src.rearrange("p (j q) -> p j q", q=P), pt_hi[at].bitcast(f32),
                                      ALU.subtract).then_inc(probsT_split, 1)
                unit = a_unit(it, i, 0)
                if unit:
                    u, s, t = unit
                    n, r = min(BAND, t + 1), t % RING
                    if t == 0:
                        wait_head(dve, it, s, t)
                    dve.wait_ge(scores_done, u + 1)
                    dve.memset(credit[:, 7:8], 0.0)
                    dve.tensor_tensor_reduce(
                        out=prob[:, r, NBW - n * P:NBW].rearrange("p (a b) -> p a b", a=2),
                        in0=psum[:, 0:2, 0:n * P // 2],
                        in1=bias[:, s, NBW - n * P:NBW].rearrange("p (a b) -> p a b", a=2),
                        scale=1.0, scalar=-3e38, op0=ALU.add, op1=ALU.max,
                        accum_out=a_col(A_MAX, r)).then_inc(scores_used, 1)
                unit = a_unit(it, i, 2)
                if unit:
                    u, s, t = unit
                    dve.wait_ge(exp_done, u + 1)
                    dve.reciprocal(a_col(A_RECIP, t % RING), a_col(A_SUM, t % RING)).then_inc(recip_ready, 1)
                unit = a_unit(it, i, 0)
                if unit:
                    u, s, t = unit
                    dve.wait_ge(scores_used, u + 2)
                    dve.tensor_scalar(a_col(A_SHIFT, t % RING), a_col(A_MAX, t % RING), -SCALE, None,
                                      ALU.mult).then_inc(shift_ready, 1)
                unit = a_unit(it, i, 3)
                if unit and unit[2] % 8 in VECTOR_NORMS:
                    u, s, t = unit
                    n, r = min(BAND, t + 1), t % RING
                    dve.wait_ge(recip_ready, u + 1)
                    dve.tensor_scalar(prob[:, r, NBW - n * P:NBW], prob[:, r, NBW - n * P:NBW],
                                      a_col(A_RECIP, r), None, ALU.mult).then_inc(normed[1], 1)
                unit = a_unit(it, i, A_DRAIN - 1)
                if unit and unit[2] % 2 == 1:
                    u, s, t = unit
                    pr = t // 2
                    dve.wait_ge(y_low_ready, (A_TURN // 2) * it + (i - A_DRAIN + 1) // 2 + 1)
                    if isinstance(it, int) and it == 0 and t == 1:
                        dve.wait_ge(p_over, 1)
                    if pr % 2 == 0:
                        quad = (i - A_DRAIN + 1) // 4
                        dve.wait_ge(y_stored[(pr // 2) % QSLOTS],
                                    16 * (A_TURN // 4 // QSLOTS * it + quad // QSLOTS + 1))
                    dve.tensor_tensor(y_a[:, (pr // 2) % QSLOTS, (pr % 2) * 2 * P:(pr % 2 + 1) * 2 * P],
                                      psum[0:HEAD, 6 + pr % 2, 0:2 * P], y_low[:, pr % 2, :], ALU.add).then_inc(y_summed, 1)

            for i in range(A_TURN):
                a_step(0, i)
            with dve.Fori(1, A_HEADS // 2) as it:
                for i in range(A_TURN):
                    a_step(it, i)
            for i in range(A_TURN, A_TURN + A_DRAIN):
                a_step(A_HEADS // 2 - 1, i)

            dve.memset(bk_hi[:, 0, 0:CHUNK].bitcast(f32), 0.0).then_inc(bden_step, 1)
            dve.memset(bk_lo[:, 0, 0:CHUNK].bitcast(f32), 0.0).then_inc(bden_step, 1)
            dve.memset(bvt[:, 0, 0:CHUNK], 0.0).then_inc(bden_step, 1)

            BDEN0 = 3

            def b_step(step):
                u = step - 5
                if 0 <= u < B_ALL:
                    dve.wait_ge(bprobsT_hi, u + 1)
                    dve.tensor_tensor(ptb_lo[:, u % 4, :, :].rearrange("p c q -> p (c q)"), psum[:, 2 + u % 2, :],
                                      ptb_hi[:, u % 4, :, :].rearrange("p c q -> p (c q)").bitcast(f32),
                                      ALU.subtract).then_inc(bprobsT_split, 1)
                u = step
                if u < B_ALL:
                    pair, s, i = b_unit(u)
                    dve.wait_ge(bscores_done, u + 1)
                    sc = psum[:, u % 2, :].rearrange("p (c k) -> p c k", k=P)
                    mx = small[:, 4 * (u % 4):4 * (u % 4) + 4]
                    if s == 0 and i == 0:
                        if u >= 4:
                            dve.wait_ge(bprobsT_done, u - 3)
                        dve.memset(prob_b[:, u % 4, 0, 0:CHUNK], 0.0)
                        dve.tensor_reduce(out=mx[:, 0:1], in_=sc[:, 0, CHUNK:P], op=ALU.max, axis=AX.X)
                        dve.tensor_reduce(out=mx[:, 1:4], in_=sc[:, 1:4, :], op=ALU.max, axis=AX.X).then_inc(bmax_done, 1)
                    else:
                        dve.tensor_reduce(out=mx, in_=sc, op=ALU.max, axis=AX.X).then_inc(bmax_done, 1)
                u = step - 2
                den = small[:, 32 + 4 * (u % 4):36 + 4 * (u % 4)]
                if 0 <= u < B_ALL:
                    dve.wait_ge(bexp_done, u + 1)
                    dve.tensor_tensor(den, den, small[:, 48 + 4 * (u % 4):52 + 4 * (u % 4)], ALU.add).then_inc(bden_step, 1)
                u = step
                if u < B_ALL:
                    dve.wait_ge(bmax_done, u + 1)
                    dve.tensor_scalar(small[:, 16 + 4 * (u % 4):20 + 4 * (u % 4)], small[:, 4 * (u % 4):4 * (u % 4) + 4],
                                      -SCALE, sink_sb[:, 1, pair:pair + 1], ALU.mult, ALU.min).then_inc(bshift_ready, 1)
                u = step - 2
                if 0 <= u < B_ALL:
                    dve.wait_ge(bden_step, BDEN0 + 2 * u + 1)
                    dve.reciprocal(den, den).then_inc(bden_step, 1)
                u = step - 8
                if 0 <= u < B_ALL:
                    dve.wait_ge(by_low_ready, u + 1)
                    dve.wait_ge(by_stored[u % 2], 16 * (u // 2 + 1))
                    dve.tensor_tensor(y_b[:, u % 2, :, :, :].rearrange("p h c q -> p c h q"),
                                      psum[0:HEAD, 4 + u % 3, :].rearrange("p (c h q) -> p c h q", c=4, h=2),
                                      yb_low[:, u % 2, :].rearrange("p (c h q) -> p c h q", c=4, h=2),
                                      ALU.add).then_inc(by_summed, 1)
                u = step - 2
                if 0 <= u < B_ALL:
                    dve.wait_ge(bden_step, BDEN0 + 2 * u + 2)
                    dve.tensor_tensor(prob_b[:, u % 4, :, :], prob_b[:, u % 4, :, :],
                                      den.unsqueeze(2).to_broadcast([P, 4, P]), ALU.mult).then_inc(bnormed, 1)

            strips = ([(wo_hi, wo_lo, k) for k in range(KT)] + [(wg_hi, wg_lo, k) for k in range(KT)]
                      + [(wp_hi, wp_lo, k) for k in range(2)])

            def strip_lo(n):
                hi, lo, k = strips[n]
                dve.wait_ge(cw_hi_done, n + 1)
                dve.tensor_tensor(lo[:, k, :], strip[:, n % STRIPS, :], hi[:, k, :].bitcast(f32),
                                  ALU.subtract).then_inc(cw_split, 1)

            for step in range(B_ALL + B_DRAIN):
                b_step(step)
                if B_ALL <= step < B_ALL + DRAIN_STRIPS:
                    strip_lo(step - B_ALL)

            LN0 = CHAINED + 6
            LN_STEPS = 8

            def y_tile_lo(t, s):
                dve.wait_ge(y_hi_done, t + 1)
                dve.tensor_tensor(y_lo[:, :, :], y_raw[:, s, :, :], y_hi[:, :, :].bitcast(f32), ALU.subtract
                                  ).then_inc(y_split, 1)

            def p_tile_lo(t, s):
                dve.wait_ge(p_hi_done, t + 1)
                dve.tensor_tensor(p_lo[:, s, :, :], p_raw[:, s, :, :], p_hi[:, s, :, :].bitcast(f32),
                                  ALU.subtract).then_inc(p_split, 1)

            def residual(t, slot, stored):
                dve.wait_ge(xn_loaded, 16 * t + 16)
                dve.wait_ge(mix_done, t + 1)
                if stored is not None:
                    dve.wait_ge(out_stored[slot], stored + 16)
                dve.scalar_tensor_tensor(h[:, slot, :], x_nat[:, :], ALPHA32,
                                         psum[:, 0:2, :].rearrange("p a b -> p (a b)"), ALU.mult, ALU.add
                                         ).then_inc(h_done, 1)

            def hT_tile_lo(t):
                dve.wait_ge(hT_hi_done, t + 1)
                dve.tensor_tensor(hT_lo[:, :, :].rearrange("p k t -> p (k t)"),
                                  psum[:, 2:4, :].rearrange("p a b -> p (a b)"),
                                  hT_hi[:, :, :].rearrange("p k t -> p (k t)").bitcast(f32),
                                  ALU.subtract).then_inc(hT_split, 1)

            def layer_norm(t, slot):
                hs = h[:, slot, :]
                dve.wait_ge(ple_done, t + 1)
                dve.wait_ge(sig_done, t + 2)
                dve.tensor_tensor(sg[:, :], sg[:, :], psum[:, 6:8, :].rearrange("p a b -> p (a b)"),
                                  ALU.mult).then_inc(ple_gated, 1)
                dve.wait_ge(ple_gated, t + 2)
                dve.tensor_tensor(hs, hs, sg[:, :], ALU.add).then_inc(h2_done, 1)
                dve.wait_ge(h2_done, t + 2)
                dve.bn_stats(small[:, 0:6], hs[:, 0:512]).then_inc(ln_step, 1)
                dve.bn_stats(small[:, 6:12], hs[:, 512:1024]).then_inc(ln_step, 1)
                dve.wait_ge(ln_step, LN0 + LN_STEPS * t + 2)
                dve.memset(credit[:, 7:8], 0.0)
                dve.bn_aggr(small[:, 12:14], small[:, 0:12]).then_inc(ln_step, 1)
                dve.wait_ge(ln_step, LN0 + LN_STEPS * t + 3)
                var, inv, root, tmp = (small[:, c:c + 1] for c in (13, 14, 15, 16))
                dve.tensor_scalar(var, var, LN_EPS, None, ALU.add).then_inc(ln_step, 1)
                dve.wait_ge(ln_step, LN0 + LN_STEPS * t + 4)
                dve.reciprocal(inv, var).then_inc(inverse_done, 1)
                dve.wait_ge(root_done, t + 1)
                dve.tensor_tensor(tmp, root, root, ALU.mult).then_inc(ln_step, 1)
                dve.wait_ge(ln_step, LN0 + LN_STEPS * t + 5)
                dve.tensor_tensor(tmp, tmp, var, ALU.mult).then_inc(ln_step, 1)
                dve.wait_ge(ln_step, LN0 + LN_STEPS * t + 6)
                dve.tensor_scalar(tmp, tmp, -0.5, 1.5, ALU.mult, ALU.add).then_inc(ln_step, 1)
                dve.wait_ge(ln_step, LN0 + LN_STEPS * t + 7)
                dve.tensor_tensor(tmp, tmp, root, ALU.mult).then_inc(ln_step, 1)
                dve.wait_ge(ln_step, LN0 + LN_STEPS * t + 8)
                dve.tensor_scalar(hs, hs, small[:, 12:13], tmp, ALU.subtract, ALU.mult).then_inc(normalized, 1)

            dve.wait_ge(by_summed, B_ALL + 3)
            y_tile_lo(0, 0)
            for n in range(DRAIN_STRIPS, 14):
                strip_lo(n)
            dve.wait_ge(cw_split, 14)
            residual(0, 0, None)
            y_tile_lo(1, 1)
            for n in range(14, len(strips)):
                strip_lo(n)
            p_tile_lo(0, 0)
            p_tile_lo(1, 1)
            dve.wait_ge(cw_split, len(strips))
            hT_tile_lo(0)
            def c_step(t, i, s, stored):
                y_tile_lo(t + 2, s)
                p_tile_lo(t + 2, s)
                residual(t + 1, (i + 1) % 3, stored)
                hT_tile_lo(t + 1)
                layer_norm(t, i % 3)
            with dve.Fori(0, 5) as it:
                for i in range(6):
                    c_step(6 * it + i, i, i % 2, 16 * (2 * it + (i + 1) // 3))
            residual(31, 1, 16 * 10)
            hT_tile_lo(31)
            layer_norm(30, 0)
            layer_norm(31, 1)
            dve.wait_ge(ln_loaded, 32)
            dve.wait_ge(normalized, NT)
            dve.tensor_tensor(h[:, 1, :], h[:, 1, :], lng[:, :], ALU.mult).then_inc(last_scaled, 1)
            dve.wait_ge(last_scaled, 1)
            dve.tensor_tensor(h[:, 1, :], h[:, 1, :], lnb[:, :], ALU.add).then_inc(last_shifted, 1)

        @block.tensor
        def _(pe):
            def mm(dst, lhs, rhs, start, stop):
                return pe.matmul(dst, lhs, rhs, start=start, stop=stop)

            for half in range(2):
                base = half * UNITS
                pbase = half * PANELS

                def unit(number, bank, slot, c, j):
                    pe.wait_ge(acc_free, number + 1)
                    for k in range(KT):
                        wh, wl = (w[:, slot, k, c * P:c * P + P] for w in (w_hi, w_lo))
                        xh, xl = (t[:, k, j * TB:j * TB + TB] for t in (x_hi, x_lo))
                        mm(psum[:, bank, :], wh, xh, k == 0, False)
                        mm(psum[:, bank, :], wh, xl, False, False)
                        last = mm(psum[:, bank, :], wl, xh, False, k == KT - 1)
                    last.then_inc(acc_done, 1)

                with pe.Fori(0, 5) as it:
                    for s in range(2):
                        pe.wait_ge(w_split, 4 * (pbase + 2 * it + s + 1))
                        for r in range(8):
                            if s == 0 and r % 2 == 0:
                                pe.wait_ge(x_split, 16 * half + 4 * (r // 2 + 1) + 2)
                            unit(base + 16 * it + 8 * s + r, r, s, r % 2, r // 2)
                for w in range(2):
                    pe.wait_ge(w_split, 4 * (pbase + 11 + w))
                    for r in range(4):
                        unit(base + 80 + 4 * w + r, 4 * w + r, w, 0, r)
                for w in range(2):
                    pe.wait_ge(w_split, 4 * (pbase + 13 + w))
                    for r in range(8):
                        pe.wait_ge(acc_free, base + 88 + 8 * w + r + 1)
                        for tt in range(2):
                            tok = (2 * r + tt) * P
                            dst = psum[:, r, tt * PW:tt * PW + PW]
                            for k in range(KT):
                                xh, xl = (t[:, k, tok:tok + P] for t in (x_hi, x_lo))
                                wh, wl = (t[:, w, k, :] for t in (w_hi, w_lo))
                                mm(dst, xh, wh, k == 0, False)
                                mm(dst, xh, wl, False, False)
                                last = mm(dst, xl, wh, False, k == KT - 1)
                        last.then_inc(acc_done, 1)

            pe.wait_ge(ident_ready, 1)

            def a_scores(u, s, t):
                n = min(BAND, t + 1)
                w = n * P // 2
                k0 = (t + 1 - n) * P
                pe.wait_ge(scores_used, u + 1)
                for q in (aq_hi, aq_lo):
                    for a in range(2):
                        last = mm(psum[:, a, 0:w], q[:, s, t * P:t * P + P], ak[:, s, k0 + a * w:k0 + a * w + w],
                                  q is aq_hi, q is aq_lo)
                last.then_inc(scores_done, 1)

            def a_transpose(u, t, done, count):
                n = min(BAND, t + 1)
                e = t % 2
                pe.wait_ge(done, count)
                pe.wait_ge(probsT_split, u + 1)
                for j in range(n):
                    b = 2 + 2 * e + j // 4
                    last = pe.transpose(psum[:, b, (j % 4) * P:(j % 4) * P + P],
                                        prob[:, t % RING, NBW - (n - j) * P:NBW - (n - j - 1) * P], ident[:, :])
                last.then_inc(probsT_done, 1)

            def a_values(u, pair, s, pr):
                pe.wait_ge(probsT_split, u + 3)
                pe.wait_ge(y_summed, pair + 1)
                first_tile = 2 * pr - (BAND - 1)
                order = [i for i in range(1, BAND) if first_tile + i >= 0]
                order += [i for i in (0, BAND) if first_tile + i >= 0]
                for m, i in enumerate(order):
                    c0, c1 = (0, P) if i == 0 else (P, 2 * P) if i == BAND else (0, 2 * P)
                    for pt in (pt_hi, pt_lo):
                        last = mm(psum[:, 6 + pr % 2, c0:c1], av[:, s, first_tile + i, :], pt[:, pr % 2, i, c0:c1],
                                  m == 0 and pt is pt_hi, m == len(order) - 1 and pt is pt_lo)
                last.then_inc(values_done, 1)

            def a_step(it, i):
                unit = a_unit(it, i, 7)
                if unit and unit[2] % 2 == 1:
                    u, s, t = unit
                    a_values(u, (A_TURN // 2) * it + (i - 7) // 2, s, t // 2)
                unit = a_unit(it, i, 4)
                if unit:
                    u, s, t = unit
                    by_vector = t % 8 in VECTOR_NORMS
                    a_transpose(u, t, normed[by_vector], norms(A_TURN - 1, by_vector) * it + norms(i - 4, by_vector))

                unit = a_unit(it, i, -1)
                if unit:
                    u, s, t = unit
                    wait_head(pe, it, s, t)
                    a_scores(u, s, t)
            pe.wait_ge(acc_free, 8 + 2 * UNITS - 6)
            for i in range(-1, A_TURN - 1):
                if i == 4:
                    pe.wait_ge(acc_free, 8 + 2 * UNITS)
                a_step(0, i)
            with pe.Fori(1, A_HEADS // 2) as it:
                for i in range(-1, A_TURN - 1):
                    a_step(it, i)
            for i in range(A_TURN - 1, A_TURN + A_DRAIN):
                a_step(A_HEADS // 2 - 1, i)

            def b_scores(u):
                pair, s, i = b_unit(u)
                if u % 4 == 0:
                    pe.wait_ge(bq_loaded[i // 2], 64 * (u // (2 * B_UNITS) + 1))
                if i == 0:
                    pe.wait_ge(bk_loaded[s], 64 * (pair // 2 + 1))
                if u >= 2:
                    pe.wait_ge(bexp_done, u - 1)
                for c in range(4):
                    t = (4 * i + c) * CHUNK
                    for bk in (bk_hi, bk_lo):
                        last = mm(psum[:, u % 2, c * P:c * P + P], bq[:, u % 2, 2 * t:2 * t + P], bk[:, s, t:t + P],
                                  bk is bk_hi, bk is bk_lo)
                last.then_inc(bscores_done, 1)

            def b_v(u):
                if u % 2 == 1:
                    return
                v = u // 2
                pair, s, i = b_unit(u)
                if i == 0:
                    pe.wait_ge(bv_loaded[s], 32 * (pair // 2 + 1))
                if v >= 1:
                    pe.wait_ge(bv_ready, v)
                for c in range(4):
                    t = (4 * i + c) * CHUNK
                    last = pe.transpose(psum[:, 7, c * P:c * P + P], bvt[:, s, t:t + P], ident[:, :])
                last.then_inc(bv_done, 1)

            def b_transpose(u):
                pe.wait_ge(bnormed, u + 1)
                if u >= 2:
                    pe.wait_ge(bprobsT_split, u - 1)
                for c in range(4):
                    last = pe.transpose(psum[:, 2 + u % 2, c * P:c * P + P], prob_b[:, u % 4, c, :], ident[:, :])
                last.then_inc(bprobsT_done, 1)

            def b_values(u):
                pe.wait_ge(bprobsT_split, u + 1)
                v = u // 2
                pe.wait_ge(bv_ready, v + 1)
                pe.wait_ge(by_summed, u + 1)
                for c in range(4):
                    for pt in (ptb_hi, ptb_lo):
                        last = mm(psum[:, 4 + u % 3, c * P:c * P + P], v_b[:, v % 4, c, :], pt[:, u % 4, c, :],
                                  pt is ptb_hi, pt is ptb_lo)
                last.then_inc(bvalues_done, 1)

            pe.wait_ge(bden_step, 3)
            for step in range(-1, B_ALL + B_DRAIN):
                for fn, lag in ((b_values, 6), (b_transpose, 3), (b_v, 3), (b_scores, -1)):
                    if 0 <= step - lag < B_ALL:
                        fn(step - lag)

            def product(bank, l_hi, l_lo, r_hi, r_lo, kts, split0=None):
                for n in range(2):
                    cols = slice(n * 512, n * 512 + 512)
                    dst = psum[:, bank + n, :]
                    for k in range(kts):
                        if split0 is not None and n == 0:
                            pe.wait_ge(cw_split, split0 + k + 1)
                        mm(dst, l_hi[:, k, :], r_hi[:, k, cols], k == 0, False)
                        mm(dst, l_hi[:, k, :], r_lo[:, k, cols], False, False)
                        last = mm(dst, l_lo[:, k, :], r_hi[:, k, cols], False, k == kts - 1)
                return last

            def mix(t, split0=None):
                pe.wait_ge(y_split, t + 1)
                if split0 is None:
                    pe.wait_ge(h_done, t)
                product(0, y_hi, y_lo, wo_hi, wo_lo, KT, split0).then_inc(mix_done, 1)

            def ple(t, s):
                pe.wait_ge(p_split, t + 1)
                pe.wait_ge(ple_gated, t + 1)
                product(6, p_hi[:, s, :, :], p_lo[:, s, :, :], wp_hi, wp_lo, 2).then_inc(ple_done, 1)

            def gate(t):
                pe.wait_ge(hT_split, t + 1)
                pe.wait_ge(sig_done, t + 1)
                product(4, hT_hi, hT_lo, wg_hi, wg_lo, KT).then_inc(gate_done, 1)

            def transpose_h(t, slot):
                pe.wait_ge(h_done, t + 1)
                for k in range(KT):
                    last = pe.transpose(psum[:, 2 + k // 4, (k % 4) * P:(k % 4) * P + P], h[:, slot, k * P:k * P + P],
                                        ident[:, :])
                last.then_inc(hT_done, 1)

            mix(0, 0)
            transpose_h(0, 0)
            pe.wait_ge(cw_split, 2 * KT + 2)
            with pe.Fori(0, 5) as it:
                for i in range(6):
                    t = 6 * it + i
                    mix(t + 1)
                    ple(t, i % 2)
                    gate(t)
                    transpose_h(t + 1, (i + 1) % 3)
            mix(31)
            ple(30, 0)
            gate(30)
            transpose_h(31, 1)
            ple(31, 1)
            gate(31)


def _rope_const():
    half = ROT // 2
    inv = np.float32(THETA) ** (-np.arange(half, dtype=np.float32) / np.float32(half))
    c = np.zeros((P, 2), np.float32)
    r = np.arange(P) % ROT
    c[:, 0] = inv[r % half]
    c[:, 1] = np.where(r < half, -1.0, 1.0)
    return c


def kernel(x, p, positions, w_in, rel_bias, sinks, w_out, ln_g, ln_b, w_ple_proj, w_ple_gate):
    import concourse.bacc as bacc
    from concourse.bass_utils import run_bass_kernel_spmd

    x, p, positions, w_in, rel_bias, sinks, w_out, ln_g, ln_b, w_ple_proj, w_ple_gate = (
        np.asarray(a) for a in (x, p, positions, w_in, rel_bias, sinks, w_out, ln_g, ln_b, w_ple_proj, w_ple_gate))
    w = w_in[0]
    aq, ak, av, ag, bq, bk, bv, bg = np.split(w, np.cumsum([D_A, D_A, D_A, D_A, D_B, D_KV, D_KV]).tolist(), axis=1)
    arrays = {
        "xT": np.ascontiguousarray(x[0].T),
        "x": np.ascontiguousarray(x[0]),
        "pT": np.ascontiguousarray(p[0, 0].T),
        "pos": np.ascontiguousarray(positions),
        "w_in": np.concatenate([aq, ak, ag, bg, bq, bk, bv, av], axis=1),
        "rel_rev": np.ascontiguousarray(rel_bias[0][:, ::-1]),
        "sinks": np.ascontiguousarray(sinks[0].reshape(B_HEADS // 2, 2).T),
        "w_out": np.ascontiguousarray(w_out[0]),
        "w_gate": np.ascontiguousarray(w_ple_gate[0]),
        "w_ple": np.ascontiguousarray(w_ple_proj[0]),
        "ln_g": np.ascontiguousarray(ln_g),
        "ln_b": np.ascontiguousarray(ln_b),
        "rope_const": _rope_const(),
    }
    nc = bacc.Bacc("TRN2", target_bir_lowering=False, num_devices=1)
    aps = {n: nc.dram_tensor("in_" + n, list(a.shape), mybir.dt.from_np(a.dtype), kind="ExternalInput").ap()
           for n, a in arrays.items()}
    out = nc.dram_tensor("out", [SEQ, D_MODEL], mybir.dt.float32, kind="ExternalOutput").ap()
    build(nc, out=out, **aps)
    r = run_bass_kernel_spmd(nc, [{"in_" + n: a for n, a in arrays.items()}], core_ids=[0])
    return r.results[0]["out"].reshape(1, SEQ, D_MODEL)
```
